# Optimizing a Trainium2 kernel written in Bass

```python
import jax, jax.numpy as jnp
from jax import lax
import numpy as np
import jax
import jax.numpy as jnp

D_MODEL = 2048
BATCH = 1
SEQ = 256
DEPTH = 2

N_META = 16
CONF_W = 1024
CONF_K = 31
SC_W = 1024
SC_K = 3
AB_SIZES = (CONF_W, CONF_W, SC_W, SC_W, SC_W)
AB_IN = sum(AB_SIZES)
GLA_HEADS = 4
GLA_DK = 128
GLA_DV = 256
GLA_QK = GLA_HEADS * GLA_DK
GLA_V = GLA_HEADS * GLA_DV
GLA_RANK = 16
GLA_GATE_NORM = 16.0
GLA_CHUNK = 64
GLA_SIZES = (GLA_QK, GLA_QK, GLA_V, GLA_V, GLA_RANK)
RW_HEADS = 16
RW_N = 64
RW_W = RW_HEADS * RW_N
RW_DECAY_RANK = 64
RW_A_RANK = 64
RW_G_RANK = 128
RW_SIZES = (RW_W, RW_W, RW_W, RW_DECAY_RANK, RW_A_RANK, RW_G_RANK)
GLA_COLS = sum(GLA_SIZES)
RW_COLS = sum(RW_SIZES)
CD_IN = GLA_COLS + RW_COLS
RW_GN_EPS = 64e-5
D_FF = 5632
FFN_K = 3
EPS = 1e-6
LN_EPS = 1e-5
N_EVEN = (DEPTH + 1) // 2
N_ODD = DEPTH // 2


def _splits(sizes):
    return [int(s) for s in np.cumsum(sizes)[:-1]]

def rmsnorm(x, g):
    x32 = x.astype(jnp.float32)
    y = x32 * lax.rsqrt(jnp.mean(x32 * x32, axis=-1, keepdims=True) + EPS)
    return (y * g.astype(jnp.float32)).astype(x.dtype)

def layernorm(x, g, b):
    x32 = x.astype(jnp.float32)
    mu = jnp.mean(x32, axis=-1, keepdims=True)
    var = jnp.mean(jnp.square(x32 - mu), axis=-1, keepdims=True)
    y = (x32 - mu) * lax.rsqrt(var + LN_EPS) * g.astype(jnp.float32) + b.astype(jnp.float32)
    return y.astype(x.dtype)

def causal_dwconv(x, w):
    K = w.shape[0]
    L = x.shape[1]
    xp = jnp.pad(x, ((0, 0), (K - 1, 0), (0, 0)))
    out = xp[:, 0:L] * w[0]
    for t in range(1, K):
        out = out + xp[:, t:t + L] * w[t]
    return out

def token_shift(z):
    return jnp.pad(z, ((0, 0), (1, 0), (0, 0)))[:, :-1]

def mixer_ab(h, w_in, conf_dw, conf_dw_b, conf_ln_g, conf_ln_b, sc_dw, w_out):
    z = h @ w_in
    a_val, a_gate, s_b, s_c, s_x = jnp.split(z, _splits(AB_SIZES), axis=-1)
    a = a_val * jax.nn.sigmoid(a_gate)
    a = causal_dwconv(a, conf_dw) + conf_dw_b
    a = jax.nn.silu(layernorm(a, conf_ln_g, conf_ln_b))
    s = s_b * causal_dwconv(s_c * s_x, sc_dw)
    return jnp.concatenate([a, s], axis=-1) @ w_out

def gla_chunked(q, k, v, log_a):
    Bs, T, H, dk = q.shape
    dv = v.shape[-1]
    C = GLA_CHUNK
    nc = T // C

    def blk(t):
        return t.reshape(Bs, nc, C, H, t.shape[-1]).transpose(0, 3, 1, 2, 4)

    q, k, v, g = blk(q), blk(k), blk(v), blk(log_a)
    cum = jnp.cumsum(g, axis=3)
    last = cum[:, :, :, -1:, :]
    q_dec = q * jnp.exp(cum)
    k_dec = k * jnp.exp(-cum)
    mask = jnp.tril(jnp.ones((C, C), dtype=bool))
    scores = jnp.where(mask, jnp.einsum('bhncd,bhnsd->bhncs', q_dec, k_dec), 0.0)
    o = jnp.einsum('bhncs,bhnsv->bhncv', scores, v)
    chunk_state = jnp.einsum('bhncd,bhncv->bhndv', k * jnp.exp(last - cum), v)
    chunk_decay = jnp.exp(last[:, :, :, 0, :])

    def step(S, inp):
        dec, cs = inp
        return S * dec[..., None] + cs, S

    _, S_prev = lax.scan(step, jnp.zeros((Bs, H, dk, dv), q.dtype),
                         (jnp.moveaxis(chunk_decay, 2, 0), jnp.moveaxis(chunk_state, 2, 0)))
    S_prev = jnp.moveaxis(S_prev, 0, 2)
    o = o + jnp.einsum('bhncd,bhndv->bhncv', q_dec, S_prev)
    return o.transpose(0, 2, 3, 1, 4).reshape(Bs, T, H, dv)

def rwkv7_scan(r, w, k, v, kk, a):
    Bs, L, H, N = r.shape

    def step(S, inp):
        r_t, w_t, k_t, v_t, kk_t, a_t = inp
        sa = jnp.einsum('bhvk,bhk->bhv', S, -kk_t)
        S = S * w_t[:, :, None, :] + sa[..., None] * (kk_t * a_t)[:, :, None, :] \
            + v_t[..., None] * k_t[:, :, None, :]
        return S, jnp.einsum('bhvk,bhk->bhv', S, r_t)

    xs = tuple(jnp.moveaxis(t, 1, 0) for t in (r, w, k, v, kk, a))
    _, y = lax.scan(step, jnp.zeros((Bs, H, N, N), r.dtype), xs)
    return jnp.moveaxis(y, 0, 1)

def mixer_cd(h, w_in, gla_w2, gla_b, gla_norm_g, rw_mu, rw_w0, rw_w2, rw_a0, rw_a2, rw_g2,
             rw_kk, rw_ka, rw_rk, rw_ln_g, rw_ln_b, w_out):
    dt = h.dtype
    Bs, L, _ = h.shape
    z = h @ w_in
    z_gla, z_rw = z[..., :GLA_COLS], z[..., GLA_COLS:]

    q, k, v, go, glr = jnp.split(z_gla.astype(jnp.float32), _splits(GLA_SIZES), axis=-1)
    log_a = jax.nn.log_sigmoid(glr @ gla_w2.astype(jnp.float32) + gla_b) / GLA_GATE_NORM
    q = q * (GLA_DK ** -0.5)
    heads = lambda t, d: t.reshape(Bs, L, GLA_HEADS, d)
    q, k, log_a, v = heads(q, GLA_DK), heads(k, GLA_DK), heads(log_a, GLA_DK), heads(v, GLA_DV)
    pad_front = (-N_META) % GLA_CHUNK
    pad_back = (-(pad_front + L)) % GLA_CHUNK
    pw = ((0, 0), (pad_front, pad_back), (0, 0), (0, 0))
    o = gla_chunked(jnp.pad(q, pw), jnp.pad(k, pw), jnp.pad(v, pw), jnp.pad(log_a, pw))
    o = o[:, pad_front:pad_front + L]
    o = o * lax.rsqrt(jnp.mean(o * o, axis=-1, keepdims=True) + EPS)
    o = o.reshape(Bs, L, GLA_V) * gla_norm_g * jax.nn.silu(go)

    zr = z_rw.astype(jnp.float32)
    zr = zr + (token_shift(zr) - zr) * rw_mu
    r, kr, vr, xw, xa, xg = jnp.split(zr, _splits(RW_SIZES), axis=-1)
    w_log = -jax.nn.softplus(-(rw_w0 + jnp.tanh(xw) @ rw_w2.astype(jnp.float32))) - 0.5
    decay = jnp.exp(-jnp.exp(w_log))
    a = jax.nn.sigmoid(rw_a0 + xa @ rw_a2.astype(jnp.float32))
    g = jax.nn.sigmoid(xg) @ rw_g2.astype(jnp.float32)
    rh = lambda t: t.reshape(Bs, L, RW_HEADS, RW_N)
    r, kr, vr, decay, a = rh(r), rh(kr), rh(vr), rh(decay), rh(a)
    kk = kr * rw_kk.reshape(RW_HEADS, RW_N)
    kk = kk / jnp.maximum(jnp.sqrt(jnp.sum(kk * kk, axis=-1, keepdims=True)), 1e-12)
    kr = kr * (1.0 + (a - 1.0) * rw_ka.reshape(RW_HEADS, RW_N))
    y = rwkv7_scan(r, decay, kr, vr, kk, a)
    mu = jnp.mean(y, axis=-1, keepdims=True)
    var = jnp.mean(jnp.square(y - mu), axis=-1, keepdims=True)
    y = (y - mu) * lax.rsqrt(var + RW_GN_EPS) * rw_ln_g.reshape(RW_HEADS, RW_N) \
        + rw_ln_b.reshape(RW_HEADS, RW_N)
    y = y + jnp.sum(r * kr * rw_rk.reshape(RW_HEADS, RW_N), axis=-1, keepdims=True) * vr
    y = y.reshape(Bs, L, RW_W) * g

    return jnp.concatenate([o, y], axis=-1).astype(dt) @ w_out

def conv_ffn(h, w_up, dw, w_down):
    u = causal_dwconv(h @ w_up, dw)
    val, gate = u[..., :D_FF], u[..., D_FF:]
    return (jax.nn.silu(gate) * val) @ w_down

def first_inputs(seed: int = 0) -> dict:
    key = jax.random.key(seed)
    ks = iter(jax.random.split(key, 48))
    nrm = lambda shape, scale: jax.random.normal(next(ks), shape, jnp.float32) * scale
    uni = lambda shape, lo, hi: jax.random.uniform(next(ks), shape, jnp.float32, lo, hi)
    gain = lambda shape: 1.0 + nrm(shape, 0.02)
    D = D_MODEL
    NE, NO = N_EVEN, N_ODD
    return {
        "x": nrm((BATCH, SEQ, D), 1.0),
        "meta": nrm((N_META, D), 1.0),
        "ab_w_in": nrm((NE, D, AB_IN), D ** -0.5),
        "ab_conf_dw": nrm((NE, CONF_K, CONF_W), CONF_K ** -0.5),
        "ab_conf_dw_b": nrm((NE, CONF_W), 0.02),
        "ab_conf_ln_g": gain((NE, CONF_W)),
        "ab_conf_ln_b": nrm((NE, CONF_W), 0.02),
        "ab_sc_dw": nrm((NE, SC_K, SC_W), SC_K ** -0.5),
        "ab_w_out": nrm((NE, CONF_W + SC_W, D), (CONF_W + SC_W) ** -0.5),
        "cd_w_in": nrm((NO, D, CD_IN), D ** -0.5),
        "cd_gla_w2": nrm((NO, GLA_RANK, GLA_QK), GLA_RANK ** -0.5),
        "cd_gla_b": nrm((NO, GLA_QK), 0.1),
        "cd_gla_norm_g": gain((NO, GLA_V)),
        "cd_rw_mu": uni((NO, RW_COLS), 0.0, 1.0),
        "cd_rw_w0": uni((NO, RW_W), -6.0, -1.0),
        "cd_rw_w2": nrm((NO, RW_DECAY_RANK, RW_W), RW_DECAY_RANK ** -0.5),
        "cd_rw_a0": nrm((NO, RW_W), 0.1),
        "cd_rw_a2": nrm((NO, RW_A_RANK, RW_W), RW_A_RANK ** -0.5),
        "cd_rw_g2": nrm((NO, RW_G_RANK, RW_W), RW_G_RANK ** -0.5),
        "cd_rw_kk": 0.85 + nrm((NO, RW_W), 0.05),
        "cd_rw_ka": 1.0 + nrm((NO, RW_W), 0.05),
        "cd_rw_rk": nrm((NO, RW_W), 0.1),
        "cd_rw_ln_g": gain((NO, RW_W)),
        "cd_rw_ln_b": nrm((NO, RW_W), 0.02),
        "cd_w_out": nrm((NO, GLA_V + RW_W, D), (GLA_V + RW_W) ** -0.5),
        "norm_mix": gain((DEPTH, D)),
        "norm_ffn": gain((DEPTH, D)),
        "ffn_w_up": nrm((DEPTH, D, 2 * D_FF), D ** -0.5),
        "ffn_dw": nrm((DEPTH, FFN_K, 2 * D_FF), FFN_K ** -0.5),
        "ffn_w_down": nrm((DEPTH, D_FF, D), D_FF ** -0.5),
        "norm_final": gain((D,)),
    }

def first_block(x, meta, ab_w_in, ab_conf_dw, ab_conf_dw_b, ab_conf_ln_g, ab_conf_ln_b, ab_sc_dw,
              ab_w_out, cd_w_in, cd_gla_w2, cd_gla_b, cd_gla_norm_g, cd_rw_mu, cd_rw_w0, cd_rw_w2,
              cd_rw_a0, cd_rw_a2, cd_rw_g2, cd_rw_kk, cd_rw_ka, cd_rw_rk, cd_rw_ln_g, cd_rw_ln_b,
              cd_w_out, norm_mix, norm_ffn, ffn_w_up, ffn_dw, ffn_w_down, norm_final):
    Bs = x.shape[0]
    h = jnp.concatenate([jnp.broadcast_to(meta[None].astype(x.dtype), (Bs, N_META, D_MODEL)), x],
                        axis=1)
    for i in range(DEPTH):
        hn = rmsnorm(h, norm_mix[i])
        j = i // 2
        if i % 2 == 0:
            mix = mixer_ab(hn, ab_w_in[j], ab_conf_dw[j], ab_conf_dw_b[j], ab_conf_ln_g[j],
                           ab_conf_ln_b[j], ab_sc_dw[j], ab_w_out[j])
        else:
            mix = mixer_cd(hn, cd_w_in[j], cd_gla_w2[j], cd_gla_b[j], cd_gla_norm_g[j], cd_rw_mu[j],
                           cd_rw_w0[j], cd_rw_w2[j], cd_rw_a0[j], cd_rw_a2[j], cd_rw_g2[j],
                           cd_rw_kk[j], cd_rw_ka[j], cd_rw_rk[j], cd_rw_ln_g[j], cd_rw_ln_b[j],
                           cd_w_out[j])
        h = h + mix.astype(h.dtype)
        h = h + conv_ffn(rmsnorm(h, norm_ffn[i]), ffn_w_up[i], ffn_dw[i], ffn_w_down[i]).astype(h.dtype)
    return rmsnorm(h, norm_final)[:, N_META:]


_first_inputs = first_inputs


def first_inputs(seed=0):
    import zlib

    import numpy as np

    out = dict(_first_inputs(seed))
    spreads = {}
    factors = {'ab_conf_dw_b': 3.068,
     'ab_conf_ln_g': 4.915,
     'ab_conf_ln_b': 5.648,
     'cd_gla_b': 4.263,
     'cd_gla_norm_g': 8.0,
     'cd_rw_w2': 3.639,
     'cd_rw_a0': 5.739,
     'cd_rw_kk': 5.174,
     'cd_rw_ka': 3.961,
     'cd_rw_ln_g': 8.0,
     'cd_rw_ln_b': 8.0,
     'norm_ffn': 3.029,
     'norm_final': 2.769}
    for name, (base, spread) in spreads.items():
        noise = np.random.default_rng([zlib.crc32(name.encode()), seed]).standard_normal(out[name].shape)
        drawn = base * np.exp(spread * noise) if base else spread * noise
        out[name] = __import__('jax').numpy.asarray(drawn.astype(out[name].dtype))
    for name, factor in factors.items():
        out[name] = (out[name] * factor).astype(out[name].dtype)
    return out


_narrow_inputs = first_inputs


def first_inputs(seed=0):

    out = dict(_narrow_inputs(seed))
    wider = {'cd_gla_norm_g': 6.63, 'cd_rw_ln_g': 7.23, 'cd_rw_ln_b': 7.75, 'norm_final': 3.13}
    for name, times in wider.items():
        mean = out[name].mean()
        out[name] = (mean + times * (out[name] - mean)).astype(out[name].dtype)
    return out


DEPTH_2 = 1

BRANCH_WIDTH = 1024
N_BRANCH = 3
A_HEADS = 8
A_KEY = 128
A_VAL = BRANCH_WIDTH // A_HEADS
A_FDIM = A_HEADS * A_KEY
A_CHUNK = 64
B_HEADS = 8
B_HDIM = BRANCH_WIDTH // B_HEADS
B_CONV = 4
B_C = 8.0
C_HDIM = 64
C_HEADS = BRANCH_WIDTH // C_HDIM
C_GROUPS = 2
C_STATE = 128
C_CONV = 4
C_CHUNK = 128
C_CONV_DIM = BRANCH_WIDTH + 2 * C_GROUPS * C_STATE
SPLITS = (A_FDIM, A_FDIM, BRANCH_WIDTH, BRANCH_WIDTH, BRANCH_WIDTH, BRANCH_WIDTH, BRANCH_WIDTH, C_CONV_DIM, C_HEADS, N_BRANCH * D_MODEL)
IN_COLS = sum(SPLITS)


def rmsnorm_2(x, w):
    xf = x.astype(jnp.float32)
    y = xf * lax.rsqrt(jnp.mean(xf * xf, axis=-1, keepdims=True) + EPS)
    return (y * w.astype(jnp.float32)).astype(x.dtype)

def causal_depthwise_conv(x, w, b):
    width, ch = w.shape
    y = lax.conv_general_dilated(x, w[:, None, :].astype(x.dtype), window_strides=(1,),
                                 padding=[(width - 1, 0)], dimension_numbers=('NWC', 'WIO', 'NWC'),
                                 feature_group_count=ch)
    return y + b.astype(x.dtype)

def hgrn2_mixer(q, f_pre, i, lb):
    bsz, s, _ = q.shape
    n = s // A_CHUNK
    lbf = lb.astype(jnp.float32)
    log_f = jnp.logaddexp(jnp.log(lbf), jnp.log1p(-lbf) + jax.nn.log_sigmoid(f_pre.astype(jnp.float32)))
    k = -jnp.expm1(log_f)

    def to_chunks(t, d):
        return t.astype(jnp.float32).reshape(bsz, n, A_CHUNK, A_HEADS, d).transpose(1, 0, 3, 2, 4)

    qc, kc, gc, vc = to_chunks(q, A_KEY), to_chunks(k, A_KEY), to_chunks(log_f, A_KEY), to_chunks(i, A_VAL)
    causal = jnp.tril(jnp.ones((A_CHUNK, A_CHUNK), dtype=bool))

    def step(state, inp):
        qb, kb, gb, vb = inp
        b = jnp.cumsum(gb, axis=-2)
        diff = b[:, :, :, None, :] - b[:, :, None, :, :]
        decay = jnp.exp(jnp.where(causal[:, :, None], diff, -jnp.inf))
        scores = jnp.einsum('bhtk,bhsk,bhtsk->bhts', qb, kb, decay)
        o = (jnp.einsum('bhts,bhsv->bhtv', scores, vb)
             + jnp.einsum('bhtk,bhkv->bhtv', qb * jnp.exp(b), state))
        b_last = b[:, :, -1:, :]
        state = (jnp.exp(b_last[:, :, 0, :, None]) * state
                 + jnp.einsum('bhsk,bhsv->bhkv', kb * jnp.exp(b_last - b), vb))
        return state, o

    s0 = jnp.zeros((bsz, A_HEADS, A_KEY, A_VAL), jnp.float32)
    _, o = lax.scan(step, s0, (qc, kc, gc, vc))
    return o.transpose(1, 0, 3, 2, 4).reshape(bsz, s, A_HEADS, A_VAL)

def rglru_mixer(x, conv_w, conv_b, wa, ba, wx, bx, lam):
    xc = causal_depthwise_conv(x, conv_w, conv_b)
    bsz, s, _ = xc.shape
    xh = xc.astype(jnp.float32).reshape(bsz, s, B_HEADS, B_HDIM)
    r = jax.nn.sigmoid(jnp.einsum('bshi,hij->bshj', xh, wa.astype(jnp.float32)) + ba).reshape(bsz, s, BRANCH_WIDTH)
    ig = jax.nn.sigmoid(jnp.einsum('bshi,hij->bshj', xh, wx.astype(jnp.float32)) + bx).reshape(bsz, s, BRANCH_WIDTH)
    log_a = -B_C * r * jax.nn.softplus(-lam.astype(jnp.float32))
    a = jnp.exp(log_a)
    u = jnp.sqrt(-jnp.expm1(2.0 * log_a)) * (ig * xh.reshape(bsz, s, BRANCH_WIDTH))

    def combine(left, right):
        a1, b1 = left
        a2, b2 = right
        return a1 * a2, a2 * b1 + b2

    _, h = lax.associative_scan(combine, (a, u), axis=1)
    return h

def segsum(x):
    t = x.shape[-1]
    cs = jnp.cumsum(x, axis=-1)
    mask = jnp.tril(jnp.ones((t, t), dtype=bool))
    return jnp.where(mask, cs[..., :, None] - cs[..., None, :], -jnp.inf)

def ssd_mixer(xbc_pre, dt_pre, conv_w, conv_b, dt_bias, a_log, d_skip):
    xbc = jax.nn.silu(causal_depthwise_conv(xbc_pre, conv_w, conv_b)).astype(jnp.float32)
    bsz, s, _ = xbc.shape
    n = s // C_CHUNK
    rep = C_HEADS // C_GROUPS
    xs, bm, cm = jnp.split(xbc, [BRANCH_WIDTH, BRANCH_WIDTH + C_GROUPS * C_STATE], axis=-1)
    xs = xs.reshape(bsz, n, C_CHUNK, C_GROUPS, rep, C_HDIM)
    bm = bm.reshape(bsz, n, C_CHUNK, C_GROUPS, C_STATE)
    cm = cm.reshape(bsz, n, C_CHUNK, C_GROUPS, C_STATE)
    dt = jax.nn.softplus(dt_pre.astype(jnp.float32) + dt_bias.astype(jnp.float32))
    a = -jnp.exp(a_log.astype(jnp.float32))
    dtc = dt.reshape(bsz, n, C_CHUNK, C_GROUPS, rep)
    da = (dtc * a.reshape(C_GROUPS, rep)).transpose(0, 3, 4, 1, 2)
    xdt = xs * dtc[..., None]
    cum = jnp.cumsum(da, axis=-1)
    lmat = jnp.exp(segsum(da))
    cb = jnp.einsum('bclgn,bcsgn->bgcls', cm, bm)
    y_diag = jnp.einsum('bgcls,bgrcls,bcsgrp->bclgrp', cb, lmat, xdt)
    decay_states = jnp.exp(cum[..., -1:] - cum)
    states = jnp.einsum('bclgn,bgrcl,bclgrp->bcgrpn', bm, decay_states, xdt)
    chunk_decay = jnp.exp(segsum(jnp.pad(cum[..., -1], [(0, 0), (0, 0), (0, 0), (1, 0)])))
    states = jnp.concatenate([jnp.zeros_like(states[:, :1]), states], axis=1)
    states = jnp.einsum('bgrzc,bcgrpn->bzgrpn', chunk_decay, states)[:, :-1]
    y_off = jnp.einsum('bclgn,bcgrpn,bgrcl->bclgrp', cm, states, jnp.exp(cum))
    y = y_diag + y_off + d_skip.astype(jnp.float32).reshape(C_GROUPS, rep)[:, :, None] * xs
    return y.reshape(bsz, s, BRANCH_WIDTH)

def second_inputs(seed: int = 0) -> dict:
    key = jax.random.key(seed)
    ks = jax.random.split(key, 24)
    f32 = jnp.float32

    def nrm(k, shape, scale):
        return scale * jax.random.normal(k, shape, f32)

    x = jax.random.normal(ks[0], (BATCH, SEQ, D_MODEL), f32)
    norm_w = 1.0 + nrm(ks[1], (DEPTH_2, D_MODEL), 0.02)
    w_in = nrm(ks[2], (DEPTH_2, D_MODEL, IN_COLS), D_MODEL ** -0.5)
    hgrn_lb_logits = nrm(ks[3], (DEPTH_2, A_FDIM), 0.5)
    hgrn_norm_w = 1.0 + nrm(ks[4], (DEPTH_2, BRANCH_WIDTH), 0.02)
    rglru_conv_w = nrm(ks[5], (DEPTH_2, B_CONV, BRANCH_WIDTH), B_CONV ** -0.5)
    rglru_conv_b = nrm(ks[6], (DEPTH_2, BRANCH_WIDTH), 0.02)
    rglru_wa = nrm(ks[7], (DEPTH_2, B_HEADS, B_HDIM, B_HDIM), B_HDIM ** -0.5)
    rglru_ba = nrm(ks[8], (DEPTH_2, B_HEADS, B_HDIM), 0.02)
    rglru_wx = nrm(ks[9], (DEPTH_2, B_HEADS, B_HDIM, B_HDIM), B_HDIM ** -0.5)
    rglru_bx = nrm(ks[10], (DEPTH_2, B_HEADS, B_HDIM), 0.02)
    u = jax.random.uniform(ks[11], (DEPTH_2, BRANCH_WIDTH), f32, 0.9, 0.999)
    p = u ** (1.0 / B_C)
    rglru_lambda = jnp.log(p) - jnp.log1p(-p)
    ssd_conv_w = nrm(ks[12], (DEPTH_2, C_CONV, C_CONV_DIM), C_CONV ** -0.5)
    ssd_conv_b = nrm(ks[13], (DEPTH_2, C_CONV_DIM), 0.02)
    dt0 = jnp.exp(jax.random.uniform(ks[14], (DEPTH_2, C_HEADS), f32, float(np.log(1e-3)), float(np.log(1e-1))))
    ssd_dt_bias = dt0 + jnp.log(-jnp.expm1(-dt0))
    ssd_a_log = jnp.log(jax.random.uniform(ks[15], (DEPTH_2, C_HEADS), f32, 1.0, 16.0))
    ssd_d = 1.0 + nrm(ks[16], (DEPTH_2, C_HEADS), 0.1)
    ssd_norm_w = 1.0 + nrm(ks[17], (DEPTH_2, BRANCH_WIDTH), 0.02)
    w_out = nrm(ks[18], (DEPTH_2, N_BRANCH * BRANCH_WIDTH, D_MODEL), (N_BRANCH * BRANCH_WIDTH) ** -0.5)
    final_norm_w = 1.0 + nrm(ks[19], (D_MODEL,), 0.02)
    return {'x': x, 'norm_w': norm_w, 'w_in': w_in, 'hgrn_lb_logits': hgrn_lb_logits,
            'hgrn_norm_w': hgrn_norm_w, 'rglru_conv_w': rglru_conv_w, 'rglru_conv_b': rglru_conv_b,
            'rglru_wa': rglru_wa, 'rglru_ba': rglru_ba, 'rglru_wx': rglru_wx, 'rglru_bx': rglru_bx,
            'rglru_lambda': rglru_lambda, 'ssd_conv_w': ssd_conv_w, 'ssd_conv_b': ssd_conv_b,
            'ssd_dt_bias': ssd_dt_bias, 'ssd_a_log': ssd_a_log, 'ssd_d': ssd_d, 'ssd_norm_w': ssd_norm_w,
            'w_out': w_out, 'final_norm_w': final_norm_w}

def second_block(x, norm_w, w_in, hgrn_lb_logits, hgrn_norm_w, rglru_conv_w, rglru_conv_b, rglru_wa, rglru_ba,
              rglru_wx, rglru_bx, rglru_lambda, ssd_conv_w, ssd_conv_b, ssd_dt_bias, ssd_a_log, ssd_d,
              ssd_norm_w, w_out, final_norm_w):
    split_idx = np.cumsum(SPLITS)[:-1].tolist()
    sm = jax.nn.softmax(hgrn_lb_logits.astype(jnp.float32), axis=0)
    cs = jnp.cumsum(sm, axis=0)
    lower_bounds = cs - cs[0:1]
    bsz, s, _ = x.shape
    for l in range(DEPTH_2):
        h = rmsnorm_2(x, norm_w[l])
        proj = h @ w_in[l]
        a_q, a_f, a_i, a_z, b_x, b_z, c_z, c_xbc, c_dt, gate_logits = jnp.split(proj, split_idx, axis=-1)
        o_a = hgrn2_mixer(a_q, a_f, a_i, lower_bounds[l])
        o_a = rmsnorm_2(o_a, hgrn_norm_w[l].reshape(A_HEADS, A_VAL)).reshape(bsz, s, BRANCH_WIDTH)
        o_a = o_a * jax.nn.silu(a_z)
        o_b = rglru_mixer(b_x, rglru_conv_w[l], rglru_conv_b[l], rglru_wa[l], rglru_ba[l], rglru_wx[l],
                          rglru_bx[l], rglru_lambda[l]) * jax.nn.silu(b_z)
        y_c = ssd_mixer(c_xbc, c_dt, ssd_conv_w[l], ssd_conv_b[l], ssd_dt_bias[l], ssd_a_log[l], ssd_d[l])
        o_c = rmsnorm_2((y_c * jax.nn.silu(c_z)).reshape(bsz, s, C_GROUPS, BRANCH_WIDTH // C_GROUPS),
                      ssd_norm_w[l].reshape(C_GROUPS, BRANCH_WIDTH // C_GROUPS)).reshape(bsz, s, BRANCH_WIDTH)
        branches = jnp.stack([o_a, o_b, o_c], axis=2).astype(x.dtype)
        branch_out = jnp.einsum('bsnc,ncd->bsnd', branches,
                                w_out[l].reshape(N_BRANCH, BRANCH_WIDTH, D_MODEL))
        gates = jax.nn.sigmoid(gate_logits.astype(jnp.float32).reshape(bsz, s, N_BRANCH, D_MODEL))
        x = x + jnp.sum(gates * branch_out, axis=2).astype(x.dtype)
    return rmsnorm_2(x, final_norm_w)


_first_inputs_2 = second_inputs


def second_inputs(seed=0):
    import zlib

    import numpy as np

    out = dict(_first_inputs_2(seed))
    spreads = {}
    factors = {'norm_w': 4.31,
     'hgrn_norm_w': 8.0,
     'rglru_conv_b': 4.076,
     'rglru_ba': 8.0,
     'rglru_bx': 8.0,
     'ssd_conv_b': 7.529,
     'ssd_norm_w': 8.0,
     'final_norm_w': 2.913}
    for name, (base, spread) in spreads.items():
        noise = np.random.default_rng([zlib.crc32(name.encode()), seed]).standard_normal(out[name].shape)
        drawn = base * np.exp(spread * noise) if base else spread * noise
        out[name] = jnp.asarray(drawn.astype(out[name].dtype))
    for name, factor in factors.items():
        out[name] = (out[name] * factor).astype(out[name].dtype)
    return out


_narrow_inputs_2 = second_inputs


def second_inputs(seed=0):

    out = dict(_narrow_inputs_2(seed))
    wider = {'hgrn_norm_w': 3.66,
     'rglru_ba': 9.81,
     'rglru_bx': 7.06,
     'ssd_conv_b': 5.18,
     'ssd_d': 12.0,
     'ssd_norm_w': 10.93,
     'final_norm_w': 3.26}
    for name, times in wider.items():
        mean = out[name].mean()
        out[name] = (mean + times * (out[name] - mean)).astype(out[name].dtype)
    return out


def setup_inputs(seed=0):
    out = dict(first_inputs(seed))
    for name, value in second_inputs(seed + 1).items():
        if name != "x":
            out[name + "_2"] = value
    return out


def reference(
    x, meta, ab_w_in, ab_conf_dw, ab_conf_dw_b, ab_conf_ln_g, ab_conf_ln_b, ab_sc_dw, ab_w_out,
    cd_w_in, cd_gla_w2, cd_gla_b, cd_gla_norm_g, cd_rw_mu, cd_rw_w0, cd_rw_w2, cd_rw_a0,
    cd_rw_a2, cd_rw_g2, cd_rw_kk, cd_rw_ka, cd_rw_rk, cd_rw_ln_g, cd_rw_ln_b, cd_w_out,
    norm_mix, norm_ffn, ffn_w_up, ffn_dw, ffn_w_down, norm_final, norm_w_2, w_in_2,
    hgrn_lb_logits_2, hgrn_norm_w_2, rglru_conv_w_2, rglru_conv_b_2, rglru_wa_2, rglru_ba_2,
    rglru_wx_2, rglru_bx_2, rglru_lambda_2, ssd_conv_w_2, ssd_conv_b_2, ssd_dt_bias_2,
    ssd_a_log_2, ssd_d_2, ssd_norm_w_2, w_out_2, final_norm_w_2,
):
    x = first_block(
        x, meta, ab_w_in, ab_conf_dw, ab_conf_dw_b, ab_conf_ln_g, ab_conf_ln_b, ab_sc_dw,
        ab_w_out, cd_w_in, cd_gla_w2, cd_gla_b, cd_gla_norm_g, cd_rw_mu, cd_rw_w0, cd_rw_w2,
        cd_rw_a0, cd_rw_a2, cd_rw_g2, cd_rw_kk, cd_rw_ka, cd_rw_rk, cd_rw_ln_g, cd_rw_ln_b,
        cd_w_out, norm_mix, norm_ffn, ffn_w_up, ffn_dw, ffn_w_down, norm_final,
    )
    return second_block(
        x, norm_w_2, w_in_2, hgrn_lb_logits_2, hgrn_norm_w_2, rglru_conv_w_2, rglru_conv_b_2,
        rglru_wa_2, rglru_ba_2, rglru_wx_2, rglru_bx_2, rglru_lambda_2, ssd_conv_w_2,
        ssd_conv_b_2, ssd_dt_bias_2, ssd_a_log_2, ssd_d_2, ssd_norm_w_2, w_out_2,
        final_norm_w_2,
    )


_drawn_inputs = setup_inputs


def setup_inputs(seed=0):
    import zlib

    import numpy as np

    out = dict(_drawn_inputs(seed))
    spreads = {}
    factors = {'ssd_d_2': 64.0}
    for name, (base, spread) in spreads.items():
        noise = np.random.default_rng([zlib.crc32(name.encode()), seed]).standard_normal(out[name].shape)
        drawn = base * np.exp(spread * noise) if base else spread * noise
        out[name] = jnp.asarray(drawn.astype(out[name].dtype))
    for name, factor in factors.items():
        out[name] = (out[name] * factor).astype(out[name].dtype)
    return out
```

```python
import numpy as np
import concourse.bass as bass
from concourse import mybir

F32 = mybir.dt.float32
F32R = mybir.dt.float32r
I32 = mybir.dt.int32
ALU = mybir.AluOpType
ACT = mybir.ActivationFunctionType

P = 128
D = 2048
DK = D // P
META, SEQ = 16, 256
T = META + SEQ
TILES = [(0, META), (META, P), (META + P, P)]
CW = 1024 // P
CONF_K, SC_K, FFN_K, CONV_K = 31, 3, 3, 4
D_FF = 5632
FF = D_FF // P
FH = FF // 2
EPS, LN_EPS, GN_EPS = 1e-6, 1e-5, 64e-5
GLA_CHUNK, GLA_H, GLA_SCALE, GLA_NORM = 64, 4, 128.0 ** -0.5, 16.0
RW_CHUNK, RW_N = 32, 64
RW_DECAY = 0.6065306597126334
GLA_COLS, GLA_GLR = 3088, 3072
DT_COL, GATE_COL = 8704, 8720
RING = 4
LEVELS = [1, 2, 4, 8, 16, 32, 64]

VECTORS = [
    ("norm_mix", 2 * DK), ("norm_ffn", 2 * DK), ("norm_final", DK), ("ab_conf_dw", CONF_K * CW),
    ("ab_conf_dw_b", CW), ("ab_conf_ln_g", CW), ("ab_conf_ln_b", CW), ("ab_sc_dw", SC_K * CW),
    ("cd_gla_b", 4), ("cd_gla_norm_g", CW), ("cd_rw_mu", 26), ("cd_rw_w0", CW), ("cd_rw_a0", CW),
    ("cd_rw_kk", CW), ("cd_rw_ka", CW), ("cd_rw_rk", CW), ("cd_rw_ln_g", CW), ("cd_rw_ln_b", CW),
    ("ffn_dw", 2 * FFN_K * 2 * FF), ("norm_w_2", DK), ("final_norm_w_2", DK), ("hgrn_norm_w_2", CW),
    ("rglru_conv_w_2", CONV_K * CW), ("rglru_conv_b_2", CW), ("rglru_ba_2", CW), ("rglru_bx_2", CW),
    ("rglru_lambda_2", CW), ("ssd_conv_w_2", CONV_K * 12), ("ssd_conv_b_2", 12), ("ssd_norm_w_2", CW),
]
VOFF, NROWS = {}, 0
for _name, _rows in VECTORS:
    VOFF[_name] = NROWS
    NROWS += _rows
ROW_GROUPS = (NROWS + P - 1) // P


def order(*names):
    return {name: n + 1 for n, name in enumerate(names)}


class Phase:

    def __init__(self, n, jobs):
        self.n, self.jobs, self.base = n, jobs, 0


def weights(ap, k0, kt, cols):
    return ap.rearrange("(k p) n -> p k n", p=P)[:, k0:k0 + kt, cols]


def columns(view, first, i, per, u):
    return view[:, :, first + u * P:][:, :, bass.ds(i * (per * P), P)]


def plan(a):
    def tiles(ap, first, per, kt=DK):
        view = ap.rearrange("(k p) n -> p k n", p=P)[:, 0:kt, :]
        return [(kt, P, lambda i, u=u: columns(view, first, i, per, u)) for u in range(per)]

    ab, cd, w2 = a["ab_w_in"][0], a["cd_w_in"][0], a["w_in_2"][0]
    ph = {}
    ph["ab_gate"] = Phase(2, tiles(ab, 1024, 4))
    ph["ab_val"] = Phase(2, tiles(ab, 0, 4))
    ph["ab_s"] = Phase(2, tiles(ab, 2048, 4) + tiles(ab, 3072, 4) + tiles(ab, 4096, 4))
    ph["ab_out"] = Phase(4, tiles(a["ab_w_out"][0], 0, 4))

    def ffn(layer):
        for f in range(2):
            up = a["ffn_w_up"][layer]
            val, gate = tiles(up, f * FH * P, 2), tiles(up, D_FF + f * FH * P, 2)
            ph[f"up{layer}{f}"] = Phase(FH // 2, [gate[0], val[0], gate[1], val[1]])
            down = a["ffn_w_down"][layer].rearrange("(k p) n -> p k n", p=P)
            half = FH // 2
            jobs = []
            for u in range(2):
                for part in range(2):
                    k0 = f * FH + part * half
                    jobs.append((half, P, lambda i, u=u, k0=k0: columns(down[:, k0:k0 + half, :], 0, i, 2, u)))
            ph[f"down{layer}{f}"] = Phase(DK // 2, jobs)

    ffn(0)
    cdv = cd.rearrange("(k p) n -> p k n", p=P)
    ph["gla"] = Phase(6, tiles(cd, 0, 4))
    ph["glr"] = Phase(1, [(DK, META, lambda i: cdv[:, :, GLA_GLR:GLA_COLS])])
    ph["rw"] = Phase(6, tiles(cd, GLA_COLS, 4))
    ph["rw_low"] = Phase(1, tiles(cd, GLA_COLS + 24 * P, 2))
    ph["cd_out"] = Phase(4, tiles(a["cd_w_out"][0], 0, 4))
    ffn(1)
    w2v = w2.rearrange("(k p) n -> p k n", p=P)
    ph["in_a"] = Phase(8, tiles(w2, 0, 4))
    ph["in_bx"] = Phase(2, tiles(w2, 4096, 4))
    ph["in_bz"] = Phase(2, tiles(w2, 5120, 4))
    ph["in_xbc"] = Phase(3, tiles(w2, 7168, 4))
    ph["in_cz"] = Phase(2, tiles(w2, 6144, 4))
    ph["dt"] = Phase(1, [(DK, 16, lambda i: w2v[:, :, DT_COL:GATE_COL])])
    jobs = []
    wo = a["w_out_2"][0].rearrange("(k p) n -> p k n", p=P)
    for u in range(2):
        for n in range(3):
            jobs.append((DK, P, lambda i, u=u, n=n: columns(w2v, GATE_COL + n * D, i, 2, u)))
            jobs.append((CW, P, lambda i, u=u, n=n: columns(wo[:, n * CW:(n + 1) * CW, :], 0, i, 2, u)))
    ph["out"] = Phase(DK // 2, jobs)
    base = 0
    names = list(ph)
    for name, nxt in zip(names, names[1:] + [None]):
        p = ph[name]
        p.base = base
        base += p.n * len(p.jobs)
        kts = [j[0] for j in p.jobs]
        wrap = [kts[0]] * (p.n > 1) + ([ph[nxt].jobs[0][0]] if nxt else [])
        p.next_kt = kts[1:] + [max(wrap)]
    return ph


def build(nc, a, out, stop=None):
    ph = plan(a)
    at = [(nc.sbuf_base + 63) // 64 * 64]

    def place(name, shape, dt=F32, offset=None):
        size = 4
        for s in shape[1:]:
            size *= s
        if offset is None:
            offset = at[0]
            at[0] += (size + 63) // 64 * 64
        return nc.alloc_sbuf_tensor_at(name, shape, dt, offset=offset), offset

    raw, _ = place("raw", [P, RING, DK, P])
    w_hi, _ = place("w_hi", [P, 2, DK, P], F32R)
    w_lo, _ = place("w_lo", [P, 2, DK, P], F32R)
    h, _ = place("h", [P, DK, T])
    x_hi, x_off = place("x_hi", [P, DK, T], F32R)
    x_lo, _ = place("x_lo", [P, DK, T], F32R)
    work2, _ = place("work2", [P, 2 * DK * T], F32, x_off)
    vec, _ = place("vec", [P, NROWS])
    ident, _ = place("ident", [P, P])
    ones, _ = place("ones", [P, P])
    pair_ones, _ = place("pair_ones", [P, P])
    le, _ = place("le", [P, P])
    le64, _ = place("le64", [P, P])
    rw_mask, _ = place("rw_mask", [P, 4, P])
    up16, _ = place("up16", [P, P])
    low16, _ = place("low16", [P, P])
    low21, _ = place("low21", [P, P])
    eye2, _ = place("eye2", [P, RW_N])
    seg, _ = place("seg", [P, T])
    eps, _ = place("eps", [P, 4])
    omka, _ = place("omka", [P, CW])
    dskip, _ = place("dskip", [P, CW])
    small, _ = place("small", [16, 4])
    side, _ = place("side", [P, 2048])
    arena, arena_off = place("arena", [P, 18432])
    act_hi, _ = place("act_hi", [P, 24 * SEQ], F32R, arena_off)
    act_lo, _ = place("act_lo", [P, 24 * SEQ], F32R, arena_off + 4 * 24 * SEQ)
    ps = nc.alloc_psum_tensor("ps", [P, 8, 512], F32)

    def view(buf, first, *shape):
        n = 1
        for s in shape:
            n *= s
        v = buf[:, first:first + n]
        if len(shape) == 1:
            return v
        names = "abcd"[:len(shape)]
        return v.rearrange(f"p ({' '.join(names)}) -> p {' '.join(names)}", **dict(zip(names, shape)))

    def col(name, tile=0):
        first = VOFF[name]
        if isinstance(tile, int):
            return vec[:, first + tile:first + tile + 1]
        return vec[:, first:][:, bass.ds(tile, 1)]

    def cols(name, n, tile=0):
        return vec[:, VOFF[name] + tile:VOFF[name] + tile + n]

    sem = nc.alloc_semaphore
    loaded = [sem(f"loaded{r}") for r in range(RING)]
    rounded = sem("rounded")
    split = sem("split")
    multiplied = sem("multiplied")
    drained = [sem(f"drained{b}") for b in range(2)]
    met = sem("met")
    params_in, masks_made = sem("params_in"), sem("masks_made")
    rows_turned, rows_kept = sem("rows_turned"), sem("rows_kept")
    x_turned, x_kept = sem("x_turned"), [sem(f"x_kept{b}") for b in range(2)]
    norm_sq, norm_sum, norm_std = sem("norm_sq"), sem("norm_sum"), sem("norm_std")
    norm_xn, norm_hi = sem("norm_xn"), sem("norm_hi")
    hid_tap, hid_silu, hid_made = sem("hid_tap"), sem("hid_silu"), sem("hid_made")
    hid_hi_made, hid_lo_made = sem("hid_hi_made"), sem("hid_lo_made")
    side_in = sem("side_in")
    seg_made = sem("seg_made")
    padded = sem("padded")
    out_turned, out_kept, out_stored = sem("out_turned"), [sem(f"out_kept{b}") for b in range(2)], sem("out_stored")
    gates_made, products_made, tile_summed = sem("gates_made"), sem("products_made"), [sem(f"tile_summed{b}") for b in range(2)]

    def trio(name):
        return sem(f"{name}_vector"), sem(f"{name}_scalar"), sem(f"{name}_tensor")

    def meet(eng, name):
        eng.drain().then_inc(met, 1)
        eng.wait_ge(met, 4 * MEETINGS[name])

    passed = sem("passed")

    def settle(eng):
        eng.sem_inc(passed, 1)

    MEETINGS = order("setup", "n0", "ab_in", "ab", "ab_out", "n1", "ffn0", "n2", "gla_in", "gla", "rw_in", "rw",
                     "cd_cat", "cd_out", "n3", "ffn1", "n4", "n5", "in_a", "hgrn", "in_b", "rglru", "in_c", "ssd",
                     "cat", "out", "n6", "end")

    def load_phase(sp, p):
        def body(i):
            for u, (kt, w, src) in enumerate(p.jobs):
                j = p.base + u
                sp.wait_ge(split, i * len(p.jobs) + (j + 1))
                settle(sp)
                sp.dma_start(raw[:, j % RING, 0:kt, 0:w], src(i)).then_inc(loaded[j % RING], 16)
        if p.n == 1:
            body(0)
        else:
            with sp.Fori(0, p.n) as i:
                body(i)

    def round_job(act, p, i, u, kt):
        j = p.base + u
        act.wait_ge(loaded[j % RING], i * (16 * len(p.jobs) // RING) + 16 * (j // RING + 1))
        act.wait_ge(multiplied, i * len(p.jobs) + (j + 1))
        nc.scalar.activation(w_hi[:, j % 2, 0:kt], raw[:, j % RING, 0:kt], ACT.Copy).then_inc(rounded, 1)

    def split_job(dve, p, i, u, kt):
        j = p.base + u
        dve.wait_ge(rounded, i * len(p.jobs) + (j + 1))
        nc.vector.tensor_tensor(w_lo[:, j % 2, 0:kt], raw[:, j % RING, 0:kt],
                                w_hi[:, j % 2, 0:kt].bitcast(F32), ALU.subtract).then_inc(split, 1)

    def run_phase(eng, p, work, prepare, last=False):
        nj = len(p.jobs)

        def body(i, ahead):
            for u in range(nj):
                if ahead or u < nj - 1:
                    prepare(eng, p, i, u + 1, p.next_kt[u])
                if work is not None:
                    work(i, u)
        n = p.n - 1 if last else p.n
        if n == 1:
            body(0, True)
        elif n > 1:
            with eng.Fori(0, n) as i:
                body(i, True)
        if last:
            body(p.n - 1, False)

    def result_ready(eng, p, i, u):
        eng.wait_ge(multiplied, i * len(p.jobs) + (p.base + u + 3))

    def multiply_job(pe, p, i, u, acc, moving, kt, w, start, stop):
        j = p.base + u
        pe.wait_ge(split, i * len(p.jobs) + (j + RING + 1))
        for k in range(kt):
            mh, ml = moving(k)
            nc.tensor.matmul(acc, w_hi[:, j % 2, k, 0:w], mh, start=start and k == 0, stop=False)
            nc.tensor.matmul(acc, w_hi[:, j % 2, k, 0:w], ml, start=False, stop=False)
            last = nc.tensor.matmul(acc, w_lo[:, j % 2, k, 0:w], mh, start=False, stop=stop and k == kt - 1)
        last.then_inc(multiplied, 1)

    results, count = {}, 0
    for name, p in ph.items():
        per = len(p.jobs) // 2 if name.startswith("down") else 0 if name == "out" else len(p.jobs)
        results[name] = (count, per)
        count += p.n * per

    def bank(name, u):
        return (results[name][0] + u) % 2

    def bank_free(pe, name, i, u):
        first, per = results[name]
        pe.wait_ge(drained[bank(name, u)], i * (per // 2) + ((first + u) // 2 + 1))

    def result_out(eng, name, i, u):
        first, per = results[name]
        eng.wait_ge(drained[bank(name, u)], i * (per // 2) + ((first + u) // 2 + 2))

    def phases_out(eng, name):
        first = results[name][0]
        for b in range(2):
            eng.wait_ge(drained[b], (first - b + 1) // 2 + 1)

    def multiply_phase(pe, name, n_cols):
        p = ph[name]

        def body(i):
            for u, (kt, w, _) in enumerate(p.jobs):
                bank_free(pe, name, i, u)
                multiply_job(pe, p, i, u, ps[0:w, bank(name, u), 0:n_cols],
                             lambda k: (x_hi[:, k, 0:n_cols], x_lo[:, k, 0:n_cols]), kt, w, True, True)
        if p.n == 1:
            body(0)
        else:
            with pe.Fori(0, p.n) as i:
                body(i)

    def tile_of(buf, first, i, per):
        if isinstance(i, int):
            return buf[:, first + per * i]
        return buf[:, first:][:, bass.ds(i * per, 1)].rearrange("p a t -> p (a t)")

    def keep_results(act, name, to):
        p = ph[name]

        def work(i, u):
            result_ready(act, p, i, u)
            w, dst = p.jobs[u][1], to(i, u)
            nc.scalar.activation(dst, ps[0:w, bank(name, u), 0:dst.shape[-1]], ACT.Copy).then_inc(drained[bank(name, u)], 1)
        run_phase(act, p, work, round_job)

    def add_residual(dve, name):
        p = ph[name]

        def work(i, u):
            result_ready(dve, p, i, u)
            t = tile_of(h, u, i, len(p.jobs))
            nc.vector.tensor_tensor(t, ps[:, bank(name, u), 0:T], t, ALU.add).then_inc(drained[bank(name, u)], 1)
        run_phase(dve, p, work, split_job)

    xn = view(arena, 0, DK, T)

    def norm_tensor(pe, n, c0):
        w = T - c0
        for g in range(4):
            pe.wait_ge(norm_sq, 4 * n + g + 1)
            for k in range(4 * g, 4 * g + 4):
                mm = nc.tensor.matmul(ps[:, 2, 0:w], ones[:], xn[:, k, 0:w], start=(k == 0), stop=(k == DK - 1))
        mm.then_inc(norm_sum, 1)

    def norm_scalar(act, n, c0, split_out):
        w = T - c0
        for g in range(4):
            t = slice(4 * g, 4 * g + 4)
            nc.scalar.activation(xn[:, t, 0:w], h[:, t, c0:T], ACT.Square).then_inc(norm_sq, 1)
        act.wait_ge(norm_sum, n + 1)
        nc.scalar.activation(ps[:, 3, 0:w], ps[:, 2, 0:w], ACT.Sqrt, bias=eps[:, 0:1], scale=1.0 / D).then_inc(norm_std, 1)
        for g in range(4):
            t = slice(4 * g, 4 * g + 4)
            if split_out:
                act.wait_ge(norm_xn, 4 * n + g + 1)
                nc.scalar.activation(x_hi[:, t, 0:w], xn[:, t, 0:w], ACT.Copy).then_inc(norm_hi, 1)
            else:
                act.sem_inc(norm_hi, 1)

    def norm_vector(dve, n, c0, gain, to=None):
        w = T - c0
        dve.wait_ge(norm_std, n + 1)
        nc.vector.reciprocal(ps[:, 3, 0:w], ps[:, 3, 0:w])
        dve.drain()
        for g in range(4):
            for k in range(4 * g, 4 * g + 4):
                mm = nc.vector.scalar_tensor_tensor(out=xn[:, k, 0:w] if to is None else to(k), in0=h[:, k, c0:T],
                                                    scalar=gain(k), in1=ps[:, 3, 0:w], op0=ALU.mult, op1=ALU.mult)
            mm.then_inc(norm_xn, 1)
        if to is None:
            for g in range(4):
                t = slice(4 * g, 4 * g + 4)
                dve.wait_ge(norm_hi, 4 * n + g + 1)
                nc.vector.tensor_tensor(x_lo[:, t, 0:w], xn[:, t, 0:w], x_hi[:, t, 0:w].bitcast(F32), ALU.subtract)

    hid_hi = act_hi[:, 0:FH * T].rearrange("p (k t) -> p k t", k=FH)
    hid_lo = act_lo[:, 0:FH * T].rearrange("p (k t) -> p k t", k=FH)
    FT0 = 2 * 24 * SEQ
    f_gate, f_val = view(arena, FT0, 2, T), view(arena, FT0 + 2 * T, 2, T)
    f_act, f_hid = view(arena, FT0 + 4 * T, 2, T), view(arena, FT0 + 6 * T, 2, T)

    def ffn_tap(layer, f, t, is_gate, i, s):
        return col("ffn_dw", i * 2 + ((layer * FFN_K + t) * 2 * FF + is_gate * FF + f * FH + s))

    def ffn_scalar(act, layer, f):
        name, n0 = f"up{layer}{f}", (2 * layer + f) * FH
        p = ph[name]

        def high(i, s):
            act.wait_ge(hid_made, i * 2 + (n0 + s + 1))
            nc.scalar.activation(tile_of(hid_hi, s, i, 2), f_hid[:, s], ACT.Copy).then_inc(hid_hi_made, 1)

        def work(i, u):
            s, is_gate = u // 2, 1 - u % 2
            if u == 2:
                high(i, 0)
            result_ready(act, p, i, u)
            nc.scalar.activation((f_gate if is_gate else f_val)[:, s], ps[:, bank(name, u), 0:T], ACT.Copy,
                                 scale=ffn_tap(layer, f, 2, is_gate, i, s)).then_inc(hid_tap, 1)
            if not is_gate:
                result_out(act, name, i, u - 1)
                nc.scalar.activation(f_act[:, s], f_gate[:, s], ACT.Silu).then_inc(hid_silu, 1)
            if u == 3:
                high(i, 1)
        run_phase(act, p, work, round_job)
        run_phase(act, ph[f"down{layer}{f}"], None, round_job)

    def ffn_vector(dve, layer, f):
        name, n0 = f"up{layer}{f}", (2 * layer + f) * FH
        p = ph[name]

        def low(i, s):
            dve.wait_ge(hid_hi_made, i * 2 + (n0 + s + 1))
            nc.vector.tensor_tensor(tile_of(hid_lo, s, i, 2), f_hid[:, s], tile_of(hid_hi, s, i, 2).bitcast(F32),
                                    ALU.subtract).then_inc(hid_lo_made, 1)

        def work(i, u):
            s, is_gate = u // 2, 1 - u % 2
            if u == 2:
                low(i, 0)
            dst, acc = (f_gate if is_gate else f_val), ps[:, bank(name, u), 0:T]
            dve.wait_ge(hid_tap, i * 4 + (2 * n0 + u + 1))
            for back in (1, 2):
                mm = nc.vector.scalar_tensor_tensor(out=dst[:, s, back:T], in0=acc[:, 0:T - back],
                                                    scalar=ffn_tap(layer, f, 2 - back, is_gate, i, s),
                                                    in1=dst[:, s, back:T], op0=ALU.mult, op1=ALU.add)
                if back == 1:
                    dve.drain()
            mm.then_inc(drained[bank(name, u)], 1)
            if not is_gate:
                dve.drain()
                dve.wait_ge(hid_silu, i * 2 + (n0 + s + 1))
                nc.vector.tensor_tensor(f_hid[:, s], f_act[:, s], f_val[:, s], ALU.mult).then_inc(hid_made, 1)
            if u == 3:
                dve.drain()
                low(i, 1)
        run_phase(dve, p, work, split_job)
        name2 = f"down{layer}{f}"
        p2 = ph[name2]

        def add(i, u):
            if u % 2:
                result_ready(dve, p2, i, u)
                t = tile_of(h, u // 2, i, 2)
                nc.vector.tensor_tensor(t, ps[:, bank(name2, u // 2), 0:T], t, ALU.add).then_inc(drained[bank(name2, u // 2)], 1)
        run_phase(dve, p2, add, split_job)

    def ffn_tensor(pe, layer, f):
        multiply_phase(pe, f"up{layer}{f}", T)
        name, half = f"down{layer}{f}", FH // 2
        p = ph[name]
        pe.wait_ge(hid_lo_made, (2 * layer + f + 1) * FH)
        with pe.Fori(0, p.n) as i:
            for u, (kt, w, _) in enumerate(p.jobs):
                part = u % 2
                if part == 0:
                    bank_free(pe, name, i, u // 2)
                multiply_job(pe, p, i, u, ps[:, bank(name, u // 2), 0:T],
                             lambda k: (hid_hi[:, part * half + k, :], hid_lo[:, part * half + k, :]),
                             kt, w, part == 0, part == 1)

    ab_sig, ab_sb, ab_sc = view(arena, 0, CW, T), view(arena, 2176, CW, T), view(arena, 4352, CW, T)
    ab_conv = view(arena, 6528, CW, T)
    ab_a = view(arena, 8704, CW, T + CONF_K - 1)
    ab_s = view(arena, 11136, CW, T + SC_K - 1)
    ab_v, ab_act, ab_t = trio("ab")
    AB_V = order("s_made", "centred", "normed")
    AB_S = order("s_hi", "mean", "squared", "std", "a_made", "a_hi")
    AB_T = order("sums", "squares")

    def ab_in_scalar(act):
        p = ph["ab_gate"]

        def gate(i, u):
            result_ready(act, p, i, u)
            nc.scalar.activation(tile_of(ab_sig, u, i, 4), ps[:, bank("ab_gate", u), 0:T],
                                 ACT.Sigmoid).then_inc(drained[bank("ab_gate", u)], 1)
        run_phase(act, p, gate, round_job)
        run_phase(act, ph["ab_val"], None, round_job)
        p2 = ph["ab_s"]

        def keep(i, u):
            if u < 8:
                result_ready(act, p2, i, u)
                nc.scalar.activation(tile_of(ab_sb if u < 4 else ab_sc, u % 4, i, 4), ps[:, bank("ab_s", u), 0:T],
                                     ACT.Copy).then_inc(drained[bank("ab_s", u)], 1)
        run_phase(act, p2, keep, round_job)

    def ab_in_vector(dve):
        run_phase(dve, ph["ab_gate"], None, split_job)
        phases_out(dve, "ab_val")
        p = ph["ab_val"]

        def gated(i, u):
            result_ready(dve, p, i, u)
            nc.vector.tensor_tensor(tile_of(ab_a, u, i, 4)[:, CONF_K - 1:], ps[:, bank("ab_val", u), 0:T],
                                    tile_of(ab_sig, u, i, 4), ALU.mult).then_inc(drained[bank("ab_val", u)], 1)
        run_phase(dve, p, gated, split_job)
        p2 = ph["ab_s"]

        def conv(i, u):
            if u >= 8:
                result_ready(dve, p2, i, u)
                result_out(dve, "ab_s", i, u - 4)
                nc.vector.tensor_tensor(tile_of(ab_s, u - 8, i, 4)[:, SC_K - 1:], ps[:, bank("ab_s", u), 0:T],
                                        tile_of(ab_sc, u - 8, i, 4), ALU.mult).then_inc(drained[bank("ab_s", u)], 1)
            tile, third = u // 3, u % 3
            src, dst = tile_of(ab_a, tile, i, 4), tile_of(ab_conv, tile, i, 4)
            for t in range((CONF_K * third + 2) // 3, (CONF_K * (third + 1) + 2) // 3):
                dve.drain()
                wt = col("ab_conf_dw", i * 4 + (t * CW + tile))
                if t == 0:
                    nc.vector.tensor_scalar(dst, src[:, 0:T], wt, col("ab_conf_dw_b", i * 4 + tile), ALU.mult, ALU.add)
                else:
                    nc.vector.scalar_tensor_tensor(out=dst, in0=src[:, t:t + T], scalar=wt, in1=dst,
                                                   op0=ALU.mult, op1=ALU.add)
        run_phase(dve, p2, conv, split_job)

    def ab_vector(dve):
        for t in range(SC_K):
            for k in range(CW):
                wt, dst = col("ab_sc_dw", t * CW + k), ab_sig[:, k]
                if t == 0:
                    nc.vector.tensor_scalar(dst, ab_s[:, k, 0:T], wt, None, ALU.mult)
                else:
                    nc.vector.scalar_tensor_tensor(out=dst, in0=ab_s[:, k, t:t + T], scalar=wt, in1=dst,
                                                   op0=ALU.mult, op1=ALU.add)
            dve.drain()
        nc.vector.tensor_tensor(ab_sb, ab_sb, ab_sig, ALU.mult).then_inc(ab_v, 1)
        dve.drain()
        dve.wait_ge(ab_act, AB_S["s_hi"])
        nc.vector.tensor_tensor(x_lo[:, CW:DK], ab_sb, x_hi[:, CW:DK].bitcast(F32), ALU.subtract)
        dve.wait_ge(ab_act, AB_S["mean"])
        mean = ps[:, 4, 0:T].unsqueeze(1).to_broadcast([P, CW, T])
        nc.vector.tensor_tensor(ab_conv, ab_conv, mean, ALU.subtract).then_inc(ab_v, 1)
        dve.wait_ge(ab_act, AB_S["std"])
        nc.vector.reciprocal(ps[:, 5, 0:T], ps[:, 5, 0:T])
        dve.drain()
        rstd = ps[:, 5, 0:T].unsqueeze(1).to_broadcast([P, CW, T])
        nc.vector.tensor_tensor(ab_conv, ab_conv, rstd, ALU.mult).then_inc(ab_v, 1)
        dve.wait_ge(ab_act, AB_S["a_hi"])
        nc.vector.tensor_tensor(x_lo[:, 0:CW], ab_conv, x_hi[:, 0:CW].bitcast(F32), ALU.subtract)

    def ab_scalar(act):
        act.wait_ge(ab_v, AB_V["s_made"])
        nc.scalar.activation(x_hi[:, CW:DK], ab_sb, ACT.Copy).then_inc(ab_act, 1)
        act.wait_ge(ab_t, AB_T["sums"])
        nc.scalar.activation(ps[:, 4, 0:T], ps[:, 2, 0:T], ACT.Copy, scale=1.0 / 1024).then_inc(ab_act, 1)
        act.wait_ge(ab_v, AB_V["centred"])
        nc.scalar.activation(ab_sc, ab_conv, ACT.Square).then_inc(ab_act, 1)
        act.wait_ge(ab_t, AB_T["squares"])
        nc.scalar.activation(ps[:, 5, 0:T], ps[:, 3, 0:T], ACT.Sqrt, bias=eps[:, 1:2], scale=1.0 / 1024).then_inc(ab_act, 1)
        act.wait_ge(ab_v, AB_V["normed"])
        for k in range(CW):
            mm = nc.scalar.activation(ab_conv[:, k], ab_conv[:, k], ACT.Silu, scale=col("ab_conf_ln_g", k),
                                      bias=col("ab_conf_ln_b", k))
        mm.then_inc(ab_act, 1)
        act.drain()
        nc.scalar.activation(x_hi[:, 0:CW], ab_conv, ACT.Copy).then_inc(ab_act, 1)

    def ab_tensor(pe):
        for k in range(CW):
            mm = nc.tensor.matmul(ps[:, 2, 0:T], ones[:], ab_conv[:, k], start=(k == 0), stop=(k == CW - 1))
        mm.then_inc(ab_t, 1)
        pe.wait_ge(ab_act, AB_S["squared"])
        for k in range(CW):
            mm = nc.tensor.matmul(ps[:, 3, 0:T], ones[:], ab_sc[:, k], start=(k == 0), stop=(k == CW - 1))
        mm.then_inc(ab_t, 1)
    GT = GLA_H * T
    zg = view(arena, 0, 24, T)
    g_low = arena[0:META, 6528:6528 + T]
    g_x, g_e = view(arena, 6800, GLA_H, T), view(arena, 7888, GLA_H, T)
    g_cum, g_end = view(arena, 8976, GLA_H, T), view(arena, 10064, GLA_H, T)
    g_dec = view(arena, 11152, GLA_H, 8)
    g_w2 = arena[0:META, 11200:11712]
    g_kd, g_ks, g_v = arena[:, 11712:11984], arena[:, 11984:12256], view(arena, 12256, 2, T)
    g_tok = view(arena, 12800, 3, 3 * P)
    g_sc = view(arena, 13952, 3, P)
    g_state = view(arena, 14336, 4, 2 * P)
    o_gla = view(arena, 16256, CW, T)
    gla_v, gla_s, gla_t = trio("gla")
    GLA_V = order("biased", "shifted", "summed", "ends", "q_ready")
    GLA_S = order("log", "grown", "shrunk", "to_end", "gate")
    GLA_T = order("low_rank")
    glh_v, glh_s, glh_t = trio("glh")
    GLH_V = order("staged", "masked", "chained")
    GLH_S = order("kept", "out")
    GLH_T = order("turned", "states", "mixed")
    gle_v, gle_s, gle_t = trio("gle")
    GLE_S = order("squared", "std")
    GLE_T = order("sums")
    CHUNK_AT = [(0, META)] + [(META + GLA_CHUNK * c, GLA_CHUNK) for c in range(4)]

    def gla_prepare_vector(dve):
        dve.wait_ge(gla_t, GLA_T["low_rank"])
        for hd in range(GLA_H):
            mm = nc.vector.tensor_scalar(g_x[:, hd], ps[:, hd, 0:T], col("cd_gla_b", hd), None, ALU.add)
        mm.then_inc(gla_v, 1)
        dve.wait_ge(gla_s, GLA_S["log"])
        nc.vector.scalar_tensor_tensor(out=g_x, in0=g_x, scalar=0.0, in1=g_e, op0=ALU.min,
                                       op1=ALU.subtract).then_inc(gla_v, 1)
        dve.drain()
        dve.wait_ge(seg_made, 1)
        for hd in range(GLA_H):
            mm = nc.vector.tensor_tensor_scan(g_cum[:, hd], seg[:], g_x[:, hd], 0.0, ALU.mult, ALU.add)
        mm.then_inc(gla_v, 1)
        dve.drain()
        nc.vector.tensor_tensor(g_end[:, :, 0:META], g_cum[:, :, META - 1:META].to_broadcast([P, GLA_H, META]),
                                g_cum[:, :, 0:META], ALU.subtract)
        for hd in range(GLA_H):
            c = g_cum[:, hd, META:].rearrange("p (c t) -> p c t", t=GLA_CHUNK)
            e = g_end[:, hd, META:].rearrange("p (c t) -> p c t", t=GLA_CHUNK)
            mm = nc.vector.tensor_tensor(e, c[:, :, GLA_CHUNK - 1:].to_broadcast([P, 4, GLA_CHUNK]), c, ALU.subtract)
        mm.then_inc(gla_v, 1)
        dve.wait_ge(gla_s, GLA_S["grown"])
        nc.vector.scalar_tensor_tensor(out=zg[:, 0:4], in0=zg[:, 0:4], scalar=GLA_SCALE, in1=g_x,
                                       op0=ALU.mult, op1=ALU.mult).then_inc(gla_v, 1)
        dve.wait_ge(gla_s, GLA_S["to_end"])
        nc.vector.tensor_tensor(g_end, zg[:, 4:8], g_end, ALU.mult)
        dve.drain()
        nc.vector.tensor_tensor(zg[:, 4:8], zg[:, 4:8], g_e, ALU.mult)
        dve.drain()

    def gla_prepare_scalar(act):
        act.wait_ge(gla_v, GLA_V["biased"])
        nc.scalar.activation(g_e, g_x, ACT.Abs)
        act.drain()
        nc.scalar.activation(g_e, g_e, ACT.Exp, scale=-1.0)
        act.drain()
        nc.scalar.activation(g_e, g_e, ACT.Ln, bias=eps[:, 3:4]).then_inc(gla_s, 1)
        act.wait_ge(gla_v, GLA_V["summed"])
        nc.scalar.activation(g_x, g_cum, ACT.Exp, scale=1.0 / GLA_NORM).then_inc(gla_s, 1)
        nc.scalar.activation(g_e, g_cum, ACT.Exp, scale=-1.0 / GLA_NORM).then_inc(gla_s, 1)
        nc.scalar.activation(g_dec[:, :, 0:1], g_cum[:, :, META - 1:META], ACT.Exp, scale=1.0 / GLA_NORM)
        nc.scalar.activation(g_dec[:, :, 1:5], g_cum[:, :, META + GLA_CHUNK - 1::GLA_CHUNK], ACT.Exp, scale=1.0 / GLA_NORM)
        act.wait_ge(gla_v, GLA_V["ends"])
        nc.scalar.activation(g_end, g_end, ACT.Exp, scale=1.0 / GLA_NORM).then_inc(gla_s, 1)
        nc.scalar.activation(zg[:, 16:24], zg[:, 16:24], ACT.Silu).then_inc(gla_s, 1)

    def gla_prepare_tensor(pe):
        pe.wait_ge(side_in, 16)
        for hd in range(GLA_H):
            mm = nc.tensor.matmul(ps[:, hd, 0:T], g_w2[:, hd * P:(hd + 1) * P], g_low, start=True, stop=True)
        mm.then_inc(gla_t, 1)

    def gla_heads_vector(dve):
        nc.vector.memset(g_sc, 0.0)
        dve.drain()
        with dve.Fori(0, GLA_H) as hd:
            v, s, t = (hd * len(GLH_V), hd * len(GLH_S), hd * len(GLH_T))
            nc.vector.tensor_copy(g_kd, tile_of(zg, 4, hd, 1))
            nc.vector.tensor_copy(g_ks, tile_of(g_end, 0, hd, 1))
            nc.vector.tensor_copy(g_v, zg[:, 8:][:, bass.ds(hd * 2, 2)]).then_inc(glh_v, 1)
            dve.wait_ge(glh_t, t + GLH_T["turned"])
            settle(dve)
            for tt, (t0, n) in enumerate(TILES):
                mm = nc.vector.copy_predicated(g_sc[0:n, tt, 0:n], le64[0:n, 0:n].bitcast(I32), ps[0:n, 3, tt * P:tt * P + n])
            mm.then_inc(glh_v, 1)
            dve.wait_ge(glh_t, t + GLH_T["states"])
            nc.vector.tensor_copy(g_state[:, 0], ps[:, 4, 0:2 * P])
            added = [None, ps[:, 4, 2 * P:4 * P], ps[:, 5, 0:2 * P], ps[:, 6, 0:2 * P]]
            for c in range(1, 4):
                dve.drain()
                dec = g_dec[:, bass.ds(hd, 1), c:c + 1].rearrange("p a b -> p (a b)")
                mm = nc.vector.scalar_tensor_tensor(out=g_state[:, c], in0=g_state[:, c - 1], scalar=dec, in1=added[c],
                                                    op0=ALU.mult, op1=ALU.add)
            mm.then_inc(glh_v, 1)
            dve.wait_ge(glh_t, t + GLH_T["mixed"])

    def gla_heads_scalar(act):
        with act.Fori(0, GLA_H) as hd:
            v, s, t = (hd * len(GLH_V), hd * len(GLH_S), hd * len(GLH_T))
            act.wait_ge(glh_t, t + GLH_T["turned"])
            for tt, (t0, n) in enumerate(TILES):
                mm = nc.scalar.activation(g_tok[0:n, tt], ps[0:n, tt, 0:3 * P], ACT.Copy)
            mm.then_inc(glh_s, 1)
            act.wait_ge(glh_t, t + GLH_T["mixed"])
            for u in range(2):
                mm = nc.scalar.activation(tile_of(o_gla, u, hd, 2), ps[:, u, 0:T], ACT.Copy)
            mm.then_inc(glh_s, 1)

    def gla_heads_tensor(pe):
        pe.wait_ge(gla_s, GLA_S["gate"])
        with pe.Fori(0, GLA_H) as hd:
            v, s, t = (hd * len(GLH_V), hd * len(GLH_S), hd * len(GLH_T))
            q = tile_of(zg, 0, hd, 1)
            pe.wait_ge(glh_v, v + GLH_V["staged"])
            for tt, (t0, n) in enumerate(TILES):
                for a_, src in enumerate((g_v[:, 0], g_v[:, 1], g_ks)):
                    nc.tensor.transpose(ps[0:n, tt, a_ * P:(a_ + 1) * P], src[:, t0:t0 + n], ident[:])
                mm = nc.tensor.matmul(ps[0:n, 3, tt * P:tt * P + n], g_kd[:, t0:t0 + n], q[:, t0:t0 + n], start=True, stop=True)
            mm.then_inc(glh_t, 1)
            pe.wait_ge(glh_s, s + GLH_S["kept"])
            for c, (tt, r0, n, b, c0) in enumerate([(0, 0, META, 4, 0), (1, 0, 64, 4, 2 * P), (1, 64, 64, 5, 0), (2, 0, 64, 6, 0)]):
                mm = nc.tensor.matmul(ps[:, b, c0:c0 + 2 * P], g_tok[r0:r0 + n, tt, 2 * P:3 * P], g_tok[r0:r0 + n, tt, 0:2 * P],
                                      start=True, stop=True)
            mm.then_inc(glh_t, 1)
            pe.wait_ge(glh_v, v + GLH_V["chained"])
            for u in range(2):
                for c, (c0, cn) in enumerate(CHUNK_AT):
                    tt = (c + 1) // 2
                    t0, n = TILES[tt]
                    mm = nc.tensor.matmul(ps[:, u, c0:c0 + cn], g_tok[0:n, tt, u * P:(u + 1) * P], g_sc[0:n, tt, c0 - t0:c0 - t0 + cn],
                                          start=True, stop=(c == 0))
                    if c:
                        mm = nc.tensor.matmul(ps[:, u, c0:c0 + cn], g_state[:, c - 1, u * P:(u + 1) * P], q[:, c0:c0 + cn],
                                              start=False, stop=True)
            mm.then_inc(glh_t, 1)
            pe.wait_ge(glh_s, s + GLH_S["out"])

    def gla_end_vector(dve):
        dve.wait_ge(gle_s, GLE_S["std"])
        nc.vector.reciprocal(g_x, g_x)
        dve.drain()
        for u in range(2):
            nc.vector.tensor_tensor(o_gla[:, u::2], o_gla[:, u::2], g_x, ALU.mult)
        dve.drain()
        for k in range(CW):
            nc.vector.scalar_tensor_tensor(out=o_gla[:, k], in0=o_gla[:, k], scalar=col("cd_gla_norm_g", k), in1=zg[:, 16 + k],
                                           op0=ALU.mult, op1=ALU.mult)

    def gla_end_scalar(act):
        act.drain()
        sq = view(arena, 8976, CW, T)
        nc.scalar.activation(sq, o_gla, ACT.Square).then_inc(gle_s, 1)
        act.wait_ge(gle_t, GLE_T["sums"])
        for hd in range(GLA_H):
            mm = nc.scalar.activation(g_x[:, hd], ps[:, hd, 0:T], ACT.Sqrt, bias=eps[:, 0:1], scale=1.0 / 256)
        mm.then_inc(gle_s, 1)

    def gla_end_tensor(pe):
        sq = view(arena, 8976, CW, T)
        pe.wait_ge(gle_s, GLE_S["squared"])
        for hd in range(GLA_H):
            for u in range(2):
                mm = nc.tensor.matmul(ps[:, hd, 0:T], ones[:], sq[:, 2 * hd + u], start=(u == 0), stop=(u == 1))
        mm.then_inc(gle_t, 1)

    ZW = T + 1
    zr = view(arena, 0, 26, ZW)
    zt = zr[:, :, 1:ZW]
    NP = 2
    NH = 2 * NP
    CH = [(0, META)] + [(META + RW_CHUNK * c, RW_CHUNK) for c in range(SEQ // RW_CHUNK)]

    def temp(n):
        return view(arena, 7104 + 544 * n, NP, T)

    (r_prev, r_a, r_cum, r_kend, r_grow, r_kh, r_kk, r_x, r_k2, r_bend) = (temp(n) for n in range(10))
    r_ar = view(arena, 7104 + 544 * 10, NP, 2, T)
    r_bh, r_bonus, r_g, r_val = temp(12), temp(13), temp(14), temp(15)
    r_wst, r_gst = view(arena, 7104 + 544 * 14, NP, P), view(arena, 7104 + 544 * 14 + 256, NP, P)
    r_wend = view(arena, 7104 + 544 * 16, 9, NP)
    r_f = r_prev
    r_q1, r_p1, r_l21, r_y, r_p2, r_q2 = (view(arena, 7104 + 544 * n, NH, P) for n in (1, 2, 4, 6, 7, 8))
    r_p4, r_q4, r_p8, r_t16, r_z1 = r_p1, r_q1, r_p2, r_p1, r_q2
    r_mm = view(work2, 0, NH, 4, P)
    r_tok = view(work2, 2048, NP, 4, P)
    r_gin, r_gh = view(work2, 3072, NH, P), view(work2, 3584, NH, P)
    r_trans = view(work2, 4096, 8, NP, P)
    r_add = view(work2, 6144, 8, NP, RW_N)
    r_state = view(work2, 7168, 8, NP, RW_N)
    rws_v, rws_s, rws_t = trio("rws")
    RWS_V, RWS_S = order("mixed"), order("low")
    rw_v, rw_s, rw_t = trio("rw")
    big = [f"{s}{t}" for t in (1, 2) for s in ("m", "q2", "q4", "y4", "y8", "z1", "t32", "fe")]
    RW_V = order("staged", "keys", "cum", "bonus", "ready", "m0", "q20", "q40", "y40", "y80", "fe0", *big,
                 *[f"s{c}" for c in range(1, 9)], "end")
    big = [f"{s}{t}" for t in (1, 2) for s in ("tok", "p2", "p4", "p8", "t16", "gh", "add")]
    RW_S = order("norm", "rates", "decays", "kept", "tok0", "p20", "p40", "p80", "gh0", "add0", *big)
    big = [f"{s}{t}" for t in (1, 2) for s in ("x", "p2", "p4", "p8", "y8", "z1", "w", "gh", "fe")]
    RW_T = order("gates", "norm", "bonus", "x0", "p20", "p40", "p80", "y80", "gh0", "fe0", *big,
                 *[f"s{c}" for c in range(2, 9)], "y")
    rwf_v, rwf_s, rwf_t = trio("rwf")
    RWF_V, RWF_S, RWF_T = order("centred"), order("squared", "std"), order("sums", "squares")

    def pair(buf, first, q):
        return buf[:, first:][:, bass.ds(q * NP, NP)]

    def rw_mix_vector(dve):
        for k in range(26):
            d = arena[:, 7104 + (k % 2) * 544:7104 + (k % 2) * 544 + T]
            nc.vector.tensor_tensor(d, zr[:, k, 0:T], zt[:, k], ALU.subtract)
            dve.drain()
            mm = nc.vector.scalar_tensor_tensor(out=zt[:, k], in0=d, scalar=col("cd_rw_mu", k), in1=zt[:, k],
                                                op0=ALU.mult, op1=ALU.add)
        mm.then_inc(rws_v, 1)
        dve.drain()

    def rw_mix_scalar(act):
        act.wait_ge(rws_v, RWS_V["mixed"])
        nc.scalar.activation(zt[0:64, 24], zt[0:64, 24], ACT.Tanh)
        nc.scalar.activation(zt[:, 25], zt[:, 25], ACT.Sigmoid).then_inc(rws_s, 1)

    def rw_vector(dve):
        dve.wait_ge(seg_made, 2)
        dve.wait_ge(side_in, 64)
        nc.vector.memset(view(work2, 4096, 2048), 0.0)
        dve.drain()
        with dve.Fori(0, 8 // NP) as q:
            V, S, TT = q * len(RW_V), q * len(RW_S), q * len(RW_T)

            def done(ins):
                ins.then_inc(rw_v, 1)
            nc.vector.tensor_copy(r_wst, side[:, 0:1024].rearrange("p (a b) -> p a b", b=P)[:, bass.ds(q * NP, NP)])
            done(nc.vector.tensor_copy(r_gst, side[:, 1024:2048].rearrange("p (a b) -> p a b", b=P)[:, bass.ds(q * NP, NP)]))
            nc.vector.tensor_copy(r_val, pair(zt, 16, q))
            for p_ in range(NP):
                nc.vector.tensor_scalar(r_kk[:, p_], tile_of(zt, 8 + p_, q, NP), col("cd_rw_kk", q * NP + p_), None, ALU.mult)
            dve.drain()
            done(nc.vector.tensor_tensor(r_x, r_kk, r_kk, ALU.mult))
            dve.wait_ge(rw_s, S + RW_S["rates"])
            for p_ in range(NP):
                nc.vector.tensor_scalar(r_k2[:, p_], r_a[:, p_], col("cd_rw_ka", q * NP + p_),
                                        omka[:, bass.ds(q * NP + p_, 1)], ALU.mult, ALU.add)
                nc.vector.tensor_tensor_scan(r_cum[:, p_], seg[:], r_prev[:, p_], 0.0, ALU.mult, ALU.add)
            dve.drain()
            nc.vector.tensor_tensor(r_prev, r_cum, r_prev, ALU.subtract)
            nc.vector.tensor_tensor(r_kend[:, :, 0:META], r_cum[:, :, META - 1:META].to_broadcast([P, NP, META]),
                                    r_cum[:, :, 0:META], ALU.subtract)
            for p_ in range(NP):
                c = r_cum[:, p_, META:].rearrange("p (c t) -> p c t", t=RW_CHUNK)
                e = r_kend[:, p_, META:].rearrange("p (c t) -> p c t", t=RW_CHUNK)
                mm = nc.vector.tensor_tensor(e, c[:, :, RW_CHUNK - 1:].to_broadcast([P, 8, RW_CHUNK]), c, ALU.subtract)
            done(mm)
            nc.vector.tensor_tensor(r_k2, r_k2, pair(zt, 8, q), ALU.mult)
            dve.wait_ge(rw_s, S + RW_S["norm"])
            nc.vector.tensor_scalar(r_x, r_x, 1e-12, None, ALU.max)
            dve.drain()
            nc.vector.reciprocal(r_x, r_x)
            dve.drain()
            nc.vector.tensor_tensor(r_kk, r_kk, r_x, ALU.mult)
            dve.drain()
            for p_ in range(NP):
                mm = nc.vector.scalar_tensor_tensor(out=r_x[:, p_], in0=tile_of(zt, p_, q, NP), scalar=col("cd_rw_rk", q * NP + p_),
                                                    in1=r_k2[:, p_], op0=ALU.mult, op1=ALU.mult)
            done(mm)
            nc.vector.tensor_tensor(r_bend, r_kk, r_a, ALU.mult)
            dve.wait_ge(rw_s, S + RW_S["decays"])
            nc.vector.tensor_tensor(r_ar[:, :, 0], r_kk, r_prev, ALU.mult)
            nc.vector.tensor_tensor(r_ar[:, :, 1], pair(zt, 0, q), r_grow, ALU.mult)
            dve.drain()
            nc.vector.tensor_tensor(r_bh, r_bend, r_kh, ALU.mult)
            dve.drain()
            nc.vector.tensor_tensor(r_kh, r_k2, r_kh, ALU.mult)
            nc.vector.tensor_tensor(r_bend, r_bend, r_cum, ALU.mult)
            nc.vector.tensor_tensor(r_kend, r_k2, r_cum, ALU.mult)
            dve.drain()
            for hh in range(2):
                w = r_wend[64 * hh:64 * hh + 64, 1:9].rearrange("p c (a b) -> p c a b", b=1).to_broadcast([64, 8, NP, RW_N])
                e = eye2[64 * hh:64 * hh + 64, :].unsqueeze(1).unsqueeze(1).to_broadcast([64, 8, NP, RW_N])
                mm = nc.vector.tensor_tensor(r_trans[64 * hh:64 * hh + 64, :, :, 64 * hh:64 * hh + 64], e, w, ALU.mult)
            done(mm)
            dve.drain()
            for tt, (t0, n) in enumerate(TILES):
                dve.wait_ge(rw_t, TT + RW_T[f"x{tt}"])
                for hd in range(NH):
                    nc.vector.tensor_tensor(r_mm[0:n, hd, :, 0:n], ps[0:n, hd, 0:4 * n].rearrange("p (a b) -> p a b", a=4),
                                            rw_mask[0:n, :, 0:n], ALU.mult)
                lo_ = low16[0:n, 0:n].unsqueeze(1).to_broadcast([n, NP, n])
                l2_ = low21[0:n, 0:n].unsqueeze(1).to_broadcast([n, NP, n])
                for hh in range(2):
                    src = ps[0:n, 4 + hh, 0:NP * n].rearrange("p (a b) -> p a b", a=NP)
                    nc.vector.tensor_tensor(r_p1[0:n, hh::2, 0:n], src, lo_, ALU.mult)
                    if n == P:
                        nc.vector.tensor_tensor(r_l21[:, hh::2, :], src, l2_, ALU.mult)
                dve.drain()
                nc.vector.tensor_tensor(r_q1[0:n, :, 0:n], r_mm[0:n, :, 0, 0:n], up16[0:n, 0:n].unsqueeze(1).to_broadcast([n, NH, n]), ALU.mult)
                dve.drain()
                done(nc.vector.tensor_tensor(r_y[0:n, :, 0:n], r_q1[0:n, :, 0:n],
                                             ident[0:n, 0:n].unsqueeze(1).to_broadcast([n, NH, n]), ALU.add))

                def res(b):
                    return ps[0:n, b, 0:NH * n].rearrange("p (a b) -> p a b", a=NH)
                y = r_y[0:n, :, 0:n]
                dve.wait_ge(rw_t, TT + RW_T[f"p2{tt}"])
                done(nc.vector.tensor_copy(r_q2[0:n, :, 0:n], res(1)))
                dve.wait_ge(rw_t, TT + RW_T[f"p4{tt}"])
                nc.vector.tensor_tensor(y, y, res(3), ALU.add)
                done(nc.vector.tensor_copy(r_q4[0:n, :, 0:n], res(5)))
                dve.drain()
                dve.wait_ge(rw_t, TT + RW_T[f"p8{tt}"])
                done(nc.vector.tensor_tensor(y, y, res(6), ALU.add))
                dve.drain()
                dve.wait_ge(rw_t, TT + RW_T[f"y8{tt}"])
                done(nc.vector.tensor_tensor(y, y, res(0), ALU.add))
                if n == P:
                    dve.wait_ge(rw_t, TT + RW_T[f"z1{tt}"])
                    done(nc.vector.tensor_copy(r_z1, res(2)))
                    dve.drain()
                    dve.wait_ge(rw_t, TT + RW_T[f"w{tt}"])
                    done(nc.vector.tensor_tensor(y, y, res(3), ALU.subtract))
                dve.wait_ge(rw_t, TT + RW_T[f"fe{tt}"])
                settle(dve)
                mm = nc.vector.tensor_copy(pair(zt, 8, q)[:, :, t0:t0 + n], ps[:, 6, 0:NP * n].rearrange("p (a b) -> p a b", a=NP))
                if n == P:
                    nc.vector.tensor_tensor(r_f[:, :, t0:t0 + n], r_ar[:, :, 1, t0:t0 + n],
                                            ps[:, 5, 0:NP * n].rearrange("p (a b) -> p a b", a=NP), ALU.add)
                    dve.wait_ge(rw_s, S + RW_S[f"add{tt}"])
                    for hh in range(2):
                        c = 4 * (tt - 1)
                        tr = r_trans[64 * hh:64 * hh + 64, c:c + 4, :, 64 * hh:64 * hh + 64]
                        mm = nc.vector.tensor_tensor(tr, tr, ps[64 * hh:64 * hh + 64, 0:4, 0:NP * P].rearrange(
                            "p c (a b) -> p c a b", a=NP)[:, :, :, 0:RW_N], ALU.add)
                done(mm)
            dve.wait_ge(rw_s, S + RW_S["add2"])
            done(nc.vector.tensor_copy(r_state[:, 0], r_add[:, 0]))
            for c in range(2, 9):
                dve.wait_ge(rw_t, TT + RW_T[f"s{c}"])
                done(nc.vector.tensor_tensor(r_state[:, c - 1], r_add[:, c - 1],
                                             ps[:, c % 2, 0:NP * RW_N].rearrange("p (a b) -> p a b", a=NP), ALU.add))
            dve.drain()
            dve.wait_ge(rw_t, TT + RW_T["y"])
            for p_ in range(NP):
                for hh in range(2):
                    yo = tile_of(zt[64 * hh:64 * hh + 64], 8 + p_, q, NP)[:, META:]
                    nc.vector.tensor_tensor(yo, yo, ps[64 * hh:64 * hh + 64, 2 + 2 * p_ + hh, META:T], ALU.add)
            nc.vector.tensor_copy(pair(zt, 0, q), r_g)
            done(nc.vector.tensor_tensor(pair(zt, 16, q), r_val, r_bonus, ALU.mult))
            dve.drain()

    def rw_scalar(act):
        with act.Fori(0, 8 // NP) as q:
            V, S, TT = q * len(RW_V), q * len(RW_S), q * len(RW_T)

            def done(ins):
                ins.then_inc(rw_s, 1)
            act.wait_ge(rw_t, TT + RW_T["norm"])
            for p_ in range(NP):
                mm = nc.scalar.activation(r_x[:, p_], ps[:, 6 + p_, 0:T], ACT.Sqrt)
            done(mm)
            for p_ in range(NP):
                nc.scalar.activation(r_prev[:, p_], ps[:, p_, 0:T], ACT.Sigmoid, bias=col("cd_rw_w0", q * NP + p_))
                mm = nc.scalar.activation(r_a[:, p_], ps[:, 2 + p_, 0:T], ACT.Sigmoid, bias=col("cd_rw_a0", q * NP + p_))
            done(mm)
            for p_ in range(NP):
                nc.scalar.activation(r_g[:, p_], ps[:, 4 + p_, 0:T], ACT.Copy)
            act.wait_ge(rw_v, V + RW_V["cum"])
            nc.scalar.activation(r_wend[:, 0], r_cum[:, :, META - 1], ACT.Exp, scale=-RW_DECAY)
            for p_ in range(NP):
                nc.scalar.activation(r_wend[:, 1:9, p_], r_cum[:, p_, META + RW_CHUNK - 1::RW_CHUNK], ACT.Exp, scale=-RW_DECAY)
            nc.scalar.activation(r_grow, r_cum, ACT.Exp, scale=-RW_DECAY)
            nc.scalar.activation(r_kh, r_cum, ACT.Exp, scale=RW_DECAY)
            nc.scalar.activation(r_prev, r_prev, ACT.Exp, scale=-RW_DECAY)
            act.drain()
            done(nc.scalar.activation(r_cum, r_kend, ACT.Exp, scale=-RW_DECAY))
            act.wait_ge(rw_t, TT + RW_T["bonus"])
            for p_ in range(NP):
                mm = nc.scalar.activation(r_bonus[:, p_], ps[:, 6 + p_, 0:T], ACT.Copy)
            done(mm)
            for tt, (t0, n) in enumerate(TILES):
                def res(b):
                    return ps[0:n, b, 0:NH * n].rearrange("p (a b) -> p a b", a=NH)
                act.wait_ge(rw_t, TT + RW_T[f"x{tt}"])
                for p_ in range(NP):
                    mm = nc.scalar.activation(r_tok[0:n, p_], ps[0:n, 6 + p_, 0:512].rearrange("p (a b) -> p a b", a=4), ACT.Copy)
                done(mm)
                act.wait_ge(rw_t, TT + RW_T[f"p2{tt}"])
                nc.scalar.activation(r_p2[0:n, :, 0:n], res(0), ACT.Copy)
                for p_ in range(NP):
                    nc.scalar.activation(r_gin[0:n, 2 * p_:2 * p_ + 2, 0:RW_N], r_tok[0:n, p_, 0].rearrange("p (a b) -> p a b", a=2), ACT.Copy)
                done(nc.scalar.activation(r_gin[0:n, :, RW_N:], ps[0:n, 2, 0:NH * RW_N].rearrange("p (a b) -> p a b", a=NH), ACT.Copy))
                act.wait_ge(rw_t, TT + RW_T[f"p4{tt}"])
                done(nc.scalar.activation(r_p4[0:n, :, 0:n], res(4), ACT.Copy))
                act.wait_ge(rw_t, TT + RW_T[f"p8{tt}"])
                done(nc.scalar.activation(r_p8[0:n, :, 0:n], res(7), ACT.Copy))
                if n == P:
                    act.wait_ge(rw_t, TT + RW_T[f"z1{tt}"])
                    done(nc.scalar.activation(r_t16, res(1), ACT.Copy))
                act.wait_ge(rw_t, TT + RW_T[f"gh{tt}"])
                done(nc.scalar.activation(r_gh[0:n], ps[0:n, 4, 0:NH * P].rearrange("p (a b) -> p a b", a=NH), ACT.Copy, scale=-1.0))
                act.wait_ge(rw_t, TT + RW_T[f"fe{tt}"])
                first, chunks = (0, 1) if tt == 0 else (4 * tt - 3, 4 if tt == 1 else 3)
                for c in range(chunks):
                    mm = nc.scalar.activation(r_add[:, first + c], ps[:, c, 0:NP * P].rearrange("p (a b) -> p a b", a=NP)[:, :, RW_N:], ACT.Copy)
                done(mm)

    def rw_tensor(pe):
        pe.wait_ge(rws_s, RWS_S["low"])
        with pe.Fori(0, 8 // NP) as q:
            V, S, TT = q * len(RW_V), q * len(RW_S), q * len(RW_T)

            def done(ins):
                ins.then_inc(rw_t, 1)
            pe.wait_ge(rw_v, V + RW_V["staged"])
            for p_ in range(NP):
                nc.tensor.matmul(ps[:, p_, 0:T], r_wst[0:64, p_], zt[0:64, 24], start=True, stop=True)
                nc.tensor.matmul(ps[:, 2 + p_, 0:T], r_wst[64:128, p_], zt[64:128, 24], start=True, stop=True)
                mm = nc.tensor.matmul(ps[:, 4 + p_, 0:T], r_gst[:, p_], zt[:, 25], start=True, stop=True)
            done(mm)
            pe.wait_ge(rw_v, V + RW_V["keys"])
            for p_ in range(NP):
                mm = nc.tensor.matmul(ps[:, 6 + p_, 0:T], pair_ones[:], r_x[:, p_], start=True, stop=True)
            done(mm)
            pe.wait_ge(rw_v, V + RW_V["bonus"])
            for p_ in range(NP):
                mm = nc.tensor.matmul(ps[:, 6 + p_, 0:T], pair_ones[:], r_x[:, p_], start=True, stop=True)
            done(mm)
            pe.wait_ge(rw_v, V + RW_V["ready"])
            pe.wait_ge(rw_s, S + RW_S["kept"])
            settle(pe)
            heads = [(p_, hh) for p_ in range(NP) for hh in range(2)]
            for tt, (t0, n) in enumerate(TILES):
                if tt:
                    pe.wait_ge(rw_v, V + RW_V[f"fe{tt - 1}"])
                    pe.wait_ge(rw_s, S + RW_S[f"add{tt - 1}"])
                for hd, (p_, hh) in enumerate(heads):
                    rows, cols_ = slice(64 * hh, 64 * hh + 64), slice(t0, t0 + n)
                    both = r_ar[rows, p_, :, cols_]
                    nc.tensor.matmul(ps[0:n, hd, 0:2 * n], r_bh[rows, p_, cols_], both, start=True, stop=True)
                    nc.tensor.matmul(ps[0:n, hd, 2 * n:4 * n], r_kh[rows, p_, cols_], both, start=True, stop=True)
                    nc.tensor.matmul(ps[0:n, 4 + hh, p_ * n:(p_ + 1) * n], r_ar[rows, p_, 0, cols_], r_bh[rows, p_, cols_], start=True, stop=True)
                for p_ in range(NP):
                    for k, src in enumerate((r_ar[:, p_, 0], r_bend[:, p_], r_kend[:, p_], r_val[:, p_])):
                        mm = nc.tensor.transpose(ps[0:n, 6 + p_, k * P:(k + 1) * P], src[:, t0:t0 + n], ident[:])
                done(mm)

                def times(b, left, right, w=n):
                    for hd in range(NH):
                        mm = nc.tensor.matmul(ps[0:n, b, hd * w:(hd + 1) * w], left[0:n, hd, 0:n], right(hd), start=True, stop=True)
                    return mm

                def of(buf):
                    return lambda hd: buf[0:n, hd, 0:n]
                pe.wait_ge(rw_v, V + RW_V[f"m{tt}"])
                pe.wait_ge(rw_s, S + RW_S[f"tok{tt}"])
                if n < P:
                    settle(pe)
                times(0, r_q1, of(r_p1))
                times(1, r_p1, of(r_q1))
                done(times(2, r_mm[:, :, 2], lambda hd: r_tok[0:n, hd // 2, 3, 64 * (hd % 2):64 * (hd % 2) + 64], RW_N))
                pe.wait_ge(rw_v, V + RW_V[f"q2{tt}"])
                pe.wait_ge(rw_s, S + RW_S[f"p2{tt}"])
                if n < P:
                    settle(pe)
                times(3, r_p2, of(r_y))
                times(4, r_q2, of(r_p2))
                done(times(5, r_p2, of(r_q2)))
                pe.wait_ge(rw_v, V + RW_V[f"q4{tt}"])
                pe.wait_ge(rw_s, S + RW_S[f"p4{tt}"])
                if n < P:
                    settle(pe)
                times(6, r_p4, of(r_y))
                done(times(7, r_q4, of(r_p4)))
                pe.wait_ge(rw_v, V + RW_V[f"y4{tt}"])
                pe.wait_ge(rw_s, S + RW_S[f"p8{tt}"])
                if n < P:
                    settle(pe)
                done(times(0, r_p8, of(r_y)))
                pe.wait_ge(rw_v, V + RW_V[f"y8{tt}"])
                if n < P:
                    settle(pe)
                if n == P:
                    for hd in range(NH):
                        nc.tensor.transpose(ps[:, 1, hd * P:(hd + 1) * P], r_y[:, hd], ident[:])
                    done(times(2, r_l21, of(r_y)))
                    pe.wait_ge(rw_v, V + RW_V[f"z1{tt}"])
                    pe.wait_ge(rw_s, S + RW_S[f"t16{tt}"])
                    done(times(3, r_t16, of(r_z1)))
                    pe.wait_ge(rw_v, V + RW_V[f"t32{tt}"])
                done(times(4, r_y, lambda hd: r_gin[0:n, hd, :], P))
                pe.wait_ge(rw_s, S + RW_S[f"gh{tt}"])
                if n < P:
                    settle(pe)
                for hd, (p_, hh) in enumerate(heads):
                    rows, v = slice(64 * hh, 64 * hh + 64), r_tok[0:n, p_, 3, 64 * hh:64 * hh + 64]
                    if n == P:
                        nc.tensor.matmul(ps[rows, 5, p_ * n:(p_ + 1) * n], r_gh[0:n, hd, 0:RW_N], r_mm[0:n, hd, 1, 0:n], start=True, stop=True)
                    nc.tensor.matmul(ps[rows, 6, p_ * n:(p_ + 1) * n], v, r_mm[0:n, hd, 3, 0:n], start=True, stop=False)
                    nc.tensor.matmul(ps[rows, 6, p_ * n:(p_ + 1) * n], r_gh[0:n, hd, RW_N:], r_mm[0:n, hd, 1, 0:n], start=False, stop=True)
                step = min(n, RW_CHUNK)
                for c in range(n // step):
                    for hd, (p_, hh) in enumerate(heads):
                        rows, k = slice(64 * hh, 64 * hh + 64), slice(64 * hh, 64 * hh + 64)
                        s = slice(c * step, (c + 1) * step)
                        b_end, k_end, v = r_tok[s, p_, 1, k], r_tok[s, p_, 2, k], r_tok[s, p_, 3, k]
                        if n == P:
                            nc.tensor.matmul(ps[rows, c, p_ * P:p_ * P + RW_N], r_gh[s, hd, 0:RW_N], b_end, start=True, stop=True)
                        nc.tensor.matmul(ps[rows, c, p_ * P + RW_N:(p_ + 1) * P], k_end, v, start=True, stop=False)
                        mm = nc.tensor.matmul(ps[rows, c, p_ * P + RW_N:(p_ + 1) * P], b_end, r_gh[s, hd, RW_N:], start=False, stop=True)
                done(mm)
            pe.wait_ge(rw_v, V + RW_V["fe2"])
            pe.wait_ge(rw_s, S + RW_S["add2"])
            for c in range(2, 9):
                pe.wait_ge(rw_v, V + RW_V[f"s{c - 1}"])
                for p_ in range(NP):
                    mm = nc.tensor.matmul(ps[:, c % 2, p_ * RW_N:(p_ + 1) * RW_N], r_trans[:, c - 2, p_], r_state[:, c - 2, p_], start=True, stop=True)
                done(mm)
            pe.wait_ge(rw_v, V + RW_V["s8"])
            settle(pe)
            for p_ in range(NP):
                for hh in range(2):
                    rows = slice(64 * hh, 64 * hh + 64)
                    for c in range(1, 9):
                        t0, n = CH[c]
                        mm = nc.tensor.matmul(ps[rows, 2 + 2 * p_ + hh, t0:t0 + n], r_state[rows, c - 1, p_], r_f[rows, p_, t0:t0 + n], start=True, stop=True)
            done(mm)
            pe.wait_ge(rw_v, V + RW_V["end"])

    def rw_end_vector(dve):
        y, sq = zt[:, 8:16], view(arena, 7104, CW, T)
        dve.wait_ge(rwf_t, RWF_T["sums"])
        for k in range(CW):
            mm = nc.vector.scalar_tensor_tensor(out=y[:, k], in0=ps[:, k, 0:T], scalar=-1.0 / RW_N, in1=y[:, k], op0=ALU.mult, op1=ALU.add)
        mm.then_inc(rwf_v, 1)
        dve.wait_ge(rwf_s, RWF_S["std"])
        nc.vector.reciprocal(sq, sq)
        dve.drain()
        nc.vector.tensor_tensor(y, y, sq, ALU.mult)
        dve.drain()
        for k in range(CW):
            nc.vector.tensor_scalar(y[:, k], y[:, k], col("cd_rw_ln_g", k), col("cd_rw_ln_b", k), ALU.mult, ALU.add)
        dve.drain()
        nc.vector.tensor_tensor(y, y, zt[:, 16:24], ALU.add)
        dve.drain()
        nc.vector.tensor_tensor(y, y, zt[:, 0:8], ALU.mult)

    def rw_end_scalar(act):
        y, sq = zt[:, 8:16], view(arena, 7104, CW, T)
        act.wait_ge(rwf_v, RWF_V["centred"])
        nc.scalar.activation(sq, y, ACT.Square).then_inc(rwf_s, 1)
        act.wait_ge(rwf_t, RWF_T["squares"])
        for k in range(CW):
            mm = nc.scalar.activation(sq[:, k], ps[:, k, 0:T], ACT.Sqrt, bias=eps[:, 2:3], scale=1.0 / RW_N)
        mm.then_inc(rwf_s, 1)

    def rw_end_tensor(pe):
        y, sq = zt[:, 8:16], view(arena, 7104, CW, T)
        for k in range(CW):
            mm = nc.tensor.matmul(ps[:, k, 0:T], pair_ones[:], y[:, k], start=True, stop=True)
        mm.then_inc(rwf_t, 1)
        pe.wait_ge(rwf_s, RWF_S["squared"])
        for k in range(CW):
            mm = nc.tensor.matmul(ps[:, k, 0:T], pair_ones[:], sq[:, k], start=True, stop=True)
        mm.then_inc(rwf_t, 1)

    cd_s = sem("cd_cat_scalar")
    CD_S = order("hi")

    def cd_cat_vector(dve):
        dve.wait_ge(cd_s, CD_S["hi"])
        nc.vector.tensor_tensor(x_lo[:, 0:CW], o_gla, x_hi[:, 0:CW].bitcast(F32), ALU.subtract)
        nc.vector.tensor_tensor(x_lo[:, CW:DK], zt[:, 8:16], x_hi[:, CW:DK].bitcast(F32), ALU.subtract)

    def cd_cat_scalar(act):
        nc.scalar.activation(x_hi[:, 0:CW], o_gla, ACT.Copy)
        nc.scalar.activation(x_hi[:, CW:DK], zt[:, 8:16], ACT.Copy).then_inc(cd_s, 1)

    S2 = SEQ
    TOKT = S2 // P

    def in_keep(act, name, to, c0=0):
        keep_results(act, name, lambda i, u: tile_of(to, c0 + u, i, 4)[:, -S2:])

    def causal_conv(dve, src, dst, weight, bias, tile, step, i, n):
        s, d = tile_of(src, tile, i, step), tile_of(dst, tile, i, step)
        for t in range(CONV_K):
            w = col(weight, i * step + (t * n + tile))
            if t == 0:
                nc.vector.tensor_scalar(d, s[:, 0:S2], w, col(bias, i * step + tile), ALU.mult, ALU.add)
            else:
                dve.drain()
                nc.vector.scalar_tensor_tensor(out=d, in0=s[:, t:t + S2], scalar=w, in1=d, op0=ALU.mult, op1=ALU.add)

    def log1p_vector(dve, e, s, s2, acc):
        nc.vector.tensor_scalar(s, e, 2.0, None, ALU.add)
        dve.drain()
        nc.vector.reciprocal(s, s)
        dve.drain()
        nc.vector.tensor_tensor(s, s, e, ALU.mult)
        dve.drain()
        nc.vector.tensor_tensor(s2, s, s, ALU.mult)
        nc.vector.memset(acc, 2.0 / 17)
        dve.drain()
        for n in range(15, 0, -2):
            nc.vector.tensor_tensor(acc, acc, s2, ALU.mult)
            dve.drain()
            nc.vector.tensor_scalar(acc, acc, 2.0 / n, None, ALU.add)
            dve.drain()
        nc.vector.tensor_tensor(acc, acc, s, ALU.mult)
        dve.drain()

    NH2 = CW
    hz = view(arena, 0, 32, S2)
    h_q, h_b, h_v, h_z = (hz[:, 8 * n:8 * n + 8] for n in range(4))
    h_k, h_e = view(arena, 8192, NH2, S2), view(arena, 10240, NH2, S2)
    h_qe, h_ke = view(arena, 12288, NH2, S2), view(arena, 14336, NH2, S2)
    h_a = view(arena, 16384, NH2 * TOKT, P)
    level_mask = view(side, 0, 8, P)
    HB = 4
    h_vst, h_kst = view(side, 1024, HB, S2), view(arena, 10240, HB, P)
    h_vtok, h_ktok = view(arena, 10752, HB * TOKT, P), view(arena, 11776, HB, P)
    h_state = view(arena, 12288, HB, P)
    h_o, o_a = h_ke, h_qe
    HALF = [slice(0, 4), slice(4, 8)]
    hg_v, hg_s, hg_t = trio("hg")
    _lv = ["logf", "summed", "d10", "d11"]
    _ls = ["k", "log", "q0"]
    _lt = ["x00", "x01"]
    for _l in range(1, 8):
        _lv += [f"m{_l}0", f"m{_l}1"] + ([f"d{_l + 1}0", f"d{_l + 1}1"] if _l < 7 else ["ends"])
        _ls += [f"e{_l}0", f"e{_l}1"]
        _lt += [f"x{_l}0", f"x{_l}1"]
    HG_V, HG_S, HG_T = order(*_lv, "ready"), order(*_ls[:2], *_ls[3:], "to_end", "gate"), order(*_lt)
    hgh_v, hgh_s, hgh_t = trio("hgh")
    HGH_V, HGH_S, HGH_T = order("staged", "ktok", "state"), order("vtok", "out"), order("turned", "states", "mixed")
    hge_s, hge_t = sem("hge_scalar"), sem("hge_tensor")
    HGE_S, HGE_T = order("squared", "std"), order("sums")

    def blocks(buf, half, m):
        return buf[:, HALF[half]].rearrange("p a b -> p (a b)").rearrange("p (n j) -> p n j", j=2 * m)

    def hgrn_vector(dve):
        dve.wait_ge(seg_made, 3)
        dve.wait_ge(hg_s, HG_S["log"])
        done = lambda ins: ins.then_inc(hg_v, 1)
        done(nc.vector.scalar_tensor_tensor(out=h_e, in0=h_b, scalar=0.0, in1=h_e, op0=ALU.min, op1=ALU.subtract))
        dve.drain()
        for k in range(NH2):
            mm = nc.vector.tensor_tensor_scan(h_b[:, k], seg[:, 0:S2], h_e[:, k], 0.0, ALU.mult, ALU.add)
        done(mm)
        dve.drain()

        def distance(m):
            for half in range(2):
                b, e = blocks(h_b, half, m), blocks(h_e, half, m)
                done(nc.vector.tensor_tensor(e, b, b[:, :, m - 1:m].to_broadcast(list(b.shape)), ALU.subtract))

        def keep_scores(level):
            for half in range(2):
                dve.wait_ge(hg_t, HG_T[f"x{level}{half}"])
                bank = 4 * (level % 2) + 2 * half
                nc.vector.copy_predicated(h_a[:, 8 * half:8 * half + 8], level_mask[:, level:level + 1, :].to_broadcast([P, 8, P]).bitcast(I32),
                                          ps[:, bank:bank + 2, :].rearrange("p a (b c) -> p (a b) c", c=P))
            dve.drain()
        distance(1)
        keep_scores(0)
        for level, m in enumerate(LEVELS, 1):
            for half in range(2):
                dve.wait_ge(hg_s, HG_S[f"e{level}{half}"])
                e, l, r = blocks(h_e, half, m), slice(0, m), slice(m, 2 * m)
                nc.vector.tensor_tensor(blocks(h_ke, half, m)[:, :, l], blocks(h_k, half, m)[:, :, l], e[:, :, l], ALU.mult)
                done(nc.vector.tensor_tensor(blocks(h_qe, half, m)[:, :, r], blocks(h_q, half, m)[:, :, r], e[:, :, r], ALU.mult))
            dve.drain()
            if level < 7:
                distance(2 * m)
            else:
                done(nc.vector.tensor_tensor(h_e[:, :, 0:P], h_b[:, :, P - 1:P].to_broadcast([P, NH2, P]), h_b[:, :, 0:P], ALU.subtract))
            keep_scores(level)
        dve.wait_ge(hg_s, HG_S["to_end"])
        nc.vector.tensor_tensor(h_k[:, :, 0:P], h_k[:, :, 0:P], h_e[:, :, 0:P], ALU.mult)
        done(nc.vector.tensor_tensor(h_q[:, :, P:], h_q[:, :, P:], h_e[:, :, P:], ALU.mult))
        dve.drain()
        with dve.Fori(0, NH2 // HB) as g:
            s, t = g * len(HGH_S), g * len(HGH_T)
            nc.vector.tensor_copy(h_vst, h_v[:, bass.ds(g * HB, HB)])
            nc.vector.tensor_copy(h_kst, h_k[:, bass.ds(g * HB, HB), 0:P]).then_inc(hgh_v, 1)
            dve.wait_ge(hgh_t, t + HGH_T["turned"])
            nc.vector.tensor_copy(h_ktok, ps[:, 2].rearrange("p (a b) -> p a b", b=P)).then_inc(hgh_v, 1)
            dve.wait_ge(hgh_t, t + HGH_T["states"])
            nc.vector.tensor_copy(h_state, ps[:, 3].rearrange("p (a b) -> p a b", b=P)).then_inc(hgh_v, 1)
            dve.wait_ge(hgh_t, t + HGH_T["mixed"])
        dve.wait_ge(hge_s, HGE_S["std"])
        nc.vector.reciprocal(h_k, h_k)
        dve.drain()
        nc.vector.tensor_tensor(h_o, h_o, h_k, ALU.mult)
        dve.drain()
        for k in range(NH2):
            nc.vector.scalar_tensor_tensor(out=o_a[:, k], in0=h_o[:, k], scalar=col("hgrn_norm_w_2", k), in1=h_z[:, k],
                                           op0=ALU.mult, op1=ALU.mult)

    def hgrn_scalar(act):
        done = lambda ins: ins.then_inc(hg_s, 1)
        done(nc.scalar.activation(h_k, h_b, ACT.Sigmoid, scale=-1.0))
        nc.scalar.activation(h_e, h_b, ACT.Abs)
        act.drain()
        nc.scalar.activation(h_e, h_e, ACT.Exp, scale=-1.0)
        act.drain()
        done(nc.scalar.activation(h_e, h_e, ACT.Ln, bias=eps[:, 3:4]))
        for level, m in enumerate(LEVELS, 1):
            for half in range(2):
                act.wait_ge(hg_v, HG_V[f"d{level}{half}"])
                e = blocks(h_e, half, m)
                nc.scalar.activation(e[:, :, 0:m], e[:, :, 0:m], ACT.Exp, scale=-1.0)
                done(nc.scalar.activation(e[:, :, m:], e[:, :, m:], ACT.Exp))
        act.wait_ge(hg_v, HG_V["ends"])
        nc.scalar.activation(h_e[:, :, 0:P], h_e[:, :, 0:P], ACT.Exp)
        done(nc.scalar.activation(h_e[:, :, P:], h_b[:, :, P:], ACT.Exp))
        done(nc.scalar.activation(h_z, h_z, ACT.Silu))
        with act.Fori(0, NH2 // HB) as g:
            t = g * len(HGH_T)
            act.wait_ge(hgh_t, t + HGH_T["turned"])
            nc.scalar.activation(h_vtok, ps[:, 0:2].rearrange("p a (b c) -> p (a b) c", c=P), ACT.Copy).then_inc(hgh_s, 1)
            act.wait_ge(hgh_t, t + HGH_T["mixed"])
            nc.scalar.activation(h_o[:, bass.ds(g * HB, HB)], ps[:, 4:6].rearrange("p a (b c) -> p (a b) c", c=S2),
                                 ACT.Copy).then_inc(hgh_s, 1)
        act.drain()
        nc.scalar.activation(h_e, h_o, ACT.Square).then_inc(hge_s, 1)
        act.wait_ge(hge_t, HGE_T["sums"])
        nc.scalar.activation(h_k, ps[:, 0:4].rearrange("p a (b c) -> p (a b) c", c=S2), ACT.Sqrt, bias=eps[:, 0:1],
                             scale=1.0 / P).then_inc(hge_s, 1)

    def hgrn_tensor(pe):
        for level in range(8):
            for half in range(2):
                if level == 0:
                    pe.wait_ge(hg_s, HG_S["k"])
                else:
                    pe.wait_ge(hg_v, HG_V[f"m{level}{half}"])
                left, right = (h_k, h_q) if level == 0 else (h_ke, h_qe)
                for n in range(8):
                    k, c = 4 * half + n // 2, slice(P * (n % 2), P * (n % 2) + P)
                    mm = nc.tensor.matmul(ps[:, 4 * (level % 2) + 2 * half + n // 4, (n % 4) * P:(n % 4 + 1) * P], left[:, k, c],
                                          right[:, k, c], start=True, stop=True)
                mm.then_inc(hg_t, 1)
        pe.wait_ge(hg_v, HG_V["ready"])
        with pe.Fori(0, NH2 // HB) as g:
            v, s = g * len(HGH_V), g * len(HGH_S)
            pe.wait_ge(hgh_v, v + HGH_V["staged"])
            for k in range(HB):
                for j in range(TOKT):
                    nc.tensor.transpose(ps[:, k // 2, ((k % 2) * 2 + j) * P:((k % 2) * 2 + j + 1) * P], h_vst[:, k, j * P:(j + 1) * P], ident[:])
                mm = nc.tensor.transpose(ps[:, 2, k * P:(k + 1) * P], h_kst[:, k], ident[:])
            mm.then_inc(hgh_t, 1)
            pe.wait_ge(hgh_s, s + HGH_S["vtok"])
            pe.wait_ge(hgh_v, v + HGH_V["ktok"])
            for k in range(HB):
                mm = nc.tensor.matmul(ps[:, 3, k * P:(k + 1) * P], h_ktok[:, k], h_vtok[:, 2 * k], start=True, stop=True)
            mm.then_inc(hgh_t, 1)
            pe.wait_ge(hgh_v, v + HGH_V["state"])
            for k in range(HB):
                for j in range(TOKT):
                    acc = ps[:, 4 + k // 2, (k % 2) * S2 + j * P:(k % 2) * S2 + (j + 1) * P]
                    mm = nc.tensor.matmul(acc, h_vtok[:, 2 * k + j], tile_of(h_a, 2 * k + j, g, 2 * HB), start=True, stop=(j == 0))
                    if j:
                        mm = nc.tensor.matmul(acc, h_state[:, k], tile_of(h_q, k, g, HB)[:, P:], start=False, stop=True)
            mm.then_inc(hgh_t, 1)
            pe.wait_ge(hgh_s, s + HGH_S["out"])
        pe.wait_ge(hge_s, HGE_S["squared"])
        for k in range(NH2):
            mm = nc.tensor.matmul(ps[:, k // 2, (k % 2) * S2:(k % 2 + 1) * S2], ones[:], h_e[:, k], start=True, stop=True)
        mm.then_inc(hge_t, 1)

    XW = S2 + CONV_K - 1
    lz = view(arena, 0, 16, XW)
    l_x, l_z = lz[:, 0:8], lz[:, 8:16, XW - S2:]
    l_xc, l_r, l_i = view(arena, 4160, CW, S2), view(arena, 6208, CW, S2), view(arena, 8256, CW, S2)
    l_lam = view(arena, 10304, 5, CW)
    l_t, l_a = view(arena, 14336, CW, S2), view(arena, 16384, CW, S2)
    o_b = l_t
    wa, wx = view(side, 0, CW, P), view(side, 1024, CW, P)
    lru_v, lru_s, lru_t = trio("lru")
    LRU_V = order("log_a", "ratio", "scanned")
    LRU_S = order("lambda", "gates", "a", "root", "silu")
    LRU_T = order("gates")

    def lru_in_vector(dve):
        run_phase(dve, ph["in_bx"], None, split_job)
        dve.wait_ge(padded, 1)
        phases_out(dve, "in_bz")
        run_phase(dve, ph["in_bz"], lambda i, u: causal_conv(dve, l_x, l_xc, "rglru_conv_w_2", "rglru_conv_b_2", u, 4, i, CW), split_job)

    def lru_vector(dve):
        dve.wait_ge(lru_s, LRU_S["lambda"])
        log1p_vector(dve, l_lam[:, 0], l_lam[:, 1], l_lam[:, 2], l_lam[:, 3])
        nc.vector.tensor_scalar(l_lam[:, 4], cols("rglru_lambda_2", CW), -1.0, 0.0, ALU.mult, ALU.max)
        dve.drain()
        nc.vector.tensor_tensor(l_lam[:, 3], l_lam[:, 3], l_lam[:, 4], ALU.add)
        dve.drain()
        nc.vector.tensor_scalar(l_lam[:, 3], l_lam[:, 3], -8.0, None, ALU.mult)
        dve.drain()
        dve.wait_ge(lru_s, LRU_S["gates"])
        nc.vector.tensor_tensor(l_r, l_r, l_lam[:, 3].unsqueeze(2).to_broadcast([P, CW, S2]), ALU.mult).then_inc(lru_v, 1)
        nc.vector.tensor_tensor(l_xc, l_xc, l_i, ALU.mult)
        dve.drain()
        dve.wait_ge(lru_s, LRU_S["a"])
        nc.vector.tensor_scalar(l_i, l_t, -1.0, 1.0, ALU.mult, ALU.add)
        dve.drain()
        nc.vector.reciprocal(l_i, l_i)
        dve.drain()
        nc.vector.tensor_tensor(l_t, l_t, l_i, ALU.mult).then_inc(lru_v, 1)
        dve.wait_ge(lru_s, LRU_S["root"])
        nc.vector.tensor_tensor(l_xc, l_xc, l_t, ALU.mult)
        dve.drain()
        for k in range(CW):
            mm = nc.vector.tensor_tensor_scan(l_r[:, k], l_a[:, k], l_xc[:, k], 0.0, ALU.mult, ALU.add)
        dve.drain()
        dve.wait_ge(lru_s, LRU_S["silu"])
        nc.vector.tensor_tensor(o_b, l_r, l_z, ALU.mult).then_inc(lru_v, 1)

    def lru_scalar(act):
        lam = l_lam[:, 0]
        nc.scalar.activation(lam, cols("rglru_lambda_2", CW), ACT.Abs)
        act.drain()
        nc.scalar.activation(lam, lam, ACT.Exp, scale=-1.0).then_inc(lru_s, 1)
        act.wait_ge(lru_t, LRU_T["gates"])
        for first, dst, bias in ((0, l_r, "rglru_ba_2"), (4, l_i, "rglru_bx_2")):
            for k in range(CW):
                mm = nc.scalar.activation(dst[:, k], ps[:, first + k // 2, (k % 2) * S2:(k % 2 + 1) * S2], ACT.Sigmoid, bias=col(bias, k))
        mm.then_inc(lru_s, 1)
        act.wait_ge(lru_v, LRU_V["log_a"])
        nc.scalar.activation(l_t, l_r, ACT.Tanh)
        nc.scalar.activation(l_a, l_r, ACT.Exp).then_inc(lru_s, 1)
        act.wait_ge(lru_v, LRU_V["ratio"])
        nc.scalar.activation(l_t, l_t, ACT.Sqrt, scale=-2.0).then_inc(lru_s, 1)
        nc.scalar.activation(l_z, l_z, ACT.Silu).then_inc(lru_s, 1)

    def lru_tensor(pe):
        pe.wait_ge(side_in, 96)
        for first, w in ((0, wa), (4, wx)):
            for k in range(CW):
                mm = nc.tensor.matmul(ps[:, first + k // 2, (k % 2) * S2:(k % 2 + 1) * S2], w[:, k], l_xc[:, k], start=True, stop=True)
        mm.then_inc(lru_t, 1)

    NX, GROUPS, SH = 12, 2, 16
    PAIRS = CW // GROUPS
    c_pad, c_z = view(arena, 0, NX, XW), view(arena, 3136, CW, S2)
    c_dt, c_e = arena[0:SH, 5184:5440], arena[0:SH, 10560:10816]
    c_x = view(arena, 5440, NX, S2)
    c_y = view(arena, 8512, CW, S2)
    c_s, c_s2, c_log = (arena[0:SH, 10816 + 256 * n:11072 + 256 * n] for n in range(3))
    c_cum, c_dec = arena[0:SH, 11584:11840], arena[0:SH, 11840:12096]
    c_tok = view(arena, 12096, 3, TOKT, SH)
    c_btok, c_cb = view(arena, 16384, TOKT, P), view(arena, 16640, TOKT, P)
    c_bst, c_xst = arena[:, 16896:17152], arena[:, 17152:17408]
    c_xtok, c_xend = view(arena, 17408, TOKT, P), arena[:, 17664:17792]
    c_state, c_cq = arena[:, 17792:17920], view(arena, 17920, 2, P)
    c_sel = side[0:SH, 0:2 * P].rearrange("p (a b) -> p a b", b=P)
    c_l = view(side, 256, 2, TOKT, P)
    c_grow = view(side, 768, 2, P)
    c_sq = view(arena, 0, CW, S2)
    c_std = view(arena, 10560, GROUPS, S2)
    o_c = view(arena, 16384, CW, S2)
    ssd_v, ssd_s, ssd_t = trio("ssd")
    SSD_V = order("biased", "summed", "tok", "gated")
    SSD_S = order("dt_e", "to_end", "gate", "squared", "std")
    SSD_T = order("turned", "sums")
    sg_v, sg_t = sem("sg_vector"), sem("sg_tensor")
    SG_V, SG_T = order("staged", "out"), order("scores")
    sp_v, sp_s, sp_t = trio("sp")
    SP_V = order("staged", "shifted", "scores", "out")
    SP_S = order("decays", "state")
    SP_T = order("turned", "state", "mixed")

    def ssd_in_vector(dve):
        run_phase(dve, ph["in_xbc"], None, split_job)
        dve.wait_ge(padded, 2)
        phases_out(dve, "in_cz")

        def conv(i, u):
            for tile in ((0, 1), (2,), (3, 4), (5,))[u]:
                causal_conv(dve, c_pad, c_x, "ssd_conv_w_2", "ssd_conv_b_2", tile, NX // 2, i, NX)
        run_phase(dve, ph["in_cz"], conv, split_job)
        run_phase(dve, ph["dt"], None, split_job)

    def ssd_vector(dve):
        done = lambda ins: ins.then_inc(ssd_v, 1)
        done(nc.vector.tensor_scalar(c_dt, c_dt, small[:, 0:1], None, ALU.add))
        dve.drain()
        dve.wait_ge(ssd_s, SSD_S["dt_e"])
        log1p_vector(dve, c_e, c_s, c_s2, c_log)
        nc.vector.tensor_scalar(c_dt, c_dt, 0.0, None, ALU.max)
        dve.drain()
        nc.vector.tensor_tensor(c_dt, c_dt, c_log, ALU.add)
        dve.drain()
        nc.vector.tensor_scalar(c_s, c_dt, small[:, 2:3], None, ALU.mult)
        dve.drain()
        nc.vector.tensor_tensor_scan(c_cum, seg[0:SH, 0:S2], c_s, 0.0, ALU.mult, ALU.add)
        dve.drain()
        cum = c_cum.rearrange("p (a b) -> p a b", b=P)
        done(nc.vector.tensor_tensor(c_dec.rearrange("p (a b) -> p a b", b=P), cum[:, :, P - 1:].to_broadcast([SH, TOKT, P]), cum, ALU.subtract))
        dve.wait_ge(ssd_t, SSD_T["turned"])
        done(nc.vector.tensor_copy(c_tok, ps[:, 7, 0:3 * TOKT * SH].rearrange("p (a b c) -> p a b c", a=3, b=TOKT)))
        dve.wait_ge(ssd_s, SSD_S["gate"])
        dve.drain()
        with dve.Fori(0, GROUPS) as g:
            nc.vector.tensor_copy(c_bst, tile_of(c_x, 8, g, 1)).then_inc(sg_v, 1)
            dve.wait_ge(sg_t, g + SG_T["scores"])
            nc.vector.tensor_copy(c_btok, ps[:, 6, 0:S2].rearrange("p (a b) -> p a b", b=P))
            nc.vector.tensor_tensor(c_cb, ps[:, 7, 0:S2].rearrange("p (a b) -> p a b", b=P),
                                    le[:].unsqueeze(1).to_broadcast([P, TOKT, P]), ALU.mult).then_inc(sg_v, 1)
            dve.drain()
            with dve.Fori(0, PAIRS) as r:
                tile = g * PAIRS + r
                s, t = tile * len(SP_S), tile * len(SP_T)
                nc.vector.tensor_copy(c_sel, ident[0:SH, bass.ds(tile * 2, 2)].unsqueeze(2).to_broadcast([SH, 2, P]))
                nc.vector.tensor_copy(c_xst, tile_of(c_x, 0, tile, 1)).then_inc(sp_v, 1)
                dve.wait_ge(sp_t, t + SP_T["turned"])
                for hh in range(2):
                    for j in range(TOKT):
                        mm = nc.vector.tensor_scalar(c_l[:, hh, j], ps[:, hh, j * P:(j + 1) * P], c_tok[:, 0, j, bass.ds(tile * 2 + hh, 1)],
                                                     0.0, ALU.subtract, ALU.min)
                mm.then_inc(sp_v, 1)
                for j in range(TOKT):
                    for hh in range(2):
                        nc.vector.tensor_scalar(c_xtok[:, j, 64 * hh:64 * hh + 64], ps[:, 2, j * P + 64 * hh:j * P + 64 * hh + 64],
                                                c_tok[:, 1, j, bass.ds(tile * 2 + hh, 1)], None, ALU.mult)
                dve.drain()
                for hh in range(2):
                    nc.vector.tensor_scalar(c_xend[:, 64 * hh:64 * hh + 64], c_xtok[:, 0, 64 * hh:64 * hh + 64],
                                            c_tok[:, 2, 0, bass.ds(tile * 2 + hh, 1)], None, ALU.mult)
                dve.wait_ge(sp_s, s + SP_S["decays"])
                for hh in range(2):
                    nc.vector.tensor_tensor(c_l[:, hh], c_l[:, hh], c_cb, ALU.mult)
                    mm = nc.vector.tensor_tensor(c_cq[:, hh], c_grow[:, hh], tile_of(c_x, 10, g, 1)[:, P:], ALU.mult)
                mm.then_inc(sp_v, 1)
                dve.wait_ge(sp_t, t + SP_T["mixed"])
                nc.vector.scalar_tensor_tensor(out=tile_of(c_y, 0, tile, 1), in0=c_xst, scalar=dskip[:, bass.ds(tile, 1)],
                                               in1=ps[:, 4, 0:S2], op0=ALU.mult, op1=ALU.add).then_inc(sp_v, 1)
                dve.drain()
        done(nc.vector.tensor_tensor(c_y, c_y, c_z, ALU.mult))
        dve.wait_ge(ssd_s, SSD_S["std"])
        nc.vector.reciprocal(c_std, c_std)
        dve.drain()
        for k in range(CW):
            nc.vector.scalar_tensor_tensor(out=o_c[:, k], in0=c_y[:, k], scalar=col("ssd_norm_w_2", k), in1=c_std[:, k // PAIRS],
                                           op0=ALU.mult, op1=ALU.mult)

    def ssd_scalar(act):
        done = lambda ins: ins.then_inc(ssd_s, 1)
        act.wait_ge(ssd_v, SSD_V["biased"])
        nc.scalar.activation(c_e, c_dt, ACT.Abs)
        act.drain()
        done(nc.scalar.activation(c_e, c_e, ACT.Exp, scale=-1.0))
        act.wait_ge(ssd_v, SSD_V["summed"])
        done(nc.scalar.activation(c_dec, c_dec, ACT.Exp))
        nc.scalar.activation(c_x, c_x, ACT.Silu)
        done(nc.scalar.activation(c_z, c_z, ACT.Silu))
        with act.Fori(0, GROUPS) as g:
            with act.Fori(0, PAIRS) as r:
                tile = g * PAIRS + r
                v, t = tile * len(SP_V), tile * len(SP_T)
                act.wait_ge(sp_v, v + SP_V["shifted"])
                nc.scalar.activation(c_grow, ps[:, 0:2, P:2 * P], ACT.Exp)
                nc.scalar.activation(c_l, c_l, ACT.Exp).then_inc(sp_s, 1)
                act.wait_ge(sp_t, t + SP_T["state"])
                nc.scalar.activation(c_state, ps[:, 3, 0:P], ACT.Copy).then_inc(sp_s, 1)
        act.wait_ge(ssd_v, SSD_V["gated"])
        done(nc.scalar.activation(c_sq, c_y, ACT.Square))
        act.wait_ge(ssd_t, SSD_T["sums"])
        done(nc.scalar.activation(c_std, ps[:, 0:GROUPS, 0:S2], ACT.Sqrt, bias=eps[:, 0:1], scale=1.0 / 512))

    def ssd_tensor(pe):
        pe.wait_ge(ssd_s, SSD_S["to_end"])
        for n, src in enumerate((c_cum, c_dt, c_dec)):
            for j in range(TOKT):
                first = (n * TOKT + j) * SH
                mm = nc.tensor.transpose(ps[:, 7, first:first + SH], src[:, j * P:(j + 1) * P], ident[0:SH, 0:SH])
        mm.then_inc(ssd_t, 1)
        pe.wait_ge(ssd_v, SSD_V["tok"])
        with pe.Fori(0, GROUPS) as g:
            pe.wait_ge(sg_v, g * len(SG_V) + SG_V["staged"])
            for j in range(TOKT):
                cols_ = slice(j * P, (j + 1) * P)
                nc.tensor.transpose(ps[:, 6, cols_], c_bst[:, cols_], ident[:])
                mm = nc.tensor.matmul(ps[:, 7, cols_], c_bst[:, cols_], tile_of(c_x, 10, g, 1)[:, cols_], start=True, stop=True)
            mm.then_inc(sg_t, 1)
            with pe.Fori(0, PAIRS) as r:
                tile = g * PAIRS + r
                v, s = tile * len(SP_V), tile * len(SP_S)
                pe.wait_ge(sp_v, v + SP_V["staged"])
                for hh in range(2):
                    nc.tensor.matmul(ps[:, hh, 0:S2], c_sel[:, hh], c_cum, start=True, stop=True)
                for j in range(TOKT):
                    mm = nc.tensor.transpose(ps[:, 2, j * P:(j + 1) * P], c_xst[:, j * P:(j + 1) * P], ident[:])
                mm.then_inc(sp_t, 1)
                pe.wait_ge(sp_v, v + SP_V["scores"])
                nc.tensor.matmul(ps[:, 3, 0:P], c_btok[:, 0], c_xend, start=True, stop=True).then_inc(sp_t, 1)
                pe.wait_ge(sp_s, s + SP_S["state"])
                for hh in range(2):
                    rows = slice(64 * hh, 64 * hh + 64)
                    for j in range(TOKT):
                        acc = ps[rows, 4, j * P:(j + 1) * P]
                        mm = nc.tensor.matmul(acc, c_xtok[:, j, rows], c_l[:, hh, j], start=True, stop=(j == 0))
                        if j:
                            mm = nc.tensor.matmul(acc, c_state[:, rows], c_cq[:, hh], start=False, stop=True)
                mm.then_inc(sp_t, 1)
        pe.wait_ge(ssd_s, SSD_S["squared"])
        for k in range(CW):
            mm = nc.tensor.matmul(ps[:, k // PAIRS, 0:S2], ones[:], c_sq[:, k], start=(k % PAIRS == 0), stop=(k % PAIRS == PAIRS - 1))
        mm.then_inc(ssd_t, 1)

    branches = view(arena, 12288, 24, S2)
    cat_hi = act_hi[:].rearrange("p (k t) -> p k t", t=S2)
    cat_lo = act_lo[:].rearrange("p (k t) -> p k t", t=S2)
    gate, prod = view(arena, 12288, 2, 3, S2), view(arena, 12288 + 6 * S2, 2, 3, S2)
    cat_hi_made = sem("cat_hi_made")

    def cat_scalar(act):
        for n in range(3):
            nc.scalar.activation(cat_hi[:, 8 * n:8 * n + 8], branches[:, 8 * n:8 * n + 8], ACT.Copy).then_inc(cat_hi_made, 1)

    def cat_vector(dve):
        for n in range(3):
            dve.wait_ge(cat_hi_made, n + 1)
            t = slice(8 * n, 8 * n + 8)
            nc.vector.tensor_tensor(cat_lo[:, t], branches[:, t], cat_hi[:, t].bitcast(F32), ALU.subtract)

    def out_scalar(act):
        p = ph["out"]

        def work(i, q):
            u, n, is_branch = q // 6, (q % 6) // 2, q % 2
            if not is_branch:
                result_ready(act, p, i, q)
                act.wait_ge(tile_summed[u], i + 1)
                nc.scalar.activation(gate[:, u, n], ps[:, q % 6, 0:S2], ACT.Sigmoid).then_inc(gates_made, 1)
        run_phase(act, p, work, round_job, last=True)

    def out_vector(dve):
        p = ph["out"]

        def work(i, q):
            u, n, is_branch = q // 6, (q % 6) // 2, q % 2
            if is_branch:
                result_ready(dve, p, i, q)
                dve.wait_ge(gates_made, i * 6 + (3 * u + n + 4))
                nc.vector.tensor_tensor(prod[:, u, n], ps[:, q % 6, 0:S2], gate[:, u, n], ALU.mult).then_inc(products_made, 1)
                dve.drain()
                if n == 2:
                    dve.sem_inc(tile_summed[u], 1)
                x = tile_of(h, u, i, 2)[:, META:]
                nc.vector.tensor_tensor(x, x, prod[:, u, n], ALU.add)
        run_phase(dve, p, work, split_job, last=True)

    def out_tensor(pe):
        p = ph["out"]
        with pe.Fori(0, p.n) as i:
            for q, (kt, w, _) in enumerate(p.jobs):
                u, n, is_branch = q // 6, (q % 6) // 2, q % 2
                pe.wait_ge(products_made if is_branch else gates_made, i * 6 + (3 * u + n + 1))
                operand = (cat_hi, cat_lo, 8 * n) if is_branch else (x_hi, x_lo, 0)
                multiply_job(pe, p, i, q, ps[:, q % 6, 0:S2],
                             lambda k: (operand[0][:, operand[2] + k, 0:S2], operand[1][:, operand[2] + k, 0:S2]), kt, w, True, True)

    x_in, meta_in = view(arena, 0, TOKT, D), arena[0:META, 4096:4096 + D]
    rows_in = view(arena, 6144, ROW_GROUPS, P)
    d_row = arena[0:1, 8000:8016]
    stage_out = view(arena, 6144, TOKT, D)
    d_turned, start_v, a_exp = sem("d_turned"), sem("start_vector"), sem("a_exp")
    PARAM_DMAS = 5 + sum((VOFF[name] + n - 1) // P - VOFF[name] // P + 1 for name, n in VECTORS)

    def flat_rows(ap):
        names = "abcd"[:len(ap.shape)]
        flat = ap.rearrange(f"{' '.join(names)} -> ({' '.join(names)})") if len(ap.shape) > 1 else ap
        return flat.rearrange("(k p) -> k p", p=P)

    def start_loads(act):
        def load(dst, src):
            act.dma_start(dst, src).then_inc(params_in, 16)
        for name, n in VECTORS:
            src, first, r = flat_rows(a[name]), VOFF[name], 0
            while r < n:
                g, p0 = (first + r) // P, (first + r) % P
                m = min(n - r, P - p0)
                load(rows_in[p0:p0 + m, g], src[r:r + m])
                r += m
        load(x_in, a["x"][0].rearrange("(j p) d -> p j d", p=P))
        load(meta_in, a["meta"])
        load(small[:, 0:1], a["ssd_dt_bias_2"].rearrange("a n -> n a"))
        load(small[:, 1:2], a["ssd_a_log_2"].rearrange("a n -> n a"))
        load(d_row, a["ssd_d_2"])

    def start_tensor(pe):
        pe.wait_ge(masks_made, 1)
        pe.wait_ge(params_in, 16 * PARAM_DMAS)
        for g in range(ROW_GROUPS):
            n = min(P, NROWS - g * P)
            mm = nc.tensor.transpose(ps[:, g // 4, (g % 4) * P:(g % 4) * P + n], rows_in[0:n, g], ident[0:n, 0:n])
        mm.then_inc(rows_turned, 1)
        nc.tensor.matmul(ps[:, 3, 0:16], ones[0:1, :], d_row, start=True, stop=True).then_inc(d_turned, 1)
        pe.wait_ge(rows_kept, 1)
        for k in range(DK):
            if k >= 8:
                pe.wait_ge(x_kept[k % 2], (k - 8) // 2 + 1)
            c = slice(k * P, (k + 1) * P)
            nc.tensor.transpose(ps[:, k % 8, 0:META], meta_in[:, c], ident[0:META, 0:META])
            for j in range(TOKT):
                mm = nc.tensor.transpose(ps[:, k % 8, META + j * P:META + (j + 1) * P], x_in[:, j, c], ident[:])
            mm.then_inc(x_turned, 1)

    def start_vector(dve):
        dve.wait_ge(rows_turned, 1)
        for b in range((ROW_GROUPS + 3) // 4):
            n = min(512, NROWS - b * 512)
            nc.vector.tensor_copy(vec[:, b * 512:b * 512 + n], ps[:, b, 0:n])
        dve.drain()
        dve.wait_ge(d_turned, 1)
        for hh in range(2):
            rows = slice(64 * hh, 64 * hh + 64)
            mm = nc.vector.tensor_copy(dskip[rows, :], ps[rows, 3, hh:16:2])
        mm.then_inc(rows_kept, 1)
        nc.vector.tensor_scalar(omka[:], cols("cd_rw_ka", CW), -1.0, 1.0, ALU.mult, ALU.add)
        for k in range(0, DK, 2):
            dve.wait_ge(x_turned, k + 1)
            nc.vector.tensor_copy(h[:, k], ps[:, k % 8, 0:T]).then_inc(x_kept[0], 1)
        dve.wait_ge(a_exp, 1)
        nc.vector.tensor_scalar(small[:, 2:3], small[:, 3:4], -1.0, None, ALU.mult)
        split_job(dve, ph["ab_gate"], 0, 0, DK)

    def start_scalar(act):
        act.wait_ge(params_in, 16 * PARAM_DMAS)
        nc.scalar.activation(small[:, 3:4], small[:, 1:2], ACT.Exp).then_inc(a_exp, 1)
        for k in range(1, DK, 2):
            act.wait_ge(x_turned, k + 1)
            nc.scalar.activation(h[:, k], ps[:, k % 8, 0:T], ACT.Copy).then_inc(x_kept[1], 1)
        round_job(act, ph["ab_gate"], 0, 0, DK)

    def end_tensor(pe):
        for b in range(8):
            j, k0 = b // 4, 4 * (b % 4)
            for k in range(4):
                mm = nc.tensor.transpose(ps[:, b, k * P:(k + 1) * P], xn[:, k0 + k, j * P:(j + 1) * P], ident[:])
            mm.then_inc(out_turned, 1)

    def end_keep(eng, parity):
        for b in range(parity, 8, 2):
            eng.wait_ge(out_turned, b + 1)
            dst = stage_out[:, b // 4, (b % 4) * 512:(b % 4 + 1) * 512]
            if parity:
                nc.scalar.activation(dst, ps[:, b, :], ACT.Copy).then_inc(out_kept[1], 1)
            else:
                nc.vector.tensor_copy(dst, ps[:, b, :]).then_inc(out_kept[0], 1)

    def end_store(sp):
        for b in range(8):
            sp.wait_ge(out_kept[b % 2], b // 2 + 1)
            j, c = b // 4, slice((b % 4) * 512, (b % 4 + 1) * 512)
            sp.dma_start(out[0, j * P:(j + 1) * P, c], stage_out[:, j, c]).then_inc(out_stored, 16)
        sp.wait_ge(out_stored, 16 * 8)

    def triangle(pool, buf, block, sign, strict):
        n = P // block
        v = buf.rearrange("p (a b) -> p a b", b=block)

        def keep(pattern, base, mult):
            pool.drain()
            nc.gpsimd.affine_select(out=v, in_=v, pattern=pattern, compare_op=ALU.is_ge, fill=0.0, base=base, channel_multiplier=mult)
        if n > 1:
            keep([[-block, n], [0, block]], 0, 1)
            keep([[block, n], [0, block]], block - 1, -1)
        if sign:
            keep([[sign * block, n], [sign, block]], -strict, -sign)

    def scan_starts(pool, count, starts):
        nc.gpsimd.memset(seg[:], 1.0)
        pool.drain()
        for t0, step, n in starts:
            nc.gpsimd.memset(seg[:, t0:t0 + (n - 1) * step + 1:step], 0.0)
        pool.drain().then_inc(seg_made, 1)

    def start_pool(pool):
        pool.sem_inc(split, RING)
        pool.sem_inc(multiplied, 2)
        for b in range(2):
            pool.sem_inc(drained[b], 1)
            pool.sem_inc(tile_summed[b], 1)
        pool.sem_inc(gates_made, 3)
        pool.sem_inc(products_made, 3)
        nc.gpsimd.memset(ident[:], 1.0)
        nc.gpsimd.memset(ones[:], 1.0)
        for n, e in enumerate((EPS, LN_EPS, GN_EPS, 1.0)):
            nc.gpsimd.memset(eps[:, n:n + 1], e)
        triangle(pool, ident[:], P, 1, 0)
        triangle(pool, ident[:], P, -1, 0)
        pool.drain().then_inc(masks_made, 1)
        for buf in (pair_ones, le, le64):
            nc.gpsimd.memset(buf[:], 1.0)
        nc.gpsimd.memset(rw_mask[:], 1.0)
        nc.gpsimd.memset(up16[:], -1.0)
        nc.gpsimd.memset(low16[:], -1.0)
        nc.gpsimd.memset(low21[:], 1.0)
        triangle(pool, pair_ones[:], 64, 0, 0)
        triangle(pool, le[:], P, 1, 0)
        triangle(pool, le64[:], 64, 1, 0)
        for n in range(4):
            triangle(pool, rw_mask[:, n], RW_CHUNK, 1, 1 - n % 2)
        triangle(pool, up16[:], 16, 1, 1)
        triangle(pool, low16[:], 16, -1, 1)
        triangle(pool, low21[:], 32, 0, 0)
        v = low21[:].rearrange("p (a b) -> p a b", b=32)
        pool.drain()
        nc.gpsimd.affine_select(out=v, in_=v, pattern=[[-32, 4], [0, 32]], compare_op=ALU.is_ge, fill=0.0, base=-16, channel_multiplier=1)
        pool.drain()
        nc.gpsimd.memset(v[:, :, 16:], 0.0)
        for hh in range(2):
            rows = slice(64 * hh, 64 * hh + 64)
            pool.drain()
            nc.gpsimd.tensor_copy(eye2[rows, :], ident[rows, rows])
        pool.drain()
        nc.gpsimd.memset(ab_a[:, :, 0:CONF_K - 1], 0.0)
        nc.gpsimd.memset(ab_s[:, :, 0:SC_K - 1], 0.0)
        scan_starts(pool, 1, [(0, 1, 1), (META, GLA_CHUNK, 4)])

    def gla_pool(pool):
        pool.dma_start(g_w2, a["cd_gla_w2"][0]).then_inc(side_in, 16)
        pool.wait_ge(side_in, 16)
        pool.dma_start(side[0:64, 0:1024], a["cd_rw_w2"][0]).then_inc(side_in, 16)
        pool.dma_start(side[64:128, 0:1024], a["cd_rw_a2"][0]).then_inc(side_in, 16)
        pool.dma_start(side[:, 1024:2048], a["cd_rw_g2"][0]).then_inc(side_in, 16)

    def rw_pool(pool):
        scan_starts(pool, 2, [(0, 1, 1), (META, RW_CHUNK, SEQ // RW_CHUNK)])
        nc.gpsimd.memset(zr[:, :, 0:1], 0.0)

    def level_pool(pool):
        scan_starts(pool, 3, [(0, P, TOKT)])
        nc.gpsimd.memset(level_mask, 1.0)
        triangle(pool, level_mask[:, 0], P, 1, 0)
        triangle(pool, level_mask[:, 0], P, -1, 0)
        for level, m in enumerate(LEVELS, 1):
            triangle(pool, level_mask[:, level], 2 * m, 0, 0)
            v = level_mask[:, level].rearrange("p (a b) -> p a b", b=2 * m)
            pool.drain()
            nc.gpsimd.affine_select(out=v, in_=v, pattern=[[2 * m, P // (2 * m)], [0, 2 * m]], compare_op=ALU.is_ge, fill=0.0,
                                    base=m - 1, channel_multiplier=-1)
            pool.drain()
            nc.gpsimd.memset(v[:, :, 0:m], 0.0)

    def hgrn_pool(pool):
        nc.gpsimd.memset(arena[:, 12288:18432], 0.0)

    def lru_pool(pool):
        for n, name in enumerate(("rglru_wa_2", "rglru_wx_2")):
            pool.dma_start(view(side, 1024 * n, CW, P), a[name][0].rearrange("h i j -> i h j")).then_inc(side_in, 16)
        nc.gpsimd.memset(l_x[:, :, 0:CONV_K - 1], 0.0).then_inc(padded, 1)

    def ssd_pool(pool):
        nc.gpsimd.memset(c_pad[:, :, 0:CONV_K - 1], 0.0).then_inc(padded, 1)

    block = nc.Block()
    with block:
        @block.sync
        def _(sp):
            for p in ph.values():
                load_phase(sp, p)
            end_store(sp)

        @block.scalar
        def _(act):
            start_loads(act)
            start_scalar(act)
            meet(act, "setup")
            norm_scalar(act, 0, 0, True)
            meet(act, "n0")
            ab_in_scalar(act)
            meet(act, "ab_in")
            ab_scalar(act)
            meet(act, "ab")
            run_phase(act, ph["ab_out"], None, round_job)
            meet(act, "ab_out")
            norm_scalar(act, 1, 0, True)
            meet(act, "n1")
            for f in range(2):
                ffn_scalar(act, 0, f)
            meet(act, "ffn0")
            norm_scalar(act, 2, 0, True)
            meet(act, "n2")
            keep_results(act, "gla", lambda i, u: tile_of(zg, u, i, 4))
            keep_results(act, "glr", lambda i, u: g_low)
            meet(act, "gla_in")
            gla_prepare_scalar(act)
            gla_heads_scalar(act)
            gla_end_scalar(act)
            meet(act, "gla")
            keep_results(act, "rw", lambda i, u: tile_of(zt, u, i, 4))
            keep_results(act, "rw_low", lambda i, u: tile_of(zt, 24 + u, i, 4))
            meet(act, "rw_in")
            rw_mix_scalar(act)
            rw_scalar(act)
            rw_end_scalar(act)
            meet(act, "rw")
            cd_cat_scalar(act)
            meet(act, "cd_cat")
            run_phase(act, ph["cd_out"], None, round_job)
            meet(act, "cd_out")
            norm_scalar(act, 3, 0, True)
            meet(act, "n3")
            for f in range(2):
                ffn_scalar(act, 1, f)
            meet(act, "ffn1")
            norm_scalar(act, 4, META, False)
            meet(act, "n4")
            norm_scalar(act, 5, META, True)
            meet(act, "n5")
            in_keep(act, "in_a", hz)
            meet(act, "in_a")
            hgrn_scalar(act)
            meet(act, "hgrn")
            in_keep(act, "in_bx", lz)
            in_keep(act, "in_bz", lz, 8)
            meet(act, "in_b")
            lru_scalar(act)
            meet(act, "rglru")
            in_keep(act, "in_xbc", c_pad)
            in_keep(act, "in_cz", c_z)
            keep_results(act, "dt", lambda i, u: c_dt)
            meet(act, "in_c")
            ssd_scalar(act)
            meet(act, "ssd")
            cat_scalar(act)
            meet(act, "cat")
            out_scalar(act)
            meet(act, "out")
            norm_scalar(act, 6, META, False)
            meet(act, "n6")
            end_keep(act, 1)

        @block.vector
        def _(dve):
            start_vector(dve)
            meet(dve, "setup")
            norm_vector(dve, 0, 0, lambda k: col("norm_mix", k))
            meet(dve, "n0")
            ab_in_vector(dve)
            meet(dve, "ab_in")
            ab_vector(dve)
            meet(dve, "ab")
            add_residual(dve, "ab_out")
            meet(dve, "ab_out")
            norm_vector(dve, 1, 0, lambda k: col("norm_ffn", k))
            meet(dve, "n1")
            for f in range(2):
                ffn_vector(dve, 0, f)
            meet(dve, "ffn0")
            norm_vector(dve, 2, 0, lambda k: col("norm_mix", DK + k))
            meet(dve, "n2")
            for name in ("gla", "glr"):
                run_phase(dve, ph[name], None, split_job)
            meet(dve, "gla_in")
            gla_prepare_vector(dve)
            gla_heads_vector(dve)
            gla_end_vector(dve)
            meet(dve, "gla")
            for name in ("rw", "rw_low"):
                run_phase(dve, ph[name], None, split_job)
            meet(dve, "rw_in")
            rw_mix_vector(dve)
            rw_vector(dve)
            rw_end_vector(dve)
            meet(dve, "rw")
            cd_cat_vector(dve)
            meet(dve, "cd_cat")
            add_residual(dve, "cd_out")
            meet(dve, "cd_out")
            norm_vector(dve, 3, 0, lambda k: col("norm_ffn", DK + k))
            meet(dve, "n3")
            for f in range(2):
                ffn_vector(dve, 1, f)
            meet(dve, "ffn1")
            norm_vector(dve, 4, META, lambda k: col("norm_final", k), lambda k: h[:, k, META:T])
            meet(dve, "n4")
            norm_vector(dve, 5, META, lambda k: col("norm_w_2", k))
            meet(dve, "n5")
            run_phase(dve, ph["in_a"], None, split_job)
            meet(dve, "in_a")
            hgrn_vector(dve)
            meet(dve, "hgrn")
            lru_in_vector(dve)
            meet(dve, "in_b")
            lru_vector(dve)
            meet(dve, "rglru")
            ssd_in_vector(dve)
            meet(dve, "in_c")
            ssd_vector(dve)
            meet(dve, "ssd")
            cat_vector(dve)
            meet(dve, "cat")
            out_vector(dve)
            meet(dve, "out")
            norm_vector(dve, 6, META, lambda k: col("final_norm_w_2", k), lambda k: xn[:, k, 0:S2])
            meet(dve, "n6")
            end_keep(dve, 0)

        @block.tensor
        def _(pe):
            start_tensor(pe)
            meet(pe, "setup")
            norm_tensor(pe, 0, 0)
            meet(pe, "n0")
            for name in ("ab_gate", "ab_val", "ab_s"):
                multiply_phase(pe, name, T)
            meet(pe, "ab_in")
            ab_tensor(pe)
            meet(pe, "ab")
            multiply_phase(pe, "ab_out", T)
            meet(pe, "ab_out")
            norm_tensor(pe, 1, 0)
            meet(pe, "n1")
            for f in range(2):
                ffn_tensor(pe, 0, f)
            meet(pe, "ffn0")
            norm_tensor(pe, 2, 0)
            meet(pe, "n2")
            for name in ("gla", "glr"):
                multiply_phase(pe, name, T)
            meet(pe, "gla_in")
            gla_prepare_tensor(pe)
            gla_heads_tensor(pe)
            gla_end_tensor(pe)
            meet(pe, "gla")
            for name in ("rw", "rw_low"):
                multiply_phase(pe, name, T)
            meet(pe, "rw_in")
            rw_tensor(pe)
            rw_end_tensor(pe)
            meet(pe, "rw")
            meet(pe, "cd_cat")
            multiply_phase(pe, "cd_out", T)
            meet(pe, "cd_out")
            norm_tensor(pe, 3, 0)
            meet(pe, "n3")
            for f in range(2):
                ffn_tensor(pe, 1, f)
            meet(pe, "ffn1")
            norm_tensor(pe, 4, META)
            meet(pe, "n4")
            norm_tensor(pe, 5, META)
            meet(pe, "n5")
            multiply_phase(pe, "in_a", S2)
            meet(pe, "in_a")
            hgrn_tensor(pe)
            meet(pe, "hgrn")
            for name in ("in_bx", "in_bz"):
                multiply_phase(pe, name, S2)
            meet(pe, "in_b")
            lru_tensor(pe)
            meet(pe, "rglru")
            for name in ("in_xbc", "in_cz", "dt"):
                multiply_phase(pe, name, S2)
            meet(pe, "in_c")
            ssd_tensor(pe)
            meet(pe, "ssd")
            meet(pe, "cat")
            out_tensor(pe)
            meet(pe, "out")
            norm_tensor(pe, 6, META)
            meet(pe, "n6")
            end_tensor(pe)

        @block.gpsimd
        def _(pool):
            behind = {"n2": gla_pool, "gla": rw_pool, "rw": level_pool, "n5": hgrn_pool, "hgrn": lru_pool, "rglru": ssd_pool}
            start_pool(pool)
            for name in MEETINGS:
                if name == "end":
                    break
                meet(pool, name)
                if name in behind:
                    behind[name](pool)


def kernel(**inputs):
    import concourse.bacc as bacc
    from concourse.bass_utils import run_bass_kernel_spmd

    arrays = {name: np.ascontiguousarray(v) for name, v in inputs.items()}
    nc = bacc.Bacc("TRN2", target_bir_lowering=False, num_devices=1)
    a = {name: nc.dram_tensor(name, v.shape, mybir.dt.from_np(v.dtype), kind="ExternalInput").ap() for name, v in arrays.items()}
    out = nc.dram_tensor("out", (1, SEQ, D), F32, kind="ExternalOutput").ap()
    build(nc, a, out)
    return run_bass_kernel_spmd(nc, [arrays], core_ids=[0]).results[0]["out"]
```

```python
import numpy as np
import concourse.bass as bass
from concourse import mybir

F32 = mybir.dt.float32
F32R = mybir.dt.float32r
I32 = mybir.dt.int32
ALU = mybir.AluOpType
ACT = mybir.ActivationFunctionType

P = 128
D = 2048
DK = D // P
META, SEQ = 16, 256
T = META + SEQ
TILES = [(0, META), (META, P), (META + P, P)]
CW = 1024 // P
CONF_K, SC_K, FFN_K, CONV_K = 31, 3, 3, 4
D_FF = 5632
FF = D_FF // P
FH = FF // 2
EPS, LN_EPS, GN_EPS = 1e-6, 1e-5, 64e-5
GLA_CHUNK, GLA_H, GLA_SCALE, GLA_NORM = 64, 4, 128.0 ** -0.5, 16.0
RW_CHUNK, RW_N = 32, 64
RW_DECAY = 0.6065306597126334
GLA_COLS, GLA_GLR = 3088, 3072
DT_COL, GATE_COL = 8704, 8720
PART = 8
RING, SLOTS = 8, 4
AHEAD = SLOTS - 1
LEVELS = [1, 2, 4, 8, 16, 32, 64]

VECTORS = [
    ("norm_mix", 2 * DK), ("norm_ffn", 2 * DK), ("norm_final", DK), ("ab_conf_dw", CONF_K * CW),
    ("ab_conf_dw_b", CW), ("ab_conf_ln_g", CW), ("ab_conf_ln_b", CW), ("ab_sc_dw", SC_K * CW),
    ("cd_gla_b", 4), ("cd_gla_norm_g", CW), ("cd_rw_mu", 26), ("cd_rw_w0", CW), ("cd_rw_a0", CW),
    ("cd_rw_kk", CW), ("cd_rw_ka", CW), ("cd_rw_rk", CW), ("cd_rw_ln_g", CW), ("cd_rw_ln_b", CW),
    ("ffn_dw", 2 * FFN_K * 2 * FF), ("norm_w_2", DK), ("final_norm_w_2", DK), ("hgrn_norm_w_2", CW),
    ("rglru_conv_w_2", CONV_K * CW), ("rglru_conv_b_2", CW), ("rglru_ba_2", CW), ("rglru_bx_2", CW),
    ("rglru_lambda_2", CW), ("ssd_conv_w_2", CONV_K * 12), ("ssd_conv_b_2", 12), ("ssd_norm_w_2", CW),
]
VOFF, NROWS = {}, 0
for _name, _rows in VECTORS:
    VOFF[_name] = NROWS
    NROWS += _rows
ROW_GROUPS = (NROWS + P - 1) // P


def order(*names):
    return {name: n + 1 for n, name in enumerate(names)}


class Phase:

    def __init__(self, n, jobs):
        self.n, self.jobs, self.base = n, jobs, 0
        self.parts = [x for u, (kt, _, _) in enumerate(jobs) for x in ((u, 0, kt - kt // 2), (u, kt - kt // 2, kt // 2))]


def weights(ap, k0, kt, cols):
    return ap.rearrange("(k p) n -> p k n", p=P)[:, k0:k0 + kt, cols]


def columns(view, first, i, per, u):
    return view[:, :, first + u * P:][:, :, bass.ds(i * (per * P), P)]


def plan(a):
    def tiles(ap, first, per, kt=DK):
        view = ap.rearrange("(k p) n -> p k n", p=P)[:, 0:kt, :]
        return [(kt, P, lambda i, u=u: columns(view, first, i, per, u)) for u in range(per)]

    ab, cd, w2 = a["ab_w_in"][0], a["cd_w_in"][0], a["w_in_2"][0]
    ph = {}
    ph["ab_gate"] = Phase(2, tiles(ab, 1024, 4))
    ph["ab_val"] = Phase(2, tiles(ab, 0, 4))
    ph["ab_s"] = Phase(2, tiles(ab, 2048, 4) + tiles(ab, 3072, 4) + tiles(ab, 4096, 4))
    ph["ab_out"] = Phase(4, tiles(a["ab_w_out"][0], 0, 4))

    def ffn(layer):
        for f in range(2):
            up = a["ffn_w_up"][layer]
            val, gate = tiles(up, f * FH * P, 2), tiles(up, D_FF + f * FH * P, 2)
            ph[f"up{layer}{f}"] = Phase(FH // 2, [gate[0], val[0], gate[1], val[1]])
            down = a["ffn_w_down"][layer].rearrange("(k p) n -> p k n", p=P)
            half = FH // 2
            jobs = []
            for u in range(2):
                for part in range(2):
                    k0 = f * FH + part * half
                    jobs.append((half, P, lambda i, u=u, k0=k0: columns(down[:, k0:k0 + half, :], 0, i, 2, u)))
            ph[f"down{layer}{f}"] = Phase(DK // 2, jobs)

    ffn(0)
    cdv = cd.rearrange("(k p) n -> p k n", p=P)
    ph["gla"] = Phase(6, tiles(cd, 0, 4))
    ph["glr"] = Phase(1, [(DK, META, lambda i: cdv[:, :, GLA_GLR:GLA_COLS])])
    ph["rw"] = Phase(6, tiles(cd, GLA_COLS, 4))
    ph["rw_low"] = Phase(1, tiles(cd, GLA_COLS + 24 * P, 2))
    ph["cd_out"] = Phase(4, tiles(a["cd_w_out"][0], 0, 4))
    ffn(1)
    w2v = w2.rearrange("(k p) n -> p k n", p=P)
    ph["in_a"] = Phase(8, tiles(w2, 0, 4))
    ph["in_bx"] = Phase(2, tiles(w2, 4096, 4))
    ph["in_bz"] = Phase(2, tiles(w2, 5120, 4))
    ph["dt"] = Phase(1, [(DK, 16, lambda i: w2v[:, :, DT_COL:GATE_COL])])
    ph["in_xbc"] = Phase(3, tiles(w2, 7168, 4))
    ph["in_cz"] = Phase(2, tiles(w2, 6144, 4))
    jobs = []
    wo = a["w_out_2"][0].rearrange("(k p) n -> p k n", p=P)
    for u in range(2):
        for n in range(3):
            jobs.append((DK, P, lambda i, u=u, n=n: columns(w2v, GATE_COL + n * D, i, 2, u)))
            jobs.append((CW, P, lambda i, u=u, n=n: columns(wo[:, n * CW:(n + 1) * CW, :], 0, i, 2, u)))
    ph["out"] = Phase(DK // 2, jobs)
    base, behind = 0, [p.parts for p in ph.values()]
    for m, p in enumerate(ph.values()):
        p.base = base
        base += p.n * len(p.parts)
        follow = p.parts + [x for parts in behind[m + 1:m + 3] for x in parts]
        again = p.parts + (p.parts if p.n > 1 else [])
        p.ahead = [max(lst[v + AHEAD][2] for lst in (follow, again) if v + AHEAD < len(lst)) if v + AHEAD < max(len(follow), len(again))
                   else 0 for v in range(len(p.parts))]
    return ph


def build(nc, a, out):
    ph = plan(a)
    at = [(nc.sbuf_base + 63) // 64 * 64]

    def place(name, shape, dt=F32, offset=None):
        size = 4
        for s in shape[1:]:
            size *= s
        if offset is None:
            offset = at[0]
            at[0] += (size + 63) // 64 * 64
        return nc.alloc_sbuf_tensor_at(name, shape, dt, offset=offset), offset

    raw, _ = place("raw", [P, RING, PART, P])
    w_hi, _ = place("w_hi", [P, SLOTS, PART, P], F32R)
    w_lo, _ = place("w_lo", [P, SLOTS, PART, P], F32R)
    h, _ = place("h", [P, DK, T])
    x_hi, x_off = place("x_hi", [P, DK, T], F32R)
    x_lo, _ = place("x_lo", [P, DK, T], F32R)
    work2, _ = place("work2", [P, 2 * DK * T], F32, x_off)
    vec, _ = place("vec", [P, NROWS])
    ident, _ = place("ident", [P, P])
    ones, _ = place("ones", [P, P])
    pair_ones, _ = place("pair_ones", [P, P])
    le, _ = place("le", [P, P])
    le64, _ = place("le64", [P, P])
    rw_mask, _ = place("rw_mask", [P, 4, P])
    up16, _ = place("up16", [P, P])
    low16, _ = place("low16", [P, P])
    low21, _ = place("low21", [P, P])
    eye2, _ = place("eye2", [P, RW_N])
    seg, _ = place("seg", [P, T])
    eps, _ = place("eps", [P, 4])
    omka, _ = place("omka", [P, CW])
    dskip, _ = place("dskip", [P, CW])
    small, _ = place("small", [16, 4])
    side, _ = place("side", [P, 2048])
    arena, arena_off = place("arena", [P, 18432])
    act_hi, _ = place("act_hi", [P, 24 * SEQ], F32R, arena_off)
    act_lo, _ = place("act_lo", [P, 24 * SEQ], F32R, arena_off + 4 * 24 * SEQ)
    ps = nc.alloc_psum_tensor("ps", [P, 8, 512], F32)

    def view(buf, first, *shape):
        n = 1
        for s in shape:
            n *= s
        v = buf[:, first:first + n]
        if len(shape) == 1:
            return v
        names = "abcd"[:len(shape)]
        return v.rearrange(f"p ({' '.join(names)}) -> p {' '.join(names)}", **dict(zip(names, shape)))

    def col(name, tile=0):
        first = VOFF[name]
        if isinstance(tile, int):
            return vec[:, first + tile:first + tile + 1]
        return vec[:, first:][:, bass.ds(tile, 1)]

    def cols(name, n, tile=0):
        return vec[:, VOFF[name] + tile:VOFF[name] + tile + n]

    sem = nc.alloc_semaphore
    loaded = [sem(f"loaded{r}") for r in range(RING)]
    rounded = sem("rounded")
    split = sem("split")
    multiplied = sem("multiplied")
    drained = [sem(f"drained{b}") for b in range(2)]
    met = sem("met")
    params_in, masks_made = sem("params_in"), sem("masks_made")
    rows_turned = sem("rows_turned")
    x_turned, x_kept = sem("x_turned"), [sem(f"x_kept{b}") for b in range(2)]
    norm_sq, norm_hi, norm_lo = ({n: sem(f"norm_{what}{n}") for n in which}
                                 for what, which in (("sq", (0, 4, 5)), ("hi", (0, 1, 2, 3, 5)), ("lo", (0, 1, 2, 3, 5))))
    norm_sum, norm_std, norm_xn = sem("norm_sum"), sem("norm_std"), sem("norm_xn")
    hid_tap, hid_silu, hid_made = sem("hid_tap"), sem("hid_silu"), sem("hid_made")
    hid_hi_made, hid_lo_made = sem("hid_hi_made"), sem("hid_lo_made")
    side_in = sem("side_in")
    seg_made = sem("seg_made")
    padded = sem("padded")
    out_turned, out_kept, out_stored = sem("out_turned"), [sem(f"out_kept{b}") for b in range(2)], sem("out_stored")
    gates_made, products_made, tile_summed = sem("gates_made"), sem("products_made"), [sem(f"tile_summed{b}") for b in range(2)]

    def trio(name):
        return sem(f"{name}_vector"), sem(f"{name}_scalar"), sem(f"{name}_tensor")

    def meet(eng, name):
        eng.drain().then_inc(met, 1)
        eng.wait_ge(met, 4 * MEETINGS[name])

    def part_early(pe):
        pe.drain().then_inc(met, 1)

    passed = sem("passed")

    def settle(eng):
        eng.sem_inc(passed, 1)

    MEETINGS = order("setup", "ab_in", "ab_out", "ffn0", "gla_in", "gla", "rw_in", "rw", "cd_out", "ffn1",
                     "in_a", "hgrn", "in_b", "rglru", "in_c", "ssd", "out")

    def load_phase(sp, p):
        n = len(p.parts)

        def body(i):
            for v, (u, k0, kt) in enumerate(p.parts):
                j, w, src = p.base + v, p.jobs[u][1], p.jobs[u][2]
                sp.wait_ge(split, i * n + (j + 1))
                settle(sp)
                sp.dma_start(raw[:, j % RING, 0:kt, 0:w], src(i)[:, k0:k0 + kt, :]).then_inc(loaded[j % RING], 16)
        if p.n == 1:
            body(0)
        else:
            with sp.Fori(0, p.n) as i:
                body(i)

    def round_part(act, p, i, v, kt):
        j, n = p.base + v, len(p.parts)
        act.wait_ge(loaded[j % RING], i * (16 * n // RING) + 16 * (j // RING + 1))
        act.wait_ge(multiplied, i * n + (j + 1))
        nc.scalar.activation(w_hi[:, j % SLOTS, 0:kt], raw[:, j % RING, 0:kt], ACT.Copy).then_inc(rounded, 1)

    def split_part(dve, p, i, v, kt):
        j = p.base + v
        dve.wait_ge(rounded, i * len(p.parts) + (j + 1))
        nc.vector.tensor_tensor(w_lo[:, j % SLOTS, 0:kt], raw[:, j % RING, 0:kt],
                                w_hi[:, j % SLOTS, 0:kt].bitcast(F32), ALU.subtract).then_inc(split, 1)

    def run_phase(eng, p, work, prepare, last=False):
        def body(i, on):
            for v, (u, k0, _) in enumerate(p.parts):
                if on or v + AHEAD < len(p.parts):
                    prepare(eng, p, i, v + AHEAD, p.ahead[v])
                if k0 and work is not None:
                    work(i, u)
        n = p.n - 1 if last else p.n
        if n == 1:
            body(0, True)
        elif n > 1:
            with eng.Fori(0, n) as i:
                body(i, True)
        if last:
            body(p.n - 1, False)

    def result_ready(eng, p, i, u):
        eng.wait_ge(multiplied, i * len(p.parts) + (p.base + 2 * u + 2 + SLOTS))

    def multiply_job(pe, p, i, u, acc, moving, kt, w, start, stop):
        for v in (2 * u, 2 * u + 1):
            j, (_, k0, n) = p.base + v, p.parts[v]
            pe.wait_ge(split, i * len(p.parts) + (j + RING + 1))
            for k in range(n):
                mh, ml = moving(k0 + k)
                first, end = start and k0 + k == 0, stop and k0 + k == kt - 1
                nc.tensor.matmul(acc, w_hi[:, j % SLOTS, k, 0:w], mh, start=first, stop=False)
                nc.tensor.matmul(acc, w_hi[:, j % SLOTS, k, 0:w], ml, start=False, stop=False)
                last = nc.tensor.matmul(acc, w_lo[:, j % SLOTS, k, 0:w], mh, start=False, stop=end)
            last.then_inc(multiplied, 1)

    results, count = {}, 0
    for name, p in ph.items():
        per = len(p.jobs) // 2 if name.startswith("down") else 0 if name == "out" else len(p.jobs)
        results[name] = (count, per)
        count += p.n * per

    def bank(name, u):
        return (results[name][0] + u) % 2

    def bank_free(pe, name, i, u):
        first, per = results[name]
        pe.wait_ge(drained[bank(name, u)], i * (per // 2) + ((first + u) // 2 + 1))

    def result_out(eng, name, i, u):
        first, per = results[name]
        eng.wait_ge(drained[bank(name, u)], i * (per // 2) + ((first + u) // 2 + 2))

    def phases_out(eng, name):
        first = results[name][0]
        for b in range(2):
            eng.wait_ge(drained[b], (first - b + 1) // 2 + 1)

    def multiply_phase(pe, name, n_cols, ready=None):
        p = ph[name]

        def operand(u, k):
            if ready is not None and u == 0 and k % 4 == 0:
                pe.wait_ge(ready, k // 4 + 1)
            return x_hi[:, k, 0:n_cols], x_lo[:, k, 0:n_cols]

        def body(i):
            for u, (kt, w, _) in enumerate(p.jobs):
                bank_free(pe, name, i, u)
                multiply_job(pe, p, i, u, ps[0:w, bank(name, u), 0:n_cols],
                             lambda k: operand(u, k), kt, w, True, True)
        if p.n == 1:
            body(0)
        else:
            with pe.Fori(0, p.n) as i:
                body(i)

    def tile_of(buf, first, i, per):
        if isinstance(i, int):
            return buf[:, first + per * i]
        return buf[:, first:][:, bass.ds(i * per, 1)].rearrange("p a t -> p (a t)")

    def keep_results(act, name, to):
        p = ph[name]

        def work(i, u):
            result_ready(act, p, i, u)
            w, dst = p.jobs[u][1], to(i, u)
            nc.scalar.activation(dst, ps[0:w, bank(name, u), 0:dst.shape[-1]], ACT.Copy).then_inc(drained[bank(name, u)], 1)
        run_phase(act, p, work, round_part)

    def add_residual(dve, name):
        p = ph[name]

        def work(i, u):
            result_ready(dve, p, i, u)
            t = tile_of(h, u, i, len(p.jobs))
            nc.vector.tensor_tensor(t, ps[:, bank(name, u), 0:T], t, ALU.add).then_inc(drained[bank(name, u)], 1)
        run_phase(dve, p, work, split_part)

    def square_residual(act, name):
        p = ph[name]

        def work(i, u):
            result_out(act, name, i, u)
            square_tile(act, name, i, u, len(p.jobs), 0)
        run_phase(act, p, work, round_part)

    xn = view(arena, 0, DK, T)
    sq_tile, sq_sum = view(arena, 15400, 2, T), arena[:, 15400 + 2 * T:15400 + 3 * T]
    sq_made, sq_used, sq_summed = sem("sq_made"), [sem(f"sq_used{b}") for b in range(2)], sem("sq_summed")
    BEHIND = {"ab_out": 0, "down01": 1, "cd_out": 2, "down11": 3, "out": 4}

    def square_tile(act, name, i, u, per, c0):
        act.wait_ge(sq_used[u % 2], i * (per // 2) + (BEHIND[name] * (DK // 2) + u // 2 + 1))
        nc.scalar.activation(sq_tile[:, u % 2, c0:T], tile_of(h, u, i, per)[:, c0:T], ACT.Square).then_inc(sq_made, 1)

    def sum_squares(pool, name, c0):
        pool.wait_ge(norm_sum, (1, 2, 3, 4, 6)[BEHIND[name]])
        nc.gpsimd.memset(sq_sum, 0.0)
        with pool.Fori(0, DK // 2) as i:
            for b in range(2):
                pool.drain()
                pool.wait_ge(sq_made, i * 2 + (BEHIND[name] * DK + b + 1))
                nc.gpsimd.tensor_tensor(sq_sum[:, c0:T], sq_sum[:, c0:T], sq_tile[:, b, c0:T], ALU.add).then_inc(sq_used[b], 1)
        pool.drain().then_inc(sq_summed, 1)

    def norm_tensor(pe, n, c0, behind=None):
        w = T - c0
        if behind is not None:
            pe.wait_ge(sq_summed, BEHIND[behind] + 1)
            nc.tensor.matmul(ps[:, 2, 0:w], ones[:], sq_sum[:, c0:T], start=True, stop=True).then_inc(norm_sum, 1)
            return
        for g in range(4):
            pe.wait_ge(norm_sq[n], g + 1)
            for k in range(4 * g, 4 * g + 4):
                mm = nc.tensor.matmul(ps[:, 2, 0:w], ones[:], xn[:, k, 0:w], start=(k == 0), stop=(k == DK - 1))
        mm.then_inc(norm_sum, 1)

    def norm_scalar(act, n, c0, split_out, behind=None, after=None):
        w = T - c0
        for g in range(4) if behind is None else ():
            t = slice(4 * g, 4 * g + 4)
            if after is not None:
                act.wait_ge(norm_xn, 4 * after + g + 1)
            nc.scalar.activation(xn[:, t, 0:w], h[:, t, c0:T], ACT.Square).then_inc(norm_sq[n], 1)
        act.wait_ge(norm_sum, n + 1)
        nc.scalar.activation(ps[:, 3, 0:w], ps[:, 2, 0:w], ACT.Sqrt, bias=eps[:, 0:1], scale=1.0 / D).then_inc(norm_std, 1)
        for g in range(4) if split_out else ():
            t = slice(4 * g, 4 * g + 4)
            act.wait_ge(norm_xn, 4 * n + g + 1)
            nc.scalar.activation(x_hi[:, t, 0:w], xn[:, t, 0:w], ACT.Copy).then_inc(norm_hi[n], 1)

    def norm_vector(dve, n, c0, gain, to=None):
        w = T - c0

        def low(g):
            t = slice(4 * g, 4 * g + 4)
            dve.wait_ge(norm_hi[n], g + 1)
            nc.vector.tensor_tensor(x_lo[:, t, 0:w], xn[:, t, 0:w], x_hi[:, t, 0:w].bitcast(F32), ALU.subtract).then_inc(norm_lo[n], 1)
        dve.wait_ge(norm_std, n + 1)
        nc.vector.reciprocal(ps[:, 3, 0:w], ps[:, 3, 0:w])
        dve.drain()
        for g in range(4):
            for k in range(4 * g, 4 * g + 4):
                mm = nc.vector.scalar_tensor_tensor(out=xn[:, k, 0:w] if to is None else to(k), in0=h[:, k, c0:T],
                                                    scalar=gain(k), in1=ps[:, 3, 0:w], op0=ALU.mult, op1=ALU.mult)
            mm.then_inc(norm_xn, 1)
            if to is None and g:
                low(g - 1)
        if to is None:
            dve.drain()
            low(3)

    hid_hi = act_hi[:, 0:FH * T].rearrange("p (k t) -> p k t", k=FH)
    hid_lo = act_lo[:, 0:FH * T].rearrange("p (k t) -> p k t", k=FH)
    FT0 = 2 * 24 * SEQ
    f_gate, f_val = view(arena, FT0, 2, T), view(arena, FT0 + 2 * T, 2, T)
    f_act, f_hid = view(arena, FT0 + 4 * T, 2, T), view(arena, FT0 + 6 * T, 2, T)

    def ffn_tap(layer, f, t, is_gate, i, s):
        return col("ffn_dw", i * 2 + ((layer * FFN_K + t) * 2 * FF + is_gate * FF + f * FH + s))

    def ffn_scalar(act, layer, f):
        name, n0 = f"up{layer}{f}", (2 * layer + f) * FH
        p = ph[name]

        def high(i, s):
            act.wait_ge(hid_made, i * 2 + (n0 + s + 1))
            nc.scalar.activation(tile_of(hid_hi, s, i, 2), f_hid[:, s], ACT.Copy).then_inc(hid_hi_made, 1)

        def work(i, u):
            s, is_gate = u // 2, 1 - u % 2
            if u == 2:
                high(i, 0)
            result_ready(act, p, i, u)
            nc.scalar.activation((f_gate if is_gate else f_val)[:, s], ps[:, bank(name, u), 0:T], ACT.Copy,
                                 scale=ffn_tap(layer, f, 2, is_gate, i, s)).then_inc(hid_tap, 1)
            if not is_gate:
                result_out(act, name, i, u - 1)
                nc.scalar.activation(f_act[:, s], f_gate[:, s], ACT.Silu).then_inc(hid_silu, 1)
            if u == 3:
                high(i, 1)
        run_phase(act, p, work, round_part)
        name2 = f"down{layer}{f}"

        def squares(i, u):
            if u % 2:
                result_out(act, name2, i, u // 2)
                square_tile(act, name2, i, u // 2, 2, META * layer)
        run_phase(act, ph[name2], squares if f else None, round_part)

    def ffn_vector(dve, layer, f):
        name, n0 = f"up{layer}{f}", (2 * layer + f) * FH
        p = ph[name]

        def low(i, s):
            dve.wait_ge(hid_hi_made, i * 2 + (n0 + s + 1))
            nc.vector.tensor_tensor(tile_of(hid_lo, s, i, 2), f_hid[:, s], tile_of(hid_hi, s, i, 2).bitcast(F32),
                                    ALU.subtract).then_inc(hid_lo_made, 1)

        def work(i, u):
            s, is_gate = u // 2, 1 - u % 2
            if u == 2:
                low(i, 0)
            dst, acc = (f_gate if is_gate else f_val), ps[:, bank(name, u), 0:T]
            dve.wait_ge(hid_tap, i * 4 + (2 * n0 + u + 1))
            for back in (1, 2):
                mm = nc.vector.scalar_tensor_tensor(out=dst[:, s, back:T], in0=acc[:, 0:T - back],
                                                    scalar=ffn_tap(layer, f, 2 - back, is_gate, i, s),
                                                    in1=dst[:, s, back:T], op0=ALU.mult, op1=ALU.add)
                if back == 1:
                    dve.drain()
            mm.then_inc(drained[bank(name, u)], 1)
            if not is_gate:
                dve.drain()
                dve.wait_ge(hid_silu, i * 2 + (n0 + s + 1))
                nc.vector.tensor_tensor(f_hid[:, s], f_act[:, s], f_val[:, s], ALU.mult).then_inc(hid_made, 1)
            if u == 3:
                dve.drain()
                low(i, 1)
        run_phase(dve, p, work, split_part)
        name2 = f"down{layer}{f}"
        p2 = ph[name2]

        def add(i, u):
            if u % 2:
                result_ready(dve, p2, i, u)
                t = tile_of(h, u // 2, i, 2)
                nc.vector.tensor_tensor(t, ps[:, bank(name2, u // 2), 0:T], t, ALU.add).then_inc(drained[bank(name2, u // 2)], 1)
        run_phase(dve, p2, add, split_part)

    def ffn_tensor(pe, layer, f):
        multiply_phase(pe, f"up{layer}{f}", T, None if f else norm_lo[2 * layer + 1])
        name, half = f"down{layer}{f}", FH // 2
        p = ph[name]
        pe.wait_ge(hid_lo_made, (2 * layer + f + 1) * FH)
        with pe.Fori(0, p.n) as i:
            for u, (kt, w, _) in enumerate(p.jobs):
                part = u % 2
                if part == 0:
                    bank_free(pe, name, i, u // 2)
                multiply_job(pe, p, i, u, ps[:, bank(name, u // 2), 0:T],
                             lambda k: (hid_hi[:, part * half + k, :], hid_lo[:, part * half + k, :]),
                             kt, w, part == 0, part == 1)

    ab_sig, ab_sb, ab_sc = view(arena, 0, CW, T), view(arena, 2176, CW, T), view(arena, 4352, CW, T)
    ab_conv = view(arena, 6528, CW, T)
    ab_a = view(arena, 8704, CW, T + CONF_K - 1)
    ab_s = view(arena, 11136, CW, T + SC_K - 1)
    ab_tap = arena[:, 13328:13328 + T]
    ab_v, ab_act, ab_t = trio("ab")
    AB_V = order("centred", "s_made", "normed0", "normed1")
    AB_S = order("mean", "squared", "std", "s_hi", "a_hi0", "a_hi1")
    AB_T = order("sums", "squares")
    ab_lo = sem("ab_lo")

    def ab_in_scalar(act):
        p = ph["ab_gate"]

        def gate(i, u):
            result_ready(act, p, i, u)
            nc.scalar.activation(tile_of(ab_sig, u, i, 4), ps[:, bank("ab_gate", u), 0:T],
                                 ACT.Sigmoid).then_inc(drained[bank("ab_gate", u)], 1)
        run_phase(act, p, gate, round_part)
        run_phase(act, ph["ab_val"], None, round_part)
        p2 = ph["ab_s"]

        def keep(i, u):
            if u < 8:
                result_ready(act, p2, i, u)
                nc.scalar.activation(tile_of(ab_sb if u < 4 else ab_sc, u % 4, i, 4), ps[:, bank("ab_s", u), 0:T],
                                     ACT.Copy).then_inc(drained[bank("ab_s", u)], 1)
        run_phase(act, p2, keep, round_part)

    def ab_in_vector(dve):
        run_phase(dve, ph["ab_gate"], None, split_part)
        phases_out(dve, "ab_val")
        p = ph["ab_val"]

        def gated(i, u):
            result_ready(dve, p, i, u)
            nc.vector.tensor_tensor(tile_of(ab_a, u, i, 4)[:, CONF_K - 1:], ps[:, bank("ab_val", u), 0:T],
                                    tile_of(ab_sig, u, i, 4), ALU.mult).then_inc(drained[bank("ab_val", u)], 1)
        run_phase(dve, p, gated, split_part)
        p2 = ph["ab_s"]

        def conv(i, u):
            if u >= 8:
                result_ready(dve, p2, i, u)
                result_out(dve, "ab_s", i, u - 4)
                nc.vector.tensor_tensor(tile_of(ab_s, u - 8, i, 4)[:, SC_K - 1:], ps[:, bank("ab_s", u), 0:T],
                                        tile_of(ab_sc, u - 8, i, 4), ALU.mult).then_inc(drained[bank("ab_s", u)], 1)
            tile, quarter = u // 4, u % 4
            src, dst = tile_of(ab_a, tile, i, 4), tile_of(ab_conv, tile, i, 4)
            for t in range((CONF_K * quarter + 3) // 4, (CONF_K * (quarter + 1) + 3) // 4):
                dve.drain()
                wt = col("ab_conf_dw", i * 4 + (t * CW + tile))
                if t == 0:
                    nc.vector.tensor_scalar(dst, src[:, 0:T], wt, col("ab_conf_dw_b", i * 4 + tile), ALU.mult, ALU.add)
                else:
                    nc.vector.scalar_tensor_tensor(out=dst, in0=src[:, t:t + T], scalar=wt, in1=dst,
                                                   op0=ALU.mult, op1=ALU.add)
        run_phase(dve, p2, conv, split_part)

    def ab_in_pool(pool):
        phases_out(pool, "ab_s")
        for tile in (3, 7):
            nc.gpsimd.tensor_copy(ab_conv[:, tile], col("ab_conf_dw_b", tile).to_broadcast([P, T]))
            with pool.Fori(0, CONF_K) as t:
                nc.gpsimd.tensor_tensor(ab_tap, ab_a[:, tile][:, bass.ds(t, T)], col("ab_conf_dw", t * CW + tile).to_broadcast([P, T]), ALU.mult)
                pool.drain()
                nc.gpsimd.tensor_tensor(ab_conv[:, tile], ab_conv[:, tile], ab_tap, ALU.add)
                pool.drain()

    def ab_vector(dve):
        dve.wait_ge(ab_act, AB_S["mean"])
        mean = ps[:, 4, 0:T].unsqueeze(1).to_broadcast([P, CW, T])
        nc.vector.tensor_tensor(ab_conv, ab_conv, mean, ALU.subtract).then_inc(ab_v, 1)
        for t in range(SC_K):
            for k in range(CW):
                wt, dst = col("ab_sc_dw", t * CW + k), ab_sig[:, k]
                if t == 0:
                    nc.vector.tensor_scalar(dst, ab_s[:, k, 0:T], wt, None, ALU.mult)
                else:
                    nc.vector.scalar_tensor_tensor(out=dst, in0=ab_s[:, k, t:t + T], scalar=wt, in1=dst,
                                                   op0=ALU.mult, op1=ALU.add)
            dve.drain()
        nc.vector.tensor_tensor(ab_sb, ab_sb, ab_sig, ALU.mult).then_inc(ab_v, 1)
        dve.wait_ge(ab_act, AB_S["std"])
        nc.vector.reciprocal(ps[:, 5, 0:T], ps[:, 5, 0:T])
        dve.drain()
        rstd = ps[:, 5, 0:T].unsqueeze(1).to_broadcast([P, 4, T])
        for half in range(2):
            t = slice(4 * half, 4 * half + 4)
            nc.vector.tensor_tensor(ab_conv[:, t], ab_conv[:, t], rstd, ALU.mult).then_inc(ab_v, 1)
        for half in range(2):
            t = slice(4 * half, 4 * half + 4)
            dve.wait_ge(ab_act, AB_S[f"a_hi{half}"])
            nc.vector.tensor_tensor(x_lo[:, t], ab_conv[:, t], x_hi[:, t].bitcast(F32), ALU.subtract).then_inc(ab_lo, 1)
        for half in range(2):
            t = slice(4 * half, 4 * half + 4)
            x = slice(CW + 4 * half, CW + 4 * half + 4)
            nc.vector.tensor_tensor(x_lo[:, x], ab_sb[:, t], x_hi[:, x].bitcast(F32), ALU.subtract).then_inc(ab_lo, 1)

    def ab_scalar(act):
        act.wait_ge(ab_t, AB_T["sums"])
        nc.scalar.activation(ps[:, 4, 0:T], ps[:, 2, 0:T], ACT.Copy, scale=1.0 / 1024).then_inc(ab_act, 1)
        act.wait_ge(ab_v, AB_V["centred"])
        nc.scalar.activation(ab_sc, ab_conv, ACT.Square).then_inc(ab_act, 1)
        act.wait_ge(ab_t, AB_T["squares"])
        nc.scalar.activation(ps[:, 5, 0:T], ps[:, 3, 0:T], ACT.Sqrt, bias=eps[:, 1:2], scale=1.0 / 1024).then_inc(ab_act, 1)
        act.wait_ge(ab_v, AB_V["s_made"])
        nc.scalar.activation(x_hi[:, CW:DK], ab_sb, ACT.Copy).then_inc(ab_act, 1)
        for half in range(2):
            act.wait_ge(ab_v, AB_V[f"normed{half}"])
            for k in range(4 * half, 4 * half + 4):
                nc.scalar.activation(ab_conv[:, k], ab_conv[:, k], ACT.Silu, scale=col("ab_conf_ln_g", k),
                                     bias=col("ab_conf_ln_b", k))
            act.drain()
            t = slice(4 * half, 4 * half + 4)
            nc.scalar.activation(x_hi[:, t], ab_conv[:, t], ACT.Copy).then_inc(ab_act, 1)

    def ab_tensor(pe):
        for k in range(CW):
            mm = nc.tensor.matmul(ps[:, 2, 0:T], ones[:], ab_conv[:, k], start=(k == 0), stop=(k == CW - 1))
        mm.then_inc(ab_t, 1)
        pe.wait_ge(ab_act, AB_S["squared"])
        for k in range(CW):
            mm = nc.tensor.matmul(ps[:, 3, 0:T], ones[:], ab_sc[:, k], start=(k == 0), stop=(k == CW - 1))
        mm.then_inc(ab_t, 1)
    GT = GLA_H * T
    zg = view(arena, 0, 24, T)
    g_low = arena[0:META, 6528:6528 + T]
    g_x, g_e = view(arena, 6800, GLA_H, T), view(arena, 7888, GLA_H, T)
    g_cum, g_end = view(arena, 8976, GLA_H, T), view(arena, 10064, GLA_H, T)
    g_dec = view(arena, 11152, GLA_H, 8)
    g_w2 = arena[0:META, 11200:11712]
    g_kd, g_ks, g_v = arena[:, 11712:11984], arena[:, 11984:12256], view(arena, 12256, 2, T)
    g_tok = view(arena, 12800, 3, 3 * P)
    g_sc = view(arena, 13952, 3, P)
    g_state = view(arena, 14336, 4, 2 * P)
    o_gla = view(arena, 16256, CW, T)
    gla_v, gla_s, gla_t = trio("gla")
    GLA_V = order("biased", "shifted", "summed", "ends", "q_ready")
    GLA_S = order("log", "grown", "shrunk", "to_end", "gate")
    GLA_T = order("low_rank")
    glh_v, glh_s, glh_t = trio("glh")
    GLH_V = order("staged", "masked", "chained")
    GLH_S = order("kept", "out")
    GLH_T = order("turned", "states", "mixed")
    gle_v, gle_s, gle_t = trio("gle")
    GLE_S = order("squared", "rstd")
    GLE_T = order("sums")
    CHUNK_AT = [(0, META)] + [(META + GLA_CHUNK * c, GLA_CHUNK) for c in range(4)]

    def gla_prepare_vector(dve):
        dve.wait_ge(gla_t, GLA_T["low_rank"])
        for hd in range(GLA_H):
            mm = nc.vector.tensor_scalar(g_x[:, hd], ps[:, hd, 0:T], col("cd_gla_b", hd), None, ALU.add)
        mm.then_inc(gla_v, 1)
        dve.wait_ge(gla_s, GLA_S["log"])
        nc.vector.scalar_tensor_tensor(out=g_x, in0=g_x, scalar=0.0, in1=g_e, op0=ALU.min,
                                       op1=ALU.subtract).then_inc(gla_v, 1)
        dve.drain()
        dve.wait_ge(seg_made, 1)
        for hd in range(GLA_H):
            mm = nc.vector.tensor_tensor_scan(g_cum[:, hd], seg[:], g_x[:, hd], 0.0, ALU.mult, ALU.add)
        mm.then_inc(gla_v, 1)
        dve.drain()
        nc.vector.tensor_tensor(g_end[:, :, 0:META], g_cum[:, :, META - 1:META].to_broadcast([P, GLA_H, META]),
                                g_cum[:, :, 0:META], ALU.subtract)
        for hd in range(GLA_H):
            c = g_cum[:, hd, META:].rearrange("p (c t) -> p c t", t=GLA_CHUNK)
            e = g_end[:, hd, META:].rearrange("p (c t) -> p c t", t=GLA_CHUNK)
            mm = nc.vector.tensor_tensor(e, c[:, :, GLA_CHUNK - 1:].to_broadcast([P, 4, GLA_CHUNK]), c, ALU.subtract)
        mm.then_inc(gla_v, 1)
        dve.wait_ge(gla_s, GLA_S["grown"])
        nc.vector.scalar_tensor_tensor(out=zg[:, 0:4], in0=zg[:, 0:4], scalar=GLA_SCALE, in1=g_x,
                                       op0=ALU.mult, op1=ALU.mult).then_inc(gla_v, 1)
        dve.wait_ge(gla_s, GLA_S["to_end"])
        nc.vector.tensor_tensor(g_end, zg[:, 4:8], g_end, ALU.mult)
        dve.drain()
        nc.vector.tensor_tensor(zg[:, 4:8], zg[:, 4:8], g_e, ALU.mult)
        dve.drain()

    def gla_prepare_scalar(act):
        act.wait_ge(gla_v, GLA_V["biased"])
        nc.scalar.activation(g_e, g_x, ACT.Abs)
        act.drain()
        nc.scalar.activation(g_e, g_e, ACT.Exp, scale=-1.0)
        act.drain()
        nc.scalar.activation(g_e, g_e, ACT.Ln, bias=eps[:, 3:4]).then_inc(gla_s, 1)
        act.wait_ge(gla_v, GLA_V["summed"])
        nc.scalar.activation(g_x, g_cum, ACT.Exp, scale=1.0 / GLA_NORM).then_inc(gla_s, 1)
        nc.scalar.activation(g_e, g_cum, ACT.Exp, scale=-1.0 / GLA_NORM).then_inc(gla_s, 1)
        nc.scalar.activation(g_dec[:, :, 0:1], g_cum[:, :, META - 1:META], ACT.Exp, scale=1.0 / GLA_NORM)
        nc.scalar.activation(g_dec[:, :, 1:5], g_cum[:, :, META + GLA_CHUNK - 1::GLA_CHUNK], ACT.Exp, scale=1.0 / GLA_NORM)
        act.wait_ge(gla_v, GLA_V["ends"])
        nc.scalar.activation(g_end, g_end, ACT.Exp, scale=1.0 / GLA_NORM).then_inc(gla_s, 1)
        nc.scalar.activation(zg[:, 16:24], zg[:, 16:24], ACT.Silu).then_inc(gla_s, 1)

    def gla_prepare_tensor(pe):
        pe.wait_ge(side_in, 16)
        for hd in range(GLA_H):
            mm = nc.tensor.matmul(ps[:, hd, 0:T], g_w2[:, hd * P:(hd + 1) * P], g_low, start=True, stop=True)
        mm.then_inc(gla_t, 1)

    def gla_heads_vector(dve):
        nc.vector.memset(g_sc, 0.0)
        dve.drain()
        with dve.Fori(0, GLA_H) as hd:
            v, s, t = (hd * len(GLH_V), hd * len(GLH_S), hd * len(GLH_T))
            nc.vector.tensor_copy(g_kd, tile_of(zg, 4, hd, 1))
            nc.vector.tensor_copy(g_ks, tile_of(g_end, 0, hd, 1))
            nc.vector.tensor_copy(g_v, zg[:, 8:][:, bass.ds(hd * 2, 2)]).then_inc(glh_v, 1)
            dve.wait_ge(glh_t, t + GLH_T["turned"])
            settle(dve)
            for tt, (t0, n) in enumerate(TILES):
                mm = nc.vector.copy_predicated(g_sc[0:n, tt, 0:n], le64[0:n, 0:n].bitcast(I32), ps[0:n, 3, tt * P:tt * P + n])
            mm.then_inc(glh_v, 1)
            dve.wait_ge(glh_t, t + GLH_T["states"])
            nc.vector.tensor_copy(g_state[:, 0], ps[:, 4, 0:2 * P])
            added = [None, ps[:, 4, 2 * P:4 * P], ps[:, 5, 0:2 * P], ps[:, 6, 0:2 * P]]
            for c in range(1, 4):
                dve.drain()
                dec = g_dec[:, bass.ds(hd, 1), c:c + 1].rearrange("p a b -> p (a b)")
                mm = nc.vector.scalar_tensor_tensor(out=g_state[:, c], in0=g_state[:, c - 1], scalar=dec, in1=added[c],
                                                    op0=ALU.mult, op1=ALU.add)
            mm.then_inc(glh_v, 1)
            dve.wait_ge(glh_t, t + GLH_T["mixed"])

    def gla_heads_scalar(act):
        with act.Fori(0, GLA_H) as hd:
            v, s, t = (hd * len(GLH_V), hd * len(GLH_S), hd * len(GLH_T))
            act.wait_ge(glh_t, t + GLH_T["turned"])
            for tt, (t0, n) in enumerate(TILES):
                mm = nc.scalar.activation(g_tok[0:n, tt], ps[0:n, tt, 0:3 * P], ACT.Copy)
            mm.then_inc(glh_s, 1)
            act.wait_ge(glh_t, t + GLH_T["mixed"])
            for u in range(2):
                mm = nc.scalar.activation(tile_of(o_gla, u, hd, 2), ps[:, u, 0:T], ACT.Copy)
            mm.then_inc(glh_s, 1)

    def gla_heads_tensor(pe):
        pe.wait_ge(gla_s, GLA_S["gate"])
        with pe.Fori(0, GLA_H) as hd:
            v, s, t = (hd * len(GLH_V), hd * len(GLH_S), hd * len(GLH_T))
            q = tile_of(zg, 0, hd, 1)
            pe.wait_ge(glh_v, v + GLH_V["staged"])
            for tt, (t0, n) in enumerate(TILES):
                for a_, src in enumerate((g_v[:, 0], g_v[:, 1], g_ks)):
                    nc.tensor.transpose(ps[0:n, tt, a_ * P:(a_ + 1) * P], src[:, t0:t0 + n], ident[:])
                mm = nc.tensor.matmul(ps[0:n, 3, tt * P:tt * P + n], g_kd[:, t0:t0 + n], q[:, t0:t0 + n], start=True, stop=True)
            mm.then_inc(glh_t, 1)
            pe.wait_ge(glh_s, s + GLH_S["kept"])
            for c, (tt, r0, n, b, c0) in enumerate([(0, 0, META, 4, 0), (1, 0, 64, 4, 2 * P), (1, 64, 64, 5, 0), (2, 0, 64, 6, 0)]):
                mm = nc.tensor.matmul(ps[:, b, c0:c0 + 2 * P], g_tok[r0:r0 + n, tt, 2 * P:3 * P], g_tok[r0:r0 + n, tt, 0:2 * P],
                                      start=True, stop=True)
            mm.then_inc(glh_t, 1)
            pe.wait_ge(glh_v, v + GLH_V["chained"])
            for u in range(2):
                for c, (c0, cn) in enumerate(CHUNK_AT):
                    tt = (c + 1) // 2
                    t0, n = TILES[tt]
                    mm = nc.tensor.matmul(ps[:, u, c0:c0 + cn], g_tok[0:n, tt, u * P:(u + 1) * P], g_sc[0:n, tt, c0 - t0:c0 - t0 + cn],
                                          start=True, stop=(c == 0))
                    if c:
                        mm = nc.tensor.matmul(ps[:, u, c0:c0 + cn], g_state[:, c - 1, u * P:(u + 1) * P], q[:, c0:c0 + cn],
                                              start=False, stop=True)
            mm.then_inc(glh_t, 1)
            pe.wait_ge(glh_s, s + GLH_S["out"])

    def gla_end_vector(dve):
        dve.wait_ge(gle_s, GLE_S["rstd"])
        for u in range(2):
            nc.vector.tensor_tensor(o_gla[:, u::2], o_gla[:, u::2], g_x, ALU.mult)
        dve.drain()
        for k in range(CW):
            nc.vector.scalar_tensor_tensor(out=o_gla[:, k], in0=o_gla[:, k], scalar=col("cd_gla_norm_g", k), in1=zg[:, 16 + k],
                                           op0=ALU.mult, op1=ALU.mult)

    def gla_end_scalar(act):
        act.drain()
        sq = view(arena, 8976, CW, T)
        nc.scalar.activation(sq, o_gla, ACT.Square).then_inc(gle_s, 1)
        act.wait_ge(gle_t, GLE_T["sums"])
        nc.scalar.activation(g_x, ps[:, 0:GLA_H, 0:T], ACT.Ln, bias=eps[:, 0:1], scale=1.0 / 256)
        act.drain()
        nc.scalar.activation(g_x, g_x, ACT.Exp, scale=-0.5).then_inc(gle_s, 1)

    def gla_end_tensor(pe):
        sq = view(arena, 8976, CW, T)
        pe.wait_ge(gle_s, GLE_S["squared"])
        for hd in range(GLA_H):
            for u in range(2):
                mm = nc.tensor.matmul(ps[:, hd, 0:T], ones[:], sq[:, 2 * hd + u], start=(u == 0), stop=(u == 1))
        mm.then_inc(gle_t, 1)

    ZW = T + 1
    zr = view(arena, 0, 26, ZW)
    zt = zr[:, :, 1:ZW]
    NP = 2
    NH = 2 * NP
    CH = [(0, META)] + [(META + RW_CHUNK * c, RW_CHUNK) for c in range(SEQ // RW_CHUNK)]

    def temp(n):
        return view(arena, 7104 + 544 * n, NP, T)

    (r_prev, r_a, r_cum, r_kend, r_grow, r_kh, r_kk, r_x, r_k2, r_bend) = (temp(n) for n in range(10))
    r_ar = view(arena, 7104 + 544 * 10, NP, 2, T)
    r_bh, r_bonus, r_g, r_val = temp(12), temp(13), temp(14), temp(15)
    r_wst, r_gst = view(arena, 7104 + 544 * 14, NP, P), view(arena, 7104 + 544 * 14 + 256, NP, P)
    r_wend = view(arena, 7104 + 544 * 16, 9, NP)
    r_f = r_prev
    r_q1, r_p1, r_l21, r_y, r_p2, r_q2 = (view(arena, 7104 + 544 * n, NH, P) for n in (1, 2, 4, 6, 7, 8))
    r_p4, r_q4, r_p8, r_t16, r_z1 = r_p1, r_q1, r_p2, r_p1, r_q2
    r_mm = view(work2, 0, NH, 4, P)
    r_tok = view(work2, 2048, NP, 4, P)
    r_gin, r_gh = view(work2, 3072, NH, P), view(work2, 3584, NH, P)
    r_trans = view(work2, 4096, 8, NP, P)
    r_add = view(work2, 6144, 8, NP, RW_N)
    r_state = view(work2, 7168, 8, NP, RW_N)
    rws_s, RWS_S = sem("rws_scalar"), order("low")
    rw_v, rw_s, rw_t = trio("rw")

    def tile_stages(stages, two):
        return [f"{st}{tt}{p_}" for tt in range(3) for group in stages if tt or group[0] not in two for p_ in range(NP) for st in group]

    RW_V = order("staged", "keys", "norm", "cum", "bonus", "ready",
                 *tile_stages([("p1", "m"), ("q2",), ("q4",), ("y4",), ("y8",), ("z1",), ("t32",), ("fe",)], ("z1", "t32")),
                 *[f"s{c}" for c in range(1, 9)], "end")
    RW_S = order("rates", "norm", "decays", "kept",
                 *tile_stages([("tok",), ("p2",), ("p4",), ("p8",), ("t16",), ("gh",), ("add",)], ("t16",)))
    RW_T = order("gates", "norm", "bonus",
                 *tile_stages([("x",), ("p2",), ("p4",), ("p8",), ("y8",), ("z1",), ("w",), ("gh",), ("fe",)], ("z1", "w")),
                 *[f"s{c}" for c in range(2, 9)], "y")
    rwf_v, rwf_s, rwf_t = trio("rwf")
    RWF_V, RWF_S, RWF_T = order("centred"), order("squared", "rstd"), order("sums", "squares")

    def pair(buf, first, q):
        return buf[:, first:][:, bass.ds(q * NP, NP)]

    def rw_in_vector(dve):
        dve.wait_ge(padded, 1)
        for name, first, per in (("rw", 0, 4), ("rw_low", 24, 2)):
            def mix(i, u, name=name, first=first, per=per):
                d = arena[:, 7104 + (u % 2) * T:7104 + (u % 2 + 1) * T]
                z = tile_of(zr, first + u, i, per)
                result_out(dve, name, i, u)
                nc.vector.tensor_tensor(d, z[:, 0:T], z[:, 1:ZW], ALU.subtract)
                dve.drain()
                nc.vector.scalar_tensor_tensor(out=z[:, 1:ZW], in0=d, scalar=col("cd_rw_mu", i * per + (first + u)), in1=z[:, 1:ZW],
                                               op0=ALU.mult, op1=ALU.add)
            run_phase(dve, ph[name], mix, split_part)

    def rw_mix_scalar(act):
        nc.scalar.activation(zt[0:64, 24], zt[0:64, 24], ACT.Tanh)
        nc.scalar.activation(zt[:, 25], zt[:, 25], ACT.Sigmoid).then_inc(rws_s, 1)

    def rw_vector(dve):
        dve.wait_ge(seg_made, 2)
        dve.wait_ge(side_in, 64)
        nc.vector.memset(view(work2, 4096, 2048), 0.0)
        dve.drain()
        with dve.Fori(0, 8 // NP) as q:
            V, S, TT = q * len(RW_V), q * len(RW_S), q * len(RW_T)

            def done(ins):
                ins.then_inc(rw_v, 1)
            nc.vector.tensor_copy(r_wst, side[:, 0:1024].rearrange("p (a b) -> p a b", b=P)[:, bass.ds(q * NP, NP)])
            done(nc.vector.tensor_copy(r_gst, side[:, 1024:2048].rearrange("p (a b) -> p a b", b=P)[:, bass.ds(q * NP, NP)]))
            nc.vector.tensor_copy(r_val, pair(zt, 16, q))
            for p_ in range(NP):
                nc.vector.tensor_scalar(r_kk[:, p_], tile_of(zt, 8 + p_, q, NP), col("cd_rw_kk", q * NP + p_), None, ALU.mult)
            dve.drain()
            done(nc.vector.tensor_tensor(r_x, r_kk, r_kk, ALU.mult))
            dve.wait_ge(rw_t, TT + RW_T["norm"])
            done(nc.vector.tensor_scalar(r_x, ps[:, 6:8, 0:T], 1e-24, None, ALU.max))
            dve.wait_ge(rw_s, S + RW_S["rates"])
            for p_ in range(NP):
                nc.vector.tensor_scalar(r_k2[:, p_], r_a[:, p_], col("cd_rw_ka", q * NP + p_),
                                        omka[:, bass.ds(q * NP + p_, 1)], ALU.mult, ALU.add)
                nc.vector.tensor_tensor_scan(r_cum[:, p_], seg[:], r_prev[:, p_], 0.0, ALU.mult, ALU.add)
            dve.drain()
            nc.vector.tensor_tensor(r_prev, r_cum, r_prev, ALU.subtract)
            nc.vector.tensor_tensor(r_kend[:, :, 0:META], r_cum[:, :, META - 1:META].to_broadcast([P, NP, META]),
                                    r_cum[:, :, 0:META], ALU.subtract)
            for p_ in range(NP):
                c = r_cum[:, p_, META:].rearrange("p (c t) -> p c t", t=RW_CHUNK)
                e = r_kend[:, p_, META:].rearrange("p (c t) -> p c t", t=RW_CHUNK)
                mm = nc.vector.tensor_tensor(e, c[:, :, RW_CHUNK - 1:].to_broadcast([P, 8, RW_CHUNK]), c, ALU.subtract)
            done(mm)
            nc.vector.tensor_tensor(r_k2, r_k2, pair(zt, 8, q), ALU.mult)
            dve.wait_ge(rw_s, S + RW_S["norm"])
            nc.vector.tensor_tensor(r_kk, r_kk, r_x, ALU.mult)
            dve.drain()
            for p_ in range(NP):
                mm = nc.vector.scalar_tensor_tensor(out=r_x[:, p_], in0=tile_of(zt, p_, q, NP), scalar=col("cd_rw_rk", q * NP + p_),
                                                    in1=r_k2[:, p_], op0=ALU.mult, op1=ALU.mult)
            done(mm)
            nc.vector.tensor_tensor(r_bend, r_kk, r_a, ALU.mult)
            dve.wait_ge(rw_s, S + RW_S["decays"])
            nc.vector.tensor_tensor(r_ar[:, :, 0], r_kk, r_prev, ALU.mult)
            nc.vector.tensor_tensor(r_ar[:, :, 1], pair(zt, 0, q), r_grow, ALU.mult)
            dve.drain()
            nc.vector.tensor_tensor(r_bh, r_bend, r_kh, ALU.mult)
            dve.drain()
            nc.vector.tensor_tensor(r_kh, r_k2, r_kh, ALU.mult)
            nc.vector.tensor_tensor(r_bend, r_bend, r_cum, ALU.mult)
            nc.vector.tensor_tensor(r_kend, r_k2, r_cum, ALU.mult)
            dve.drain()
            for hh in range(2):
                w = r_wend[64 * hh:64 * hh + 64, 1:9].rearrange("p c (a b) -> p c a b", b=1).to_broadcast([64, 8, NP, RW_N])
                e = eye2[64 * hh:64 * hh + 64, :].unsqueeze(1).unsqueeze(1).to_broadcast([64, 8, NP, RW_N])
                mm = nc.vector.tensor_tensor(r_trans[64 * hh:64 * hh + 64, :, :, 64 * hh:64 * hh + 64], e, w, ALU.mult)
            done(mm)
            dve.drain()
            for tt, (t0, n) in enumerate(TILES):
                def res(b):
                    return ps[0:n, b, 0:2 * n].rearrange("p (a b) -> p a b", a=2)

                def over(mask):
                    return mask[0:n, 0:n].unsqueeze(1).to_broadcast([n, 2, n])
                for p_ in range(NP):
                    B, hs = 4 * p_, slice(2 * p_, 2 * p_ + 2)
                    dve.wait_ge(rw_t, TT + RW_T[f"x{tt}{p_}"])
                    src = ps[0:n, B + 2:B + 4, 0:n]
                    if n == P:
                        nc.vector.tensor_tensor(r_l21[:, hs], src, over(low21), ALU.mult)
                    done(nc.vector.tensor_tensor(r_p1[0:n, hs, 0:n], src, over(low16), ALU.mult))
                    for hh in range(2):
                        nc.vector.tensor_tensor(r_mm[0:n, 2 * p_ + hh, :, 0:n], ps[0:n, B + hh, 0:4 * n].rearrange("p (a b) -> p a b", a=4),
                                                rw_mask[0:n, :, 0:n], ALU.mult)
                    dve.drain()
                    nc.vector.tensor_tensor(r_q1[0:n, hs, 0:n], r_mm[0:n, hs, 0, 0:n], over(up16), ALU.mult)
                    dve.drain()
                    done(nc.vector.tensor_tensor(r_y[0:n, hs, 0:n], r_q1[0:n, hs, 0:n], over(ident), ALU.add))
                for p_ in range(NP):
                    dve.wait_ge(rw_t, TT + RW_T[f"p2{tt}{p_}"])
                    done(nc.vector.tensor_copy(r_q2[0:n, 2 * p_:2 * p_ + 2, 0:n], res(4 * p_ + 1)))

                def add_to_y(stage, p_, b, op=ALU.add):
                    y = r_y[0:n, 2 * p_:2 * p_ + 2, 0:n]
                    dve.wait_ge(rw_t, TT + RW_T[f"{stage}{tt}{p_}"])
                    return nc.vector.tensor_tensor(y, y, res(4 * p_ + b), op)
                dve.drain()
                for p_ in range(NP):
                    add_to_y("p4", p_, 3)
                    done(nc.vector.tensor_copy(r_q4[0:n, 2 * p_:2 * p_ + 2, 0:n], res(4 * p_ + 1)))
                dve.drain()
                for p_ in range(NP):
                    done(add_to_y("p8", p_, 2))
                dve.drain()
                for p_ in range(NP):
                    done(add_to_y("y8", p_, 3))
                if n == P:
                    for p_ in range(NP):
                        dve.wait_ge(rw_t, TT + RW_T[f"z1{tt}{p_}"])
                        done(nc.vector.tensor_copy(r_z1[:, 2 * p_:2 * p_ + 2], res(4 * p_ + 1)))
                    dve.drain()
                    for p_ in range(NP):
                        done(add_to_y("w", p_, 2, ALU.subtract))
                for p_ in range(NP):
                    B = 4 * p_
                    dve.wait_ge(rw_t, TT + RW_T[f"fe{tt}{p_}"])
                    dve.wait_ge(rw_s, S + RW_S[f"add{tt}{p_}"])
                    settle(dve)
                    mm = nc.vector.tensor_copy(tile_of(zt, 8 + p_, q, NP)[:, t0:t0 + n], ps[:, B, P:P + n])
                    if n == P:
                        nc.vector.tensor_tensor(r_f[:, p_, t0:t0 + n], r_ar[:, p_, 1, t0:t0 + n], ps[:, B, 0:n], ALU.add)
                        c = 4 * (tt - 1)
                        for hh in range(2):
                            rows = slice(64 * hh, 64 * hh + 64)
                            tr = r_trans[rows, c:c + 4, p_, rows]
                            mm = nc.vector.tensor_tensor(tr, tr, ps[rows, B:B + 4, 2 * P:2 * P + RW_N], ALU.add)
                    done(mm)
            dve.drain()
            done(nc.vector.tensor_copy(r_state[:, 0], r_add[:, 0]))
            for c in range(2, 9):
                dve.wait_ge(rw_t, TT + RW_T[f"s{c}"])
                done(nc.vector.tensor_tensor(r_state[:, c - 1], r_add[:, c - 1],
                                             ps[:, c % 2, 0:NP * RW_N].rearrange("p (a b) -> p a b", a=NP), ALU.add))
            dve.drain()
            dve.wait_ge(rw_t, TT + RW_T["y"])
            for p_ in range(NP):
                for hh in range(2):
                    yo = tile_of(zt[64 * hh:64 * hh + 64], 8 + p_, q, NP)[:, META:]
                    nc.vector.tensor_tensor(yo, yo, ps[64 * hh:64 * hh + 64, 2 + 2 * p_ + hh, META:T], ALU.add)
            nc.vector.tensor_copy(pair(zt, 0, q), r_g)
            done(nc.vector.tensor_tensor(pair(zt, 16, q), r_val, r_bonus, ALU.mult))
            dve.drain()

    def rw_scalar(act):
        with act.Fori(0, 8 // NP) as q:
            V, S, TT = q * len(RW_V), q * len(RW_S), q * len(RW_T)

            def done(ins):
                ins.then_inc(rw_s, 1)
            act.wait_ge(rw_t, TT + RW_T["gates"])
            for p_ in range(NP):
                nc.scalar.activation(r_prev[:, p_], ps[:, p_, 0:T], ACT.Sigmoid, bias=col("cd_rw_w0", q * NP + p_))
                mm = nc.scalar.activation(r_a[:, p_], ps[:, 2 + p_, 0:T], ACT.Sigmoid, bias=col("cd_rw_a0", q * NP + p_))
            done(mm)
            act.wait_ge(rw_v, V + RW_V["norm"])
            nc.scalar.activation(r_x, r_x, ACT.Ln)
            act.drain()
            done(nc.scalar.activation(r_x, r_x, ACT.Exp, scale=-0.5))
            for p_ in range(NP):
                nc.scalar.activation(r_g[:, p_], ps[:, 4 + p_, 0:T], ACT.Copy)
            act.wait_ge(rw_v, V + RW_V["cum"])
            nc.scalar.activation(r_wend[:, 0], r_cum[:, :, META - 1], ACT.Exp, scale=-RW_DECAY)
            for p_ in range(NP):
                nc.scalar.activation(r_wend[:, 1:9, p_], r_cum[:, p_, META + RW_CHUNK - 1::RW_CHUNK], ACT.Exp, scale=-RW_DECAY)
            nc.scalar.activation(r_grow, r_cum, ACT.Exp, scale=-RW_DECAY)
            nc.scalar.activation(r_kh, r_cum, ACT.Exp, scale=RW_DECAY)
            nc.scalar.activation(r_prev, r_prev, ACT.Exp, scale=-RW_DECAY)
            act.drain()
            done(nc.scalar.activation(r_cum, r_kend, ACT.Exp, scale=-RW_DECAY))
            act.wait_ge(rw_t, TT + RW_T["bonus"])
            for p_ in range(NP):
                mm = nc.scalar.activation(r_bonus[:, p_], ps[:, 6 + p_, 0:T], ACT.Copy)
            done(mm)
            for tt, (t0, n) in enumerate(TILES):
                def keep(stage, to, b, **how):
                    for p_ in range(NP):
                        w = to.shape[-1] if n == P or to is r_gh else n
                        act.wait_ge(rw_t, TT + RW_T[f"{stage}{tt}{p_}"])
                        done(nc.scalar.activation(to[0:n, 2 * p_:2 * p_ + 2, 0:w],
                                                  ps[0:n, 4 * p_ + b, 0:2 * w].rearrange("p (a b) -> p a b", a=2), ACT.Copy, **how))
                for p_ in range(NP):
                    act.wait_ge(rw_v, V + RW_V[f"p1{tt}{p_}"])
                    for k in range(2):
                        mm = nc.scalar.activation(r_tok[0:n, p_, 2 * k:2 * k + 2], ps[0:n, 4 * p_ + 2 + k, P:3 * P].rearrange(
                            "p (a b) -> p a b", a=2), ACT.Copy)
                    done(mm)
                act.drain()
                for p_ in range(NP):
                    hs = slice(2 * p_, 2 * p_ + 2)
                    nc.scalar.activation(r_gin[0:n, hs, 0:RW_N], r_tok[0:n, p_, 0].rearrange("p (a b) -> p a b", a=2), ACT.Copy)
                    act.wait_ge(rw_t, TT + RW_T[f"p2{tt}{p_}"])
                    nc.scalar.activation(r_gin[0:n, hs, RW_N:], ps[0:n, 4 * p_ + 2, 0:2 * RW_N].rearrange("p (a b) -> p a b", a=2), ACT.Copy)
                    done(nc.scalar.activation(r_p2[0:n, hs, 0:n], ps[0:n, 4 * p_, 0:2 * n].rearrange("p (a b) -> p a b", a=2), ACT.Copy))
                keep("p4", r_p4, 0)
                keep("p8", r_p8, 0)
                if n == P:
                    keep("z1", r_t16, 0)
                keep("gh", r_gh, 3, scale=-1.0)
                first, chunks = (0, 1) if tt == 0 else (4 * tt - 3, 4 if tt == 1 else 3)
                for p_ in range(NP):
                    act.wait_ge(rw_t, TT + RW_T[f"fe{tt}{p_}"])
                    done(nc.scalar.activation(r_add[:, first:first + chunks, p_], ps[:, 4 * p_:4 * p_ + chunks, 2 * P + RW_N:3 * P], ACT.Copy))

    def rw_tensor(pe):
        pe.wait_ge(rws_s, RWS_S["low"])
        with pe.Fori(0, 8 // NP) as q:
            V, S, TT = q * len(RW_V), q * len(RW_S), q * len(RW_T)

            def done(ins):
                ins.then_inc(rw_t, 1)
            pe.wait_ge(rw_v, V + RW_V["staged"])
            for p_ in range(NP):
                nc.tensor.matmul(ps[:, p_, 0:T], r_wst[0:64, p_], zt[0:64, 24], start=True, stop=True)
                nc.tensor.matmul(ps[:, 2 + p_, 0:T], r_wst[64:128, p_], zt[64:128, 24], start=True, stop=True)
                mm = nc.tensor.matmul(ps[:, 4 + p_, 0:T], r_gst[:, p_], zt[:, 25], start=True, stop=True)
            done(mm)
            pe.wait_ge(rw_v, V + RW_V["keys"])
            for p_ in range(NP):
                mm = nc.tensor.matmul(ps[:, 6 + p_, 0:T], pair_ones[:], r_x[:, p_], start=True, stop=True)
            done(mm)
            pe.wait_ge(rw_v, V + RW_V["bonus"])
            for p_ in range(NP):
                mm = nc.tensor.matmul(ps[:, 6 + p_, 0:T], pair_ones[:], r_x[:, p_], start=True, stop=True)
            done(mm)
            pe.wait_ge(rw_v, V + RW_V["ready"])
            pe.wait_ge(rw_s, S + RW_S["kept"])
            settle(pe)
            heads = [(p_, hh) for p_ in range(NP) for hh in range(2)]
            for tt, (t0, n) in enumerate(TILES):
                def waits(p_, vector=None, scalar=None):
                    if vector:
                        pe.wait_ge(rw_v, V + RW_V[f"{vector}{tt}{p_}"])
                    if scalar:
                        pe.wait_ge(rw_s, S + RW_S[f"{scalar}{tt}{p_}"])
                    if n < P:
                        settle(pe)

                def times(p_, b, left, right, w=n):
                    for hh in range(2):
                        mm = nc.tensor.matmul(ps[0:n, 4 * p_ + b, hh * w:(hh + 1) * w], left[0:n, 2 * p_ + hh, 0:n], right(2 * p_ + hh),
                                              start=True, stop=True)
                    return mm

                def of(buf):
                    return lambda hd: buf[0:n, hd, 0:n]

                def value(hd):
                    return r_tok[0:n, hd // 2, 3, 64 * (hd % 2):64 * (hd % 2) + 64]
                tiles_ = range(NP)
                for p_ in tiles_:
                    B = 4 * p_
                    if tt:
                        pe.wait_ge(rw_v, V + RW_V[f"fe{tt - 1}{p_}"])
                        pe.wait_ge(rw_s, S + RW_S[f"add{tt - 1}{p_}"])
                        settle(pe)
                    for hh in range(2):
                        rows, cols_ = slice(64 * hh, 64 * hh + 64), slice(t0, t0 + n)
                        both = r_ar[rows, p_, :, cols_]
                        nc.tensor.matmul(ps[0:n, B + hh, 0:2 * n], r_bh[rows, p_, cols_], both, start=True, stop=True)
                        nc.tensor.matmul(ps[0:n, B + hh, 2 * n:4 * n], r_kh[rows, p_, cols_], both, start=True, stop=True)
                        nc.tensor.matmul(ps[0:n, B + 2 + hh, 0:n], r_ar[rows, p_, 0, cols_], r_bh[rows, p_, cols_], start=True, stop=True)
                    for k, src in enumerate((r_ar[:, p_, 0], r_bend[:, p_], r_kend[:, p_], r_val[:, p_])):
                        mm = nc.tensor.transpose(ps[0:n, B + 2 + k // 2, (1 + k % 2) * P:(2 + k % 2) * P], src[:, t0:t0 + n], ident[:])
                    done(mm)
                for p_ in tiles_:
                    waits(p_, "m", "tok")
                    times(p_, 0, r_q1, of(r_p1))
                    times(p_, 1, r_p1, of(r_q1))
                    done(times(p_, 2, r_mm[:, :, 2], value, RW_N))
                for p_ in tiles_:
                    waits(p_, "q2", "p2")
                    times(p_, 3, r_p2, of(r_y))
                    times(p_, 0, r_q2, of(r_p2))
                    done(times(p_, 1, r_p2, of(r_q2)))
                for p_ in tiles_:
                    waits(p_, "q4", "p4")
                    times(p_, 2, r_p4, of(r_y))
                    done(times(p_, 0, r_q4, of(r_p4)))
                for p_ in tiles_:
                    waits(p_, "y4", "p8")
                    done(times(p_, 3, r_p8, of(r_y)))
                if n == P:
                    for p_ in tiles_:
                        waits(p_, "y8")
                        for hh in range(2):
                            nc.tensor.transpose(ps[:, 4 * p_, hh * P:(hh + 1) * P], r_y[:, 2 * p_ + hh], ident[:])
                        done(times(p_, 1, r_l21, of(r_y)))
                    for p_ in tiles_:
                        waits(p_, "z1", "t16")
                        done(times(p_, 2, r_t16, of(r_z1)))
                for p_ in tiles_:
                    waits(p_, "t32" if n == P else "y8")
                    done(times(p_, 3, r_y, lambda hd: r_gin[0:n, hd, :], P))
                step = min(n, RW_CHUNK)
                for p_ in tiles_:
                    B = 4 * p_
                    waits(p_, None, "gh")
                    for hh in range(2):
                        hd, rows = 2 * p_ + hh, slice(64 * hh, 64 * hh + 64)
                        if n == P:
                            nc.tensor.matmul(ps[rows, B, 0:n], r_gh[0:n, hd, 0:RW_N], r_mm[0:n, hd, 1, 0:n], start=True, stop=True)
                        nc.tensor.matmul(ps[rows, B, P:P + n], value(hd), r_mm[0:n, hd, 3, 0:n], start=True, stop=False)
                        nc.tensor.matmul(ps[rows, B, P:P + n], r_gh[0:n, hd, RW_N:], r_mm[0:n, hd, 1, 0:n], start=False, stop=True)
                    for c in range(n // step):
                        for hh in range(2):
                            hd, rows = 2 * p_ + hh, slice(64 * hh, 64 * hh + 64)
                            s = slice(c * step, (c + 1) * step)
                            b_end, k_end, v = r_tok[s, p_, 1, rows], r_tok[s, p_, 2, rows], r_tok[s, p_, 3, rows]
                            if n == P:
                                nc.tensor.matmul(ps[rows, B + c, 2 * P:2 * P + RW_N], r_gh[s, hd, 0:RW_N], b_end, start=True, stop=True)
                            added = ps[rows, B + c, 2 * P + RW_N:3 * P]
                            nc.tensor.matmul(added, k_end, v, start=True, stop=False)
                            mm = nc.tensor.matmul(added, b_end, r_gh[s, hd, RW_N:], start=False, stop=True)
                    done(mm)
            for p_ in range(NP):
                pe.wait_ge(rw_v, V + RW_V[f"fe2{p_}"])
                pe.wait_ge(rw_s, S + RW_S[f"add2{p_}"])
            def outputs(c):
                t0, n = CH[c]
                for p_ in range(NP):
                    for hh in range(2):
                        rows = slice(64 * hh, 64 * hh + 64)
                        mm = nc.tensor.matmul(ps[rows, 2 + 2 * p_ + hh, t0:t0 + n], r_state[rows, c - 1, p_], r_f[rows, p_, t0:t0 + n], start=True, stop=True)
                return mm
            for c in range(2, 9):
                pe.wait_ge(rw_v, V + RW_V[f"s{c - 1}"])
                for p_ in range(NP):
                    mm = nc.tensor.matmul(ps[:, c % 2, p_ * RW_N:(p_ + 1) * RW_N], r_trans[:, c - 2, p_], r_state[:, c - 2, p_], start=True, stop=True)
                done(mm)
                outputs(c - 1)
            pe.wait_ge(rw_v, V + RW_V["s8"])
            settle(pe)
            mm = outputs(8)
            done(mm)
            pe.wait_ge(rw_v, V + RW_V["end"])

    def rw_end_vector(dve):
        y, sq = zt[:, 8:16], view(arena, 7104, CW, T)
        dve.wait_ge(rwf_t, RWF_T["sums"])
        for k in range(CW):
            mm = nc.vector.scalar_tensor_tensor(out=y[:, k], in0=ps[:, k, 0:T], scalar=-1.0 / RW_N, in1=y[:, k], op0=ALU.mult, op1=ALU.add)
        mm.then_inc(rwf_v, 1)
        dve.wait_ge(rwf_s, RWF_S["rstd"])
        nc.vector.tensor_tensor(y, y, sq, ALU.mult)
        dve.drain()
        for k in range(CW):
            nc.vector.tensor_scalar(y[:, k], y[:, k], col("cd_rw_ln_g", k), col("cd_rw_ln_b", k), ALU.mult, ALU.add)
        dve.drain()
        nc.vector.tensor_tensor(y, y, zt[:, 16:24], ALU.add)
        dve.drain()
        nc.vector.tensor_tensor(y, y, zt[:, 0:8], ALU.mult)

    def rw_end_scalar(act):
        y, sq = zt[:, 8:16], view(arena, 7104, CW, T)
        act.wait_ge(rwf_v, RWF_V["centred"])
        nc.scalar.activation(sq, y, ACT.Square).then_inc(rwf_s, 1)
        act.wait_ge(rwf_t, RWF_T["squares"])
        nc.scalar.activation(sq, ps[:, :, 0:T], ACT.Ln, bias=eps[:, 2:3], scale=1.0 / RW_N)
        act.drain()
        nc.scalar.activation(sq, sq, ACT.Exp, scale=-0.5).then_inc(rwf_s, 1)

    def rw_end_tensor(pe):
        y, sq = zt[:, 8:16], view(arena, 7104, CW, T)
        for k in range(CW):
            mm = nc.tensor.matmul(ps[:, k, 0:T], pair_ones[:], y[:, k], start=True, stop=True)
        mm.then_inc(rwf_t, 1)
        pe.wait_ge(rwf_s, RWF_S["squared"])
        for k in range(CW):
            mm = nc.tensor.matmul(ps[:, k, 0:T], pair_ones[:], sq[:, k], start=True, stop=True)
        mm.then_inc(rwf_t, 1)

    cd_hi, cd_lo = sem("cd_hi"), sem("cd_lo")
    CD_GROUPS = [o_gla[:, 0:4], o_gla[:, 4:8], zt[:, 8:12], zt[:, 12:16]]

    def cd_cat_vector(dve):
        for g, src in enumerate(CD_GROUPS):
            dve.wait_ge(cd_hi, g + 1)
            x = slice(4 * g, 4 * g + 4)
            nc.vector.tensor_tensor(x_lo[:, x], src, x_hi[:, x].bitcast(F32), ALU.subtract).then_inc(cd_lo, 1)

    def cd_cat_scalar(act):
        for g, src in enumerate(CD_GROUPS):
            nc.scalar.activation(x_hi[:, 4 * g:4 * g + 4], src, ACT.Copy).then_inc(cd_hi, 1)

    S2 = SEQ
    TOKT = S2 // P

    def in_keep(act, name, to, c0=0):
        keep_results(act, name, lambda i, u: tile_of(to, c0 + u, i, 4)[:, -S2:])

    def causal_conv(dve, src, dst, weight, bias, tile, step, i, n):
        s, d = tile_of(src, tile, i, step), tile_of(dst, tile, i, step)
        for t in range(CONV_K):
            w = col(weight, i * step + (t * n + tile))
            if t == 0:
                nc.vector.tensor_scalar(d, s[:, 0:S2], w, col(bias, i * step + tile), ALU.mult, ALU.add)
            else:
                dve.drain()
                nc.vector.scalar_tensor_tensor(out=d, in0=s[:, t:t + S2], scalar=w, in1=d, op0=ALU.mult, op1=ALU.add)

    def log1p_vector(dve, e, s, s2, acc):
        nc.vector.tensor_scalar(s, e, 2.0, None, ALU.add)
        dve.drain()
        nc.vector.reciprocal(s, s)
        dve.drain()
        nc.vector.tensor_tensor(s, s, e, ALU.mult)
        dve.drain()
        nc.vector.tensor_tensor(s2, s, s, ALU.mult)
        nc.vector.memset(acc, 2.0 / 17)
        dve.drain()
        for n in range(15, 0, -2):
            nc.vector.tensor_tensor(acc, acc, s2, ALU.mult)
            dve.drain()
            nc.vector.tensor_scalar(acc, acc, 2.0 / n, None, ALU.add)
            dve.drain()
        nc.vector.tensor_tensor(acc, acc, s, ALU.mult)
        dve.drain()

    NH2 = CW
    hz = view(arena, 0, 32, S2)
    h_q, h_b, h_v, h_z = (hz[:, 8 * n:8 * n + 8] for n in range(4))
    h_k, h_e = view(arena, 8192, NH2, S2), view(arena, 10240, NH2, S2)
    h_qe, h_ke = view(arena, 12288, NH2, S2), view(arena, 14336, NH2, S2)
    h_a = view(arena, 16384, NH2 * TOKT, P)
    level_mask = view(side, 0, 8, P)
    HB = 4
    h_vst, h_kst = view(side, 1024, HB, S2), view(arena, 10240, HB, P)
    h_vtok, h_ktok = view(arena, 10752, HB * TOKT, P), view(arena, 11776, HB, P)
    h_state = view(arena, 12288, HB, P)
    h_o, o_a = h_ke, h_qe
    HALF = [slice(0, 4), slice(4, 8)]
    hg_v, hg_s, hg_t = trio("hg")
    _lv = ["logf", "summed", "d10", "d11"]
    _ls = ["k", "log", "q0"]
    _lt = ["x00", "x01"]
    for _l in range(1, 8):
        _lv += [f"m{_l}0", f"m{_l}1"] + ([f"d{_l + 1}0", f"d{_l + 1}1"] if _l < 7 else ["ends"])
        _ls += [f"e{_l}0", f"e{_l}1"]
        _lt += [f"x{_l}0", f"x{_l}1"]
    HG_V, HG_S, HG_T = order(*_lv, "ready"), order(*_ls[:2], *_ls[3:], "to_end", "gate"), order(*_lt)
    hgh_v, hgh_s, hgh_t = trio("hgh")
    HGH_V, HGH_S, HGH_T = order("staged", "ktok", "state"), order("vtok", "out"), order("turned", "states", "mixed")
    hge_s, hge_t = sem("hge_scalar"), sem("hge_tensor")
    HGE_S, HGE_T = order("squared", "rstd"), order("sums")

    def blocks(buf, half, m):
        return buf[:, HALF[half]].rearrange("p a b -> p (a b)").rearrange("p (n j) -> p n j", j=2 * m)

    def hgrn_vector(dve):
        dve.wait_ge(seg_made, 3)
        dve.wait_ge(hg_s, HG_S["log"])
        done = lambda ins: ins.then_inc(hg_v, 1)
        done(nc.vector.scalar_tensor_tensor(out=h_e, in0=h_b, scalar=0.0, in1=h_e, op0=ALU.min, op1=ALU.subtract))
        dve.drain()
        for k in range(NH2):
            mm = nc.vector.tensor_tensor_scan(h_b[:, k], seg[:, 0:S2], h_e[:, k], 0.0, ALU.mult, ALU.add)
        done(mm)
        dve.drain()

        def distance(m):
            for half in range(2):
                b, e = blocks(h_b, half, m), blocks(h_e, half, m)
                done(nc.vector.tensor_tensor(e, b, b[:, :, m - 1:m].to_broadcast(list(b.shape)), ALU.subtract))

        def keep_scores(level):
            for half in range(2):
                dve.wait_ge(hg_t, HG_T[f"x{level}{half}"])
                bank = 4 * (level % 2) + 2 * half
                nc.vector.copy_predicated(h_a[:, 8 * half:8 * half + 8], level_mask[:, level:level + 1, :].to_broadcast([P, 8, P]).bitcast(I32),
                                          ps[:, bank:bank + 2, :].rearrange("p a (b c) -> p (a b) c", c=P))
            dve.drain()
        distance(1)
        keep_scores(0)
        for level, m in enumerate(LEVELS, 1):
            for half in range(2):
                dve.wait_ge(hg_s, HG_S[f"e{level}{half}"])
                e, l, r = blocks(h_e, half, m), slice(0, m), slice(m, 2 * m)
                nc.vector.tensor_tensor(blocks(h_ke, half, m)[:, :, l], blocks(h_k, half, m)[:, :, l], e[:, :, l], ALU.mult)
                done(nc.vector.tensor_tensor(blocks(h_qe, half, m)[:, :, r], blocks(h_q, half, m)[:, :, r], e[:, :, r], ALU.mult))
            dve.drain()
            if level < 7:
                distance(2 * m)
            else:
                done(nc.vector.tensor_tensor(h_e[:, :, 0:P], h_b[:, :, P - 1:P].to_broadcast([P, NH2, P]), h_b[:, :, 0:P], ALU.subtract))
            keep_scores(level)
        dve.wait_ge(hg_s, HG_S["to_end"])
        nc.vector.tensor_tensor(h_k[:, :, 0:P], h_k[:, :, 0:P], h_e[:, :, 0:P], ALU.mult)
        done(nc.vector.tensor_tensor(h_q[:, :, P:], h_q[:, :, P:], h_e[:, :, P:], ALU.mult))
        dve.drain()
        with dve.Fori(0, NH2 // HB) as g:
            s, t = g * len(HGH_S), g * len(HGH_T)
            nc.vector.tensor_copy(h_vst, h_v[:, bass.ds(g * HB, HB)])
            nc.vector.tensor_copy(h_kst, h_k[:, bass.ds(g * HB, HB), 0:P]).then_inc(hgh_v, 1)
            dve.wait_ge(hgh_t, t + HGH_T["turned"])
            nc.vector.tensor_copy(h_ktok, ps[:, 2].rearrange("p (a b) -> p a b", b=P)).then_inc(hgh_v, 1)
            dve.wait_ge(hgh_t, t + HGH_T["states"])
            nc.vector.tensor_copy(h_state, ps[:, 3].rearrange("p (a b) -> p a b", b=P)).then_inc(hgh_v, 1)
            dve.wait_ge(hgh_t, t + HGH_T["mixed"])
        dve.wait_ge(hge_s, HGE_S["rstd"])
        nc.vector.tensor_tensor(h_o, h_o, h_k, ALU.mult)
        dve.drain()
        for k in range(NH2):
            nc.vector.scalar_tensor_tensor(out=o_a[:, k], in0=h_o[:, k], scalar=col("hgrn_norm_w_2", k), in1=h_z[:, k],
                                           op0=ALU.mult, op1=ALU.mult)

    def hgrn_scalar(act):
        done = lambda ins: ins.then_inc(hg_s, 1)
        done(nc.scalar.activation(h_k, h_b, ACT.Sigmoid, scale=-1.0))
        nc.scalar.activation(h_e, h_b, ACT.Abs)
        act.drain()
        nc.scalar.activation(h_e, h_e, ACT.Exp, scale=-1.0)
        act.drain()
        done(nc.scalar.activation(h_e, h_e, ACT.Ln, bias=eps[:, 3:4]))
        for level, m in enumerate(LEVELS, 1):
            for half in range(2):
                act.wait_ge(hg_v, HG_V[f"d{level}{half}"])
                e = blocks(h_e, half, m)
                nc.scalar.activation(e[:, :, 0:m], e[:, :, 0:m], ACT.Exp, scale=-1.0)
                done(nc.scalar.activation(e[:, :, m:], e[:, :, m:], ACT.Exp))
        act.wait_ge(hg_v, HG_V["ends"])
        nc.scalar.activation(h_e[:, :, 0:P], h_e[:, :, 0:P], ACT.Exp)
        done(nc.scalar.activation(h_e[:, :, P:], h_b[:, :, P:], ACT.Exp))
        done(nc.scalar.activation(h_z, h_z, ACT.Silu))
        with act.Fori(0, NH2 // HB) as g:
            t = g * len(HGH_T)
            act.wait_ge(hgh_t, t + HGH_T["turned"])
            nc.scalar.activation(h_vtok, ps[:, 0:2].rearrange("p a (b c) -> p (a b) c", c=P), ACT.Copy).then_inc(hgh_s, 1)
            act.wait_ge(hgh_t, t + HGH_T["mixed"])
            nc.scalar.activation(h_o[:, bass.ds(g * HB, HB)], ps[:, 4:6].rearrange("p a (b c) -> p (a b) c", c=S2),
                                 ACT.Copy).then_inc(hgh_s, 1)
        act.drain()
        nc.scalar.activation(h_e, h_o, ACT.Square).then_inc(hge_s, 1)
        act.wait_ge(hge_t, HGE_T["sums"])
        nc.scalar.activation(h_k, ps[:, 0:4].rearrange("p a (b c) -> p (a b) c", c=S2), ACT.Ln, bias=eps[:, 0:1], scale=1.0 / P)
        act.drain()
        nc.scalar.activation(h_k, h_k, ACT.Exp, scale=-0.5).then_inc(hge_s, 1)

    def hgrn_tensor(pe):
        for level in range(8):
            for half in range(2):
                if level == 0:
                    pe.wait_ge(hg_s, HG_S["k"])
                else:
                    pe.wait_ge(hg_v, HG_V[f"m{level}{half}"])
                left, right = (h_k, h_q) if level == 0 else (h_ke, h_qe)
                for n in range(8):
                    k, c = 4 * half + n // 2, slice(P * (n % 2), P * (n % 2) + P)
                    mm = nc.tensor.matmul(ps[:, 4 * (level % 2) + 2 * half + n // 4, (n % 4) * P:(n % 4 + 1) * P], left[:, k, c],
                                          right[:, k, c], start=True, stop=True)
                mm.then_inc(hg_t, 1)
        pe.wait_ge(hg_v, HG_V["ready"])
        with pe.Fori(0, NH2 // HB) as g:
            v, s = g * len(HGH_V), g * len(HGH_S)
            pe.wait_ge(hgh_v, v + HGH_V["staged"])
            for k in range(HB):
                for j in range(TOKT):
                    nc.tensor.transpose(ps[:, k // 2, ((k % 2) * 2 + j) * P:((k % 2) * 2 + j + 1) * P], h_vst[:, k, j * P:(j + 1) * P], ident[:])
                mm = nc.tensor.transpose(ps[:, 2, k * P:(k + 1) * P], h_kst[:, k], ident[:])
            mm.then_inc(hgh_t, 1)
            pe.wait_ge(hgh_s, s + HGH_S["vtok"])
            pe.wait_ge(hgh_v, v + HGH_V["ktok"])
            for k in range(HB):
                mm = nc.tensor.matmul(ps[:, 3, k * P:(k + 1) * P], h_ktok[:, k], h_vtok[:, 2 * k], start=True, stop=True)
            mm.then_inc(hgh_t, 1)
            pe.wait_ge(hgh_v, v + HGH_V["state"])
            for k in range(HB):
                for j in range(TOKT):
                    acc = ps[:, 4 + k // 2, (k % 2) * S2 + j * P:(k % 2) * S2 + (j + 1) * P]
                    mm = nc.tensor.matmul(acc, h_vtok[:, 2 * k + j], tile_of(h_a, 2 * k + j, g, 2 * HB), start=True, stop=(j == 0))
                    if j:
                        mm = nc.tensor.matmul(acc, h_state[:, k], tile_of(h_q, k, g, HB)[:, P:], start=False, stop=True)
            mm.then_inc(hgh_t, 1)
            pe.wait_ge(hgh_s, s + HGH_S["out"])
        pe.wait_ge(hge_s, HGE_S["squared"])
        for k in range(NH2):
            mm = nc.tensor.matmul(ps[:, k // 2, (k % 2) * S2:(k % 2 + 1) * S2], ones[:], h_e[:, k], start=True, stop=True)
        mm.then_inc(hge_t, 1)

    XW = S2 + CONV_K - 1
    lz = view(arena, 0, 16, XW)
    l_x, l_z = lz[:, 0:8], lz[:, 8:16, XW - S2:]
    l_xc, l_r, l_i = view(arena, 4160, CW, S2), view(arena, 6208, CW, S2), view(arena, 8256, CW, S2)
    l_lam = view(arena, 10304, 5, CW)
    l_t, l_a = view(arena, 14336, CW, S2), view(arena, 16384, CW, S2)
    o_b = l_t
    wa, wx = view(side, 0, CW, P), view(side, 1024, CW, P)
    lru_v, lru_s, lru_t = trio("lru")
    l_u = view(arena, 10368, CW // 2, S2)
    LRU_V = order("log_a0", "log_a1", "used0", "used1")
    LRU_S = order("lambda", "gates0", "gates1", "a0", "a1", "silu")
    LRU_T = order("gates0", "gates1")

    def lru_in_vector(dve):
        run_phase(dve, ph["in_bx"], None, split_part)
        dve.wait_ge(lru_s, LRU_S["lambda"])
        log1p_vector(dve, l_lam[:, 0], l_lam[:, 1], l_lam[:, 2], l_lam[:, 3])
        nc.vector.tensor_scalar(l_lam[:, 4], cols("rglru_lambda_2", CW), -1.0, 0.0, ALU.mult, ALU.max)
        dve.drain()
        nc.vector.tensor_tensor(l_lam[:, 3], l_lam[:, 3], l_lam[:, 4], ALU.add)
        dve.drain()
        nc.vector.tensor_scalar(l_lam[:, 3], l_lam[:, 3], -8.0, None, ALU.mult)
        dve.wait_ge(padded, 2)
        phases_out(dve, "in_bz")
        run_phase(dve, ph["in_bz"], lambda i, u: causal_conv(dve, l_x, l_xc, "rglru_conv_w_2", "rglru_conv_b_2", u, 4, i, CW), split_part)

    def lru_in_scalar(act):
        lam = l_lam[:, 0]
        nc.scalar.activation(lam, cols("rglru_lambda_2", CW), ACT.Abs)
        act.drain()
        nc.scalar.activation(lam, lam, ACT.Exp, scale=-1.0).then_inc(lru_s, 1)
        in_keep(act, "in_bx", lz)
        in_keep(act, "in_bz", lz, 8)

    def lru_vector(dve):
        for half, t in enumerate(HALF):
            dve.wait_ge(lru_s, LRU_S[f"gates{half}"])
            nc.vector.tensor_tensor(l_r[:, t], l_r[:, t], l_lam[:, 3, t].unsqueeze(2).to_broadcast([P, 4, S2]), ALU.mult).then_inc(lru_v, 1)
            nc.vector.tensor_tensor(l_xc[:, t], l_xc[:, t], l_i[:, t], ALU.mult)
        dve.drain()
        for half, t in enumerate(HALF):
            dve.wait_ge(lru_s, LRU_S[f"a{half}"])
            nc.vector.tensor_tensor(l_xc[:, t], l_xc[:, t], l_t[:, t], ALU.mult)
            dve.drain()
            nc.vector.tensor_tensor(l_xc[:, t], l_xc[:, t], l_u, ALU.mult).then_inc(lru_v, 1)
            dve.drain()
            for k in range(t.start, t.stop):
                nc.vector.tensor_tensor_scan(l_r[:, k], l_a[:, k], l_xc[:, k], 0.0, ALU.mult, ALU.add)
        dve.drain()
        dve.wait_ge(lru_s, LRU_S["silu"])
        nc.vector.tensor_tensor(o_b, l_r, l_z, ALU.mult)

    def lru_scalar(act):
        for half, t in enumerate(HALF):
            act.wait_ge(lru_t, LRU_T[f"gates{half}"])
            for first, dst, bias in ((0, l_r, "rglru_ba_2"), (4, l_i, "rglru_bx_2")):
                for k in range(t.start, t.stop):
                    mm = nc.scalar.activation(dst[:, k], ps[:, first + k // 2, (k % 2) * S2:(k % 2 + 1) * S2], ACT.Sigmoid, bias=col(bias, k))
            mm.then_inc(lru_s, 1)
        for half, t in enumerate(HALF):
            act.wait_ge(lru_v, LRU_V[f"log_a{half}"])
            nc.scalar.activation(l_t[:, t], l_r[:, t], ACT.Tanh)
            nc.scalar.activation(l_a[:, t], l_r[:, t], ACT.Exp)
            if half:
                act.wait_ge(lru_v, LRU_V["used0"])
            act.drain()
            nc.scalar.activation(l_u, l_t[:, t], ACT.Ln, bias=eps[:, 3:4], scale=-1.0)
            act.drain()
            nc.scalar.activation(l_u, l_u, ACT.Exp, scale=-0.5)
            nc.scalar.activation(l_t[:, t], l_t[:, t], ACT.Sqrt, scale=-2.0).then_inc(lru_s, 1)
        nc.scalar.activation(l_z, l_z, ACT.Silu).then_inc(lru_s, 1)

    def lru_tensor(pe):
        pe.wait_ge(side_in, 96)
        for t in HALF:
            for first, w in ((0, wa), (4, wx)):
                for k in range(t.start, t.stop):
                    mm = nc.tensor.matmul(ps[:, first + k // 2, (k % 2) * S2:(k % 2 + 1) * S2], w[:, k], l_xc[:, k], start=True, stop=True)
            mm.then_inc(lru_t, 1)

    NX, GROUPS, SH = 12, 2, 16
    PAIRS = CW // GROUPS
    AT_ONCE = 2
    c_pad, c_z = view(arena, 0, NX, XW), view(arena, 3136, CW, S2)
    c_dt, c_e = arena[0:SH, 5184:5440], arena[0:SH, 10560:10816]
    c_x = view(arena, 5440, NX, S2)
    c_y = view(arena, 8512, CW, S2)
    c_s, c_s2, c_log = (arena[0:SH, 10816 + 256 * n:11072 + 256 * n] for n in range(3))
    c_cum, c_dec = arena[0:SH, 11584:11840], arena[0:SH, 11840:12096]
    c_tok = view(arena, 12096, 3, TOKT, SH)
    c_btok, c_cb = view(arena, 16384, TOKT, P), view(arena, 16640, TOKT, P)
    c_bst, c_xst = arena[:, 16896:17152], view(arena, 17152, 2, S2)
    c_xtok, c_xend = view(arena, 17664, 2, TOKT, P), view(arena, 18176, 2, P)
    c_state, c_cq = view(side, 1536, 2, P), view(arena, 11072, 4, P)
    c_sel = side[0:SH, 0:4 * P].rearrange("p (a b) -> p a b", b=P)
    c_l = view(side, 512, 4, TOKT, P)
    c_grow = view(arena, 10560, 4, P)
    c_sq = view(arena, 0, CW, S2)
    c_std = view(arena, 10560, GROUPS, S2)
    o_c = view(arena, 16384, CW, S2)
    ssd_v, ssd_s, ssd_t = trio("ssd")
    SSD_V = order("summed", "tok", "gated")
    SSD_S = order("dt_e", "to_end", "gate", "squared", "std")
    SSD_T = order("turned", "sums")
    sg_v, sg_t = sem("sg_vector"), sem("sg_tensor")
    SG_V, SG_T = order("staged", "out"), order("scores")
    sp_v, sp_s, sp_t = trio("sp")
    SP_V = order("staged", "shifted0", "shifted1", "scores0", "scores1", "out")
    SP_S = order("decays0", "decays1", "state0", "state1")
    SP_T = order("turned0", "turned1", "state0", "state1", "mixed0", "mixed1")

    def ssd_in_vector(dve):
        done = lambda ins: ins.then_inc(ssd_v, 1)
        run_phase(dve, ph["dt"], None, split_part)
        run_phase(dve, ph["in_xbc"], None, split_part)
        dve.wait_ge(ssd_s, SSD_S["dt_e"])
        log1p_vector(dve, c_e, c_s, c_s2, c_log)
        nc.vector.tensor_scalar(c_dt, c_dt, small[:, 0:1], 0.0, ALU.add, ALU.max)
        dve.drain()
        nc.vector.tensor_tensor(c_dt, c_dt, c_log, ALU.add)
        dve.drain()
        nc.vector.tensor_scalar(c_s, c_dt, small[:, 2:3], None, ALU.mult)
        dve.drain()
        nc.vector.tensor_tensor_scan(c_cum, seg[0:SH, 0:S2], c_s, 0.0, ALU.mult, ALU.add)
        dve.drain()
        cum = c_cum.rearrange("p (a b) -> p a b", b=P)
        done(nc.vector.tensor_tensor(c_dec.rearrange("p (a b) -> p a b", b=P), cum[:, :, P - 1:].to_broadcast([SH, TOKT, P]), cum, ALU.subtract))
        dve.wait_ge(padded, 3)
        phases_out(dve, "in_cz")

        def conv(i, u):
            for tile in ((0, 1), (2,), (3, 4), (5,))[u]:
                causal_conv(dve, c_pad, c_x, "ssd_conv_w_2", "ssd_conv_b_2", tile, NX // 2, i, NX)
        run_phase(dve, ph["in_cz"], conv, split_part)

    def ssd_in_scalar(act):
        keep_results(act, "dt", lambda i, u: c_dt)
        in_keep(act, "in_xbc", c_pad)
        nc.scalar.activation(c_e, c_dt, ACT.Abs, bias=small[:, 0:1])
        act.drain()
        nc.scalar.activation(c_e, c_e, ACT.Exp, scale=-1.0).then_inc(ssd_s, 1)
        in_keep(act, "in_cz", c_z)

    def ssd_vector(dve):
        done = lambda ins: ins.then_inc(ssd_v, 1)
        dve.wait_ge(ssd_t, SSD_T["turned"])
        done(nc.vector.tensor_copy(c_tok, ps[:, 7, 0:3 * TOKT * SH].rearrange("p (a b c) -> p a b c", a=3, b=TOKT)))
        dve.wait_ge(ssd_s, SSD_S["gate"])
        dve.drain()
        with dve.Fori(0, GROUPS) as g:
            nc.vector.tensor_copy(c_bst, tile_of(c_x, 8, g, 1)).then_inc(sg_v, 1)
            dve.wait_ge(sg_t, g + SG_T["scores"])
            nc.vector.tensor_copy(c_btok, ps[:, 6, 0:S2].rearrange("p (a b) -> p a b", b=P))
            nc.vector.tensor_tensor(c_cb, ps[:, 7, 0:S2].rearrange("p (a b) -> p a b", b=P),
                                    le[:].unsqueeze(1).to_broadcast([P, TOKT, P]), ALU.mult).then_inc(sg_v, 1)
            dve.drain()
            with dve.Fori(0, PAIRS // AT_ONCE) as r:
                tile = g * PAIRS + r * AT_ONCE
                n = g * (PAIRS // AT_ONCE) + r
                s, t = n * len(SP_S), n * len(SP_T)
                nc.vector.tensor_copy(c_sel, ident[0:SH, bass.ds(tile * 2, 4)].unsqueeze(2).to_broadcast([SH, 4, P]))
                nc.vector.tensor_copy(c_xst, c_x[:, bass.ds(tile, AT_ONCE)]).then_inc(sp_v, 1)
                for e in range(AT_ONCE):
                    dve.wait_ge(sp_t, t + SP_T[f"turned{e}"])
                    for hh in range(2):
                        for j in range(TOKT):
                            mm = nc.vector.tensor_scalar(c_l[:, 2 * e + hh, j], ps[:, 2 * e + hh, j * P:(j + 1) * P],
                                                         c_tok[:, 0, j, bass.ds(tile * 2 + (2 * e + hh), 1)], 0.0, ALU.subtract, ALU.min)
                    mm.then_inc(sp_v, 1)
                for e in range(AT_ONCE):
                    for j in range(TOKT):
                        for hh in range(2):
                            c0 = e * S2 + j * P + 64 * hh
                            nc.vector.tensor_scalar(c_xtok[:, e, j, 64 * hh:64 * hh + 64], ps[:, 4, c0:c0 + 64],
                                                    c_tok[:, 1, j, bass.ds(tile * 2 + (2 * e + hh), 1)], None, ALU.mult)
                dve.drain()
                for e in range(AT_ONCE):
                    for hh in range(2):
                        nc.vector.tensor_scalar(c_xend[:, e, 64 * hh:64 * hh + 64], c_xtok[:, e, 0, 64 * hh:64 * hh + 64],
                                                c_tok[:, 2, 0, bass.ds(tile * 2 + (2 * e + hh), 1)], None, ALU.mult)
                for e in range(AT_ONCE):
                    dve.wait_ge(sp_s, s + SP_S[f"decays{e}"])
                    for hh in range(2 * e, 2 * e + 2):
                        nc.vector.tensor_tensor(c_l[:, hh], c_l[:, hh], c_cb, ALU.mult)
                        mm = nc.vector.tensor_tensor(c_cq[:, hh], c_grow[:, hh], tile_of(c_x, 10, g, 1)[:, P:], ALU.mult)
                    mm.then_inc(sp_v, 1)
                for e in range(AT_ONCE):
                    if e == 0:
                        dve.wait_ge(sp_t, t + SP_T["mixed1"])
                    mm = nc.vector.scalar_tensor_tensor(out=tile_of(c_y[:, e:], 0, tile, 1), in0=c_xst[:, e], scalar=dskip[:, e:][:, bass.ds(tile, 1)],
                                                        in1=ps[:, 6, e * S2:(e + 1) * S2], op0=ALU.mult, op1=ALU.add)
                mm.then_inc(sp_v, 1)
                dve.drain()
        done(nc.vector.tensor_tensor(c_y, c_y, c_z, ALU.mult))
        dve.wait_ge(ssd_s, SSD_S["std"])
        nc.vector.reciprocal(c_std, c_std)
        dve.drain()
        for k in range(CW):
            nc.vector.scalar_tensor_tensor(out=o_c[:, k], in0=c_y[:, k], scalar=col("ssd_norm_w_2", k), in1=c_std[:, k // PAIRS],
                                           op0=ALU.mult, op1=ALU.mult)

    def ssd_scalar(act):
        done = lambda ins: ins.then_inc(ssd_s, 1)
        act.wait_ge(ssd_v, SSD_V["summed"])
        done(nc.scalar.activation(c_dec, c_dec, ACT.Exp))
        nc.scalar.activation(c_x, c_x, ACT.Silu)
        done(nc.scalar.activation(c_z, c_z, ACT.Silu))
        with act.Fori(0, CW // AT_ONCE) as n:
            v, t = n * len(SP_V), n * len(SP_T)
            for e in range(AT_ONCE):
                h2 = slice(2 * e, 2 * e + 2)
                act.wait_ge(sp_v, v + SP_V[f"shifted{e}"])
                nc.scalar.activation(c_grow[:, h2], ps[:, h2, P:2 * P], ACT.Exp)
                nc.scalar.activation(c_l[:, h2], c_l[:, h2], ACT.Exp).then_inc(sp_s, 1)
            for e in range(AT_ONCE):
                act.wait_ge(sp_t, t + SP_T[f"state{e}"])
                nc.scalar.activation(c_state[:, e], ps[:, 5, e * P:(e + 1) * P], ACT.Copy).then_inc(sp_s, 1)
        act.wait_ge(ssd_v, SSD_V["gated"])
        done(nc.scalar.activation(c_sq, c_y, ACT.Square))
        act.wait_ge(ssd_t, SSD_T["sums"])
        done(nc.scalar.activation(c_std, ps[:, 0:GROUPS, 0:S2], ACT.Sqrt, bias=eps[:, 0:1], scale=1.0 / 512))

    def ssd_tensor(pe):
        pe.wait_ge(ssd_s, SSD_S["to_end"])
        for n, src in enumerate((c_cum, c_dt, c_dec)):
            for j in range(TOKT):
                first = (n * TOKT + j) * SH
                mm = nc.tensor.transpose(ps[:, 7, first:first + SH], src[:, j * P:(j + 1) * P], ident[0:SH, 0:SH])
        mm.then_inc(ssd_t, 1)
        pe.wait_ge(ssd_v, SSD_V["tok"])
        with pe.Fori(0, GROUPS) as g:
            pe.wait_ge(sg_v, g * len(SG_V) + SG_V["staged"])
            for j in range(TOKT):
                cols_ = slice(j * P, (j + 1) * P)
                nc.tensor.transpose(ps[:, 6, cols_], c_bst[:, cols_], ident[:])
                mm = nc.tensor.matmul(ps[:, 7, cols_], c_bst[:, cols_], tile_of(c_x, 10, g, 1)[:, cols_], start=True, stop=True)
            mm.then_inc(sg_t, 1)
            with pe.Fori(0, PAIRS // AT_ONCE) as r:
                n = g * (PAIRS // AT_ONCE) + r
                v, s = n * len(SP_V), n * len(SP_S)
                pe.wait_ge(sp_v, v + SP_V["staged"])
                for e in range(AT_ONCE):
                    for hh in range(2 * e, 2 * e + 2):
                        nc.tensor.matmul(ps[:, hh, 0:S2], c_sel[:, hh], c_cum, start=True, stop=True)
                    for j in range(TOKT):
                        mm = nc.tensor.transpose(ps[:, 4, e * S2 + j * P:e * S2 + (j + 1) * P], c_xst[:, e, j * P:(j + 1) * P], ident[:])
                    mm.then_inc(sp_t, 1)
                for e in range(AT_ONCE):
                    pe.wait_ge(sp_v, v + SP_V[f"scores{e}"])
                    if e:
                        pe.wait_ge(sp_s, s + SP_S["state0"])
                    nc.tensor.matmul(ps[:, 5, e * P:(e + 1) * P], c_btok[:, 0], c_xend[:, e], start=True, stop=True).then_inc(sp_t, 1)
                for e in range(AT_ONCE):
                    pe.wait_ge(sp_s, s + SP_S[f"state{e}"])
                    for hh in range(2):
                        rows = slice(64 * hh, 64 * hh + 64)
                        for j in range(TOKT):
                            acc = ps[rows, 6, e * S2 + j * P:e * S2 + (j + 1) * P]
                            mm = nc.tensor.matmul(acc, c_xtok[:, e, j, rows], c_l[:, 2 * e + hh, j], start=True, stop=(j == 0))
                            if j:
                                mm = nc.tensor.matmul(acc, c_state[:, e, rows], c_cq[:, 2 * e + hh], start=False, stop=True)
                    mm.then_inc(sp_t, 1)
                pe.wait_ge(sp_v, v + SP_V["out"])
        pe.wait_ge(ssd_s, SSD_S["squared"])
        for k in range(CW):
            mm = nc.tensor.matmul(ps[:, k // PAIRS, 0:S2], ones[:], c_sq[:, k], start=(k % PAIRS == 0), stop=(k % PAIRS == PAIRS - 1))
        mm.then_inc(ssd_t, 1)

    branches = view(arena, 12288, 24, S2)
    cat_hi = act_hi[:].rearrange("p (k t) -> p k t", t=S2)
    cat_lo = act_lo[:].rearrange("p (k t) -> p k t", t=S2)
    gate, prod = view(arena, 12288, 2, 3, S2), view(arena, 12288 + 6 * S2, 2, 3, S2)
    cat_hi_made, cat_lo_made = sem("cat_hi_made"), sem("cat_lo_made")

    def cat_scalar(act):
        for n in range(3):
            nc.scalar.activation(cat_hi[:, 8 * n:8 * n + 8], branches[:, 8 * n:8 * n + 8], ACT.Copy).then_inc(cat_hi_made, 1)

    def cat_vector(dve):
        for n in range(3):
            dve.wait_ge(cat_hi_made, n + 1)
            t = slice(8 * n, 8 * n + 8)
            nc.vector.tensor_tensor(cat_lo[:, t], branches[:, t], cat_hi[:, t].bitcast(F32), ALU.subtract).then_inc(cat_lo_made, 1)

    def out_scalar(act):
        p = ph["out"]

        def work(i, q):
            u, n, is_branch = q // 6, (q % 6) // 2, q % 2
            if q % 6 == 5:
                act.wait_ge(tile_summed[u], i + 2)
                square_tile(act, "out", i, u, 2, META)
            if not is_branch:
                result_ready(act, p, i, q)
                act.wait_ge(tile_summed[u], i + 1)
                act.wait_ge(cat_lo_made, 3)
                nc.scalar.activation(gate[:, u, n], ps[:, q % 6, 0:S2], ACT.Sigmoid).then_inc(gates_made, 1)
        run_phase(act, p, work, round_part, last=True)

    def out_vector(dve):
        p = ph["out"]

        def work(i, q):
            u, n, is_branch = q // 6, (q % 6) // 2, q % 2
            if is_branch:
                result_ready(dve, p, i, q)
                dve.wait_ge(gates_made, i * 6 + (3 * u + n + 4))
                nc.vector.tensor_tensor(prod[:, u, n], ps[:, q % 6, 0:S2], gate[:, u, n], ALU.mult).then_inc(products_made, 1)
                dve.drain()
                x = tile_of(h, u, i, 2)[:, META:]
                mm = nc.vector.tensor_tensor(x, x, prod[:, u, n], ALU.add)
                if n == 2:
                    mm.then_inc(tile_summed[u], 1)
        run_phase(dve, p, work, split_part, last=True)

    def out_tensor(pe):
        p = ph["out"]
        with pe.Fori(0, p.n) as i:
            for q, (kt, w, _) in enumerate(p.jobs):
                u, n, is_branch = q // 6, (q % 6) // 2, q % 2
                pe.wait_ge(products_made if is_branch else gates_made, i * 6 + (3 * u + n + 1))
                if is_branch:
                    pe.wait_ge(cat_lo_made, n + 1)
                operand = (cat_hi, cat_lo, 8 * n) if is_branch else (x_hi, x_lo, 0)
                multiply_job(pe, p, i, q, ps[:, q % 6, 0:S2],
                             lambda k: (operand[0][:, operand[2] + k, 0:S2], operand[1][:, operand[2] + k, 0:S2]), kt, w, True, True)

    x_in, meta_in = view(arena, 0, TOKT, D), arena[0:META, 4096:4096 + D]
    rows_in = view(arena, 6144, ROW_GROUPS, P)
    d_row = arena[0:1, 8000:8016]
    stage_out = view(arena, 6144, TOKT, D)
    d_turned, start_v, a_exp = sem("d_turned"), sem("start_vector"), sem("a_exp")
    input_in = sem("input_in")
    PARAM_DMAS = 3 + sum((VOFF[name] + n - 1) // P - VOFF[name] // P + 1 for name, n in VECTORS)

    def flat_rows(ap):
        names = "abcd"[:len(ap.shape)]
        flat = ap.rearrange(f"{' '.join(names)} -> ({' '.join(names)})") if len(ap.shape) > 1 else ap
        return flat.rearrange("(k p) -> k p", p=P)

    def start_loads(act):
        def load(dst, src, arrived=params_in):
            act.dma_start(dst, src).then_inc(arrived, 16)
        load(meta_in, a["meta"], input_in)
        for j in range(TOKT):
            load(x_in[:, j], a["x"][0, j * P:(j + 1) * P, :], input_in)
        for name, n in VECTORS:
            src, first, r = flat_rows(a[name]), VOFF[name], 0
            while r < n:
                g, p0 = (first + r) // P, (first + r) % P
                m = min(n - r, P - p0)
                load(rows_in[p0:p0 + m, g], src[r:r + m])
                r += m
        load(small[:, 0:1], a["ssd_dt_bias_2"].rearrange("a n -> n a"))
        load(small[:, 1:2], a["ssd_a_log_2"].rearrange("a n -> n a"))
        load(d_row, a["ssd_d_2"])

    def start_tensor(pe):
        pe.wait_ge(masks_made, 1)
        pe.wait_ge(input_in, 16 * (1 + TOKT))
        for k in range(DK):
            if k >= 4:
                pe.wait_ge(x_kept[k % 2], (k - 4) // 2 + 1)
            c = slice(k * P, (k + 1) * P)
            nc.tensor.transpose(ps[:, 4 + k % 4, 0:META], meta_in[:, c], ident[0:META, 0:META])
            for j in range(TOKT):
                mm = nc.tensor.transpose(ps[:, 4 + k % 4, META + j * P:META + (j + 1) * P], x_in[:, j, c], ident[:])
            mm.then_inc(x_turned, 1)
        pe.wait_ge(params_in, 16 * PARAM_DMAS)
        for g in range(ROW_GROUPS):
            n = min(P, NROWS - g * P)
            mm = nc.tensor.transpose(ps[:, g // 4, (g % 4) * P:(g % 4) * P + n], rows_in[0:n, g], ident[0:n, 0:n])
        mm.then_inc(rows_turned, 1)
        nc.tensor.matmul(ps[:, 3, 0:16], ones[0:1, :], d_row, start=True, stop=True).then_inc(d_turned, 1)

    def start_vector(dve):
        for k in range(0, DK, 2):
            dve.wait_ge(x_turned, k + 1)
            nc.vector.tensor_copy(h[:, k], ps[:, 4 + k % 4, 0:T]).then_inc(x_kept[0], 1)
        for v in range(AHEAD):
            split_part(dve, ph["ab_gate"], 0, v, PART)
        dve.wait_ge(rows_turned, 1)
        for b in range((ROW_GROUPS + 3) // 4):
            n = min(512, NROWS - b * 512)
            nc.vector.tensor_copy(vec[:, b * 512:b * 512 + n], ps[:, b, 0:n])
        dve.drain()
        dve.wait_ge(d_turned, 1)
        for hh in range(2):
            rows = slice(64 * hh, 64 * hh + 64)
            nc.vector.tensor_copy(dskip[rows, :], ps[rows, 3, hh:16:2])
        nc.vector.tensor_scalar(omka[:], cols("cd_rw_ka", CW), -1.0, 1.0, ALU.mult, ALU.add)
        dve.wait_ge(a_exp, 1)
        nc.vector.tensor_scalar(small[:, 2:3], small[:, 3:4], -1.0, None, ALU.mult)

    def start_scalar(act):
        for k in range(1, DK, 2):
            act.wait_ge(x_turned, k + 1)
            nc.scalar.activation(h[:, k], ps[:, 4 + k % 4, 0:T], ACT.Copy).then_inc(x_kept[1], 1)
        for v in range(AHEAD):
            round_part(act, ph["ab_gate"], 0, v, PART)
        act.wait_ge(params_in, 16 * PARAM_DMAS)
        nc.scalar.activation(small[:, 3:4], small[:, 1:2], ACT.Exp).then_inc(a_exp, 1)

    def end_tensor(pe):
        for b in range(8):
            j, k0 = b // 4, 4 * (b % 4)
            pe.wait_ge(norm_xn, 4 * 6 + b % 4 + 1)
            for k in range(4):
                mm = nc.tensor.transpose(ps[:, (b + 4) % 8, k * P:(k + 1) * P], xn[:, k0 + k, j * P:(j + 1) * P], ident[:])
            mm.then_inc(out_turned, 1)

    def end_keep(eng, parity):
        for b in range(parity, 8, 2):
            eng.wait_ge(out_turned, b + 1)
            dst = stage_out[:, b // 4, (b % 4) * 512:(b % 4 + 1) * 512]
            if parity:
                nc.scalar.activation(dst, ps[:, (b + 4) % 8, :], ACT.Copy).then_inc(out_kept[1], 1)
            else:
                nc.vector.tensor_copy(dst, ps[:, (b + 4) % 8, :]).then_inc(out_kept[0], 1)

    def end_store(sp):
        for b in range(8):
            sp.wait_ge(out_kept[b % 2], b // 2 + 1)
            j, c = b // 4, slice((b % 4) * 512, (b % 4 + 1) * 512)
            sp.dma_start(out[0, j * P:(j + 1) * P, c], stage_out[:, j, c]).then_inc(out_stored, 16)
        sp.wait_ge(out_stored, 16 * 8)

    def triangle(pool, buf, block, sign, strict):
        n = P // block
        v = buf.rearrange("p (a b) -> p a b", b=block) if n > 1 else buf

        def keep(of_block, of_column, base, mult):
            pool.drain()
            pattern = [[of_block, n], [of_column, block]] if n > 1 else [[of_column, block]]
            nc.gpsimd.affine_select(out=v, in_=v, pattern=pattern, compare_op=ALU.is_ge, fill=0.0, base=base, channel_multiplier=mult)
        if n > 1:
            keep(-block, 0, 0, 1)
            keep(block, 0, block - 1, -1)
        if sign:
            keep(sign * block, sign, -strict, -sign)

    def scan_starts(pool, starts):
        nc.gpsimd.memset(seg[:], 1.0)
        pool.drain()
        for t0, step, n in starts:
            nc.gpsimd.memset(seg[:, t0:t0 + (n - 1) * step + 1:step], 0.0)
        pool.drain().then_inc(seg_made, 1)

    def start_pool(pool):
        pool.sem_inc(split, RING)
        pool.sem_inc(multiplied, SLOTS)
        for b in range(2):
            pool.sem_inc(drained[b], 1)
            pool.sem_inc(tile_summed[b], 1)
        pool.sem_inc(gates_made, 3)
        pool.sem_inc(products_made, 3)
        nc.gpsimd.memset(ident[:], 1.0)
        nc.gpsimd.memset(ones[:], 1.0)
        for n, e in enumerate((EPS, LN_EPS, GN_EPS, 1.0)):
            nc.gpsimd.memset(eps[:, n:n + 1], e)
        triangle(pool, ident[:], P, 1, 0)
        triangle(pool, ident[:], P, -1, 0)
        pool.drain().then_inc(masks_made, 1)
        for buf in (pair_ones, le, le64):
            nc.gpsimd.memset(buf[:], 1.0)
        nc.gpsimd.memset(rw_mask[:], 1.0)
        nc.gpsimd.memset(up16[:], -1.0)
        nc.gpsimd.memset(low16[:], -1.0)
        nc.gpsimd.memset(low21[:], 1.0)
        triangle(pool, pair_ones[:], 64, 0, 0)
        triangle(pool, le[:], P, 1, 0)
        triangle(pool, le64[:], 64, 1, 0)
        for n in range(4):
            triangle(pool, rw_mask[:, n], RW_CHUNK, 1, 1 - n % 2)
        triangle(pool, up16[:], 16, 1, 1)
        triangle(pool, low16[:], 16, -1, 1)
        triangle(pool, low21[:], 32, 0, 0)
        v = low21[:].rearrange("p (a b) -> p a b", b=32)
        pool.drain()
        nc.gpsimd.affine_select(out=v, in_=v, pattern=[[-32, 4], [0, 32]], compare_op=ALU.is_ge, fill=0.0, base=-16, channel_multiplier=1)
        pool.drain()
        nc.gpsimd.memset(v[:, :, 16:], 0.0)
        for hh in range(2):
            rows = slice(64 * hh, 64 * hh + 64)
            pool.drain()
            nc.gpsimd.tensor_copy(eye2[rows, :], ident[rows, rows])
        pool.drain()
        nc.gpsimd.memset(ab_a[:, :, 0:CONF_K - 1], 0.0)
        nc.gpsimd.memset(ab_s[:, :, 0:SC_K - 1], 0.0)
        scan_starts(pool, [(0, 1, 1), (META, GLA_CHUNK, 4)])

    def gla_pool(pool):
        pool.dma_start(g_w2, a["cd_gla_w2"][0]).then_inc(side_in, 16)
        pool.wait_ge(side_in, 16)
        pool.dma_start(side[0:64, 0:1024], a["cd_rw_w2"][0]).then_inc(side_in, 16)
        pool.dma_start(side[64:128, 0:1024], a["cd_rw_a2"][0]).then_inc(side_in, 16)
        pool.dma_start(side[:, 1024:2048], a["cd_rw_g2"][0]).then_inc(side_in, 16)

    def rw_pool(pool):
        scan_starts(pool, [(0, 1, 1), (META, RW_CHUNK, SEQ // RW_CHUNK)])
        nc.gpsimd.memset(zr[:, :, 0:1], 0.0).then_inc(padded, 1)

    def level_pool(pool):
        scan_starts(pool, [(0, P, TOKT)])
        nc.gpsimd.memset(level_mask, 1.0)
        triangle(pool, level_mask[:, 0], P, 1, 0)
        triangle(pool, level_mask[:, 0], P, -1, 0)
        for level, m in enumerate(LEVELS, 1):
            triangle(pool, level_mask[:, level], 2 * m, 0, 0)
            v = level_mask[:, level].rearrange("p (a b) -> p a b", b=2 * m)
            pool.drain()
            nc.gpsimd.affine_select(out=v, in_=v, pattern=[[2 * m, P // (2 * m)], [0, 2 * m]], compare_op=ALU.is_ge, fill=0.0,
                                    base=m - 1, channel_multiplier=-1)
            pool.drain()
            nc.gpsimd.memset(v[:, :, 0:m], 0.0)

    def hgrn_pool(pool):
        pool.wait_ge(norm_sum, 5)
        nc.gpsimd.memset(arena[:, 12288:18432], 0.0)

    def lru_pool(pool):
        for n, name in enumerate(("rglru_wa_2", "rglru_wx_2")):
            pool.dma_start(view(side, 1024 * n, CW, P), a[name][0].rearrange("h i j -> i h j")).then_inc(side_in, 16)
        nc.gpsimd.memset(l_x[:, :, 0:CONV_K - 1], 0.0).then_inc(padded, 1)

    def ssd_pool(pool):
        nc.gpsimd.memset(c_pad[:, :, 0:CONV_K - 1], 0.0).then_inc(padded, 1)

    block = nc.Block()
    with block:
        @block.sync
        def _(sp):
            for p in ph.values():
                load_phase(sp, p)
            end_store(sp)

        @block.scalar
        def _(act):
            start_loads(act)
            start_scalar(act)
            meet(act, "setup")
            norm_scalar(act, 0, 0, True)
            ab_in_scalar(act)
            meet(act, "ab_in")
            ab_scalar(act)
            square_residual(act, "ab_out")
            meet(act, "ab_out")
            norm_scalar(act, 1, 0, True, "ab_out")
            for f in range(2):
                ffn_scalar(act, 0, f)
            meet(act, "ffn0")
            norm_scalar(act, 2, 0, True, "down01")
            keep_results(act, "gla", lambda i, u: tile_of(zg, u, i, 4))
            keep_results(act, "glr", lambda i, u: g_low)
            meet(act, "gla_in")
            gla_prepare_scalar(act)
            gla_heads_scalar(act)
            gla_end_scalar(act)
            meet(act, "gla")
            keep_results(act, "rw", lambda i, u: tile_of(zt, u, i, 4))
            keep_results(act, "rw_low", lambda i, u: tile_of(zt, 24 + u, i, 4))
            meet(act, "rw_in")
            rw_mix_scalar(act)
            rw_scalar(act)
            rw_end_scalar(act)
            meet(act, "rw")
            cd_cat_scalar(act)
            square_residual(act, "cd_out")
            meet(act, "cd_out")
            norm_scalar(act, 3, 0, True, "cd_out")
            for f in range(2):
                ffn_scalar(act, 1, f)
            meet(act, "ffn1")
            norm_scalar(act, 4, META, False, "down11")
            norm_scalar(act, 5, META, True, after=4)
            in_keep(act, "in_a", hz)
            meet(act, "in_a")
            hgrn_scalar(act)
            meet(act, "hgrn")
            lru_in_scalar(act)
            meet(act, "in_b")
            lru_scalar(act)
            meet(act, "rglru")
            ssd_in_scalar(act)
            meet(act, "in_c")
            ssd_scalar(act)
            meet(act, "ssd")
            cat_scalar(act)
            out_scalar(act)
            meet(act, "out")
            norm_scalar(act, 6, META, False, "out")
            end_keep(act, 1)

        @block.vector
        def _(dve):
            start_vector(dve)
            meet(dve, "setup")
            norm_vector(dve, 0, 0, lambda k: col("norm_mix", k))
            ab_in_vector(dve)
            meet(dve, "ab_in")
            ab_vector(dve)
            add_residual(dve, "ab_out")
            meet(dve, "ab_out")
            norm_vector(dve, 1, 0, lambda k: col("norm_ffn", k))
            for f in range(2):
                ffn_vector(dve, 0, f)
            meet(dve, "ffn0")
            norm_vector(dve, 2, 0, lambda k: col("norm_mix", DK + k))
            for name in ("gla", "glr"):
                run_phase(dve, ph[name], None, split_part)
            meet(dve, "gla_in")
            gla_prepare_vector(dve)
            gla_heads_vector(dve)
            gla_end_vector(dve)
            meet(dve, "gla")
            rw_in_vector(dve)
            meet(dve, "rw_in")
            rw_vector(dve)
            rw_end_vector(dve)
            meet(dve, "rw")
            cd_cat_vector(dve)
            add_residual(dve, "cd_out")
            meet(dve, "cd_out")
            norm_vector(dve, 3, 0, lambda k: col("norm_ffn", DK + k))
            for f in range(2):
                ffn_vector(dve, 1, f)
            meet(dve, "ffn1")
            norm_vector(dve, 4, META, lambda k: col("norm_final", k), lambda k: h[:, k, META:T])
            norm_vector(dve, 5, META, lambda k: col("norm_w_2", k))
            run_phase(dve, ph["in_a"], None, split_part)
            meet(dve, "in_a")
            hgrn_vector(dve)
            meet(dve, "hgrn")
            lru_in_vector(dve)
            meet(dve, "in_b")
            lru_vector(dve)
            meet(dve, "rglru")
            ssd_in_vector(dve)
            meet(dve, "in_c")
            ssd_vector(dve)
            meet(dve, "ssd")
            cat_vector(dve)
            out_vector(dve)
            meet(dve, "out")
            norm_vector(dve, 6, META, lambda k: col("final_norm_w_2", k), lambda k: xn[:, k, 0:S2])
            end_keep(dve, 0)

        @block.tensor
        def _(pe):
            start_tensor(pe)
            meet(pe, "setup")
            norm_tensor(pe, 0, 0)
            for name in ("ab_gate", "ab_val", "ab_s"):
                multiply_phase(pe, name, T, norm_lo[0] if name == "ab_gate" else None)
            meet(pe, "ab_in")
            ab_tensor(pe)
            multiply_phase(pe, "ab_out", T, ab_lo)
            meet(pe, "ab_out")
            norm_tensor(pe, 1, 0, "ab_out")
            for f in range(2):
                ffn_tensor(pe, 0, f)
            meet(pe, "ffn0")
            norm_tensor(pe, 2, 0, "down01")
            for name in ("gla", "glr"):
                multiply_phase(pe, name, T, norm_lo[2] if name == "gla" else None)
            meet(pe, "gla_in")
            gla_prepare_tensor(pe)
            gla_heads_tensor(pe)
            gla_end_tensor(pe)
            part_early(pe)
            pe.wait_ge(gle_s, GLE_S["rstd"])
            for name in ("rw", "rw_low"):
                multiply_phase(pe, name, T)
            meet(pe, "rw_in")
            rw_tensor(pe)
            rw_end_tensor(pe)
            meet(pe, "rw")
            multiply_phase(pe, "cd_out", T, cd_lo)
            meet(pe, "cd_out")
            norm_tensor(pe, 3, 0, "cd_out")
            for f in range(2):
                ffn_tensor(pe, 1, f)
            meet(pe, "ffn1")
            norm_tensor(pe, 4, META, "down11")
            norm_tensor(pe, 5, META)
            multiply_phase(pe, "in_a", S2, norm_lo[5])
            meet(pe, "in_a")
            hgrn_tensor(pe)
            part_early(pe)
            pe.wait_ge(hge_s, HGE_S["rstd"])
            for name in ("in_bx", "in_bz"):
                multiply_phase(pe, name, S2)
            meet(pe, "in_b")
            lru_tensor(pe)
            part_early(pe)
            pe.wait_ge(lru_s, LRU_S["gates1"])
            for name in ("dt", "in_xbc", "in_cz"):
                multiply_phase(pe, name, S2)
            meet(pe, "in_c")
            ssd_tensor(pe)
            part_early(pe)
            pe.wait_ge(ssd_s, SSD_S["std"])
            out_tensor(pe)
            meet(pe, "out")
            norm_tensor(pe, 6, META, "out")
            end_tensor(pe)

        @block.gpsimd
        def _(pool):
            behind = {
                "setup": lambda: ab_in_pool(pool), "ab_in": lambda: sum_squares(pool, "ab_out", 0),
                "ab_out": lambda: sum_squares(pool, "down01", 0), "ffn0": lambda: gla_pool(pool), "gla": lambda: rw_pool(pool),
                "rw": lambda: sum_squares(pool, "cd_out", 0),
                "cd_out": lambda: (level_pool(pool), sum_squares(pool, "down11", META)), "ffn1": lambda: hgrn_pool(pool), "hgrn": lambda: lru_pool(pool),
                "rglru": lambda: ssd_pool(pool), 
                "ssd": lambda: (pool.wait_ge(cat_lo_made, 3), sum_squares(pool, "out", META)),
            }
            start_pool(pool)
            for b in range(2):
                pool.sem_inc(sq_used[b], 1)
            for name in MEETINGS:
                meet(pool, name)
                if name in behind:
                    behind[name]()


def kernel(**inputs):
    import concourse.bacc as bacc
    from concourse.bass_utils import run_bass_kernel_spmd

    arrays = {name: np.ascontiguousarray(v) for name, v in inputs.items()}
    nc = bacc.Bacc("TRN2", target_bir_lowering=False, num_devices=1)
    a = {name: nc.dram_tensor(name, v.shape, mybir.dt.from_np(v.dtype), kind="ExternalInput").ap() for name, v in arrays.items()}
    out = nc.dram_tensor("out", (1, SEQ, D), F32, kind="ExternalOutput").ap()
    build(nc, a, out)
    return run_bass_kernel_spmd(nc, [arrays], core_ids=[0]).results[0]["out"]
```
